# Optimizing a Trainium2 kernel written in Bass

```python
import math, functools
import jax, jax.numpy as jnp
from jax import lax
import numpy as np

D_MODEL = 1024
BATCH = 1
SEQ = 128
DEPTH = 2
DEC_BATCH = 1
DEC_SEQ = 256
PAST_LEN = 128

GRID_W = 64
Q_BLOCK = 128
EPS = 1e-6
ROPE_THETA = 10000.0
N_EVEN = (DEPTH + 1) // 2
N_ODD = DEPTH // 2
N_MOD = 6
HY_DIM = D_MODEL // 2
HY_ORDER = 2
FILT_EMB = 33
FILT_BANDS = (FILT_EMB - 1) // 2
FILT_HIDDEN = 64
HY_MIN_DECAY = math.log(1e-2) / 1.5
HY_MAX_DECAY = math.log(1e-2) / 0.3
GQA_HEADS = 8
GQA_KV_HEADS = 2
GQA_HEAD_DIM = 64
GQA_Q = GQA_HEADS * GQA_HEAD_DIM
GQA_KV = GQA_KV_HEADS * GQA_HEAD_DIM
EVEN_IN = (HY_ORDER + 1) * HY_DIM + GQA_Q + 2 * GQA_KV
EVEN_OUT = HY_DIM + GQA_Q
MLA_HEADS = 16
MLA_NOPE_DIM = 64
MLA_ROPE_DIM = 32
MLA_QK_DIM = MLA_NOPE_DIM + MLA_ROPE_DIM
MLA_V_DIM = 64
MLA_Q_RANK = 256
MLA_KV_RANK = 128
ODD_IN = MLA_Q_RANK + MLA_KV_RANK + MLA_ROPE_DIM
ODD_OUT = MLA_HEADS * MLA_V_DIM
N_EXPERTS = 16
N_GROUPS = 4
EXPERTS_PER_GROUP = N_EXPERTS // N_GROUPS
TOP_K = 2
D_EXPERT = 256

kernel_name = 'hybrid_diffusion_hyena_gqa_mla_moe_step'

def _rmsnorm(x, g):
    xf = x.astype(jnp.float32)
    y = xf * lax.rsqrt(jnp.mean(xf * xf, axis=-1, keepdims=True) + EPS)
    return (y * g.astype(jnp.float32)).astype(x.dtype)

def _grid_positions(n):
    rows = n // GRID_W
    row = jnp.repeat(jnp.arange(rows, dtype=jnp.int32), GRID_W)
    col = jnp.tile(jnp.arange(GRID_W, dtype=jnp.int32), rows)
    return row, col

def _rope_axis(x, pos):
    npair = x.shape[-1] // 2
    freqs = ROPE_THETA ** (-jnp.arange(npair, dtype=jnp.float32) / npair)
    ang = pos.astype(jnp.float32)[:, None] * freqs[None, :]
    cos = jnp.cos(ang)[None, :, None, :]
    sin = jnp.sin(ang)[None, :, None, :]
    xf = x.astype(jnp.float32)
    x1, x2 = xf[..., :npair], xf[..., npair:]
    return jnp.concatenate([x1 * cos - x2 * sin, x2 * cos + x1 * sin], axis=-1).astype(x.dtype)

def _rope_2d(x):
    row, col = _grid_positions(x.shape[1])
    half = x.shape[-1] // 2
    return jnp.concatenate([_rope_axis(x[..., :half], row), _rope_axis(x[..., half:], col)], axis=-1)

def _rope_tail(x, n_pass):
    return jnp.concatenate([x[..., :n_pass], _rope_2d(x[..., n_pass:])], axis=-1)

def _attend(q, k, v):
    b, lq, h, dh = q.shape
    hkv = k.shape[2]
    grp = h // hkv
    nb = lq // Q_BLOCK
    qb = q.reshape(b, nb, Q_BLOCK, hkv, grp, dh).transpose(1, 0, 2, 3, 4, 5)
    kf = k.astype(jnp.float32)
    vf = v.astype(jnp.float32)
    scale = dh ** -0.5

    def one_block(qblk):
        s = jnp.einsum('bqkgd,bskd->bkgqs', qblk.astype(jnp.float32), kf) * scale
        p = jax.nn.softmax(s, axis=-1)
        return jnp.einsum('bkgqs,bskd->bqkgd', p, vf)

    o = lax.map(one_block, qb)
    o = o.transpose(1, 0, 2, 3, 4, 5).reshape(b, lq, h, v.shape[-1])
    return o.astype(q.dtype)

def _short_conv3(u, w, b):
    zero = jnp.zeros_like(u[:, :1])
    prev = jnp.concatenate([zero, u[:, :-1]], axis=1)
    nxt = jnp.concatenate([u[:, 1:], zero], axis=1)
    return w[0] * prev + w[1] * u + w[2] * nxt + b

def _hyena_spectrum(n, w1, b1, w2, b2, w3, b3, freq):
    f32 = jnp.float32
    t01 = jnp.linspace(0.0, 1.0, n, dtype=f32)
    w = (2.0 * math.pi / n) * jnp.arange(n, dtype=f32)
    bands = jnp.linspace(1e-4, FILT_BANDS - 1, FILT_BANDS, dtype=f32)
    z = jnp.concatenate([t01[:, None], jnp.cos(w[:, None] * bands[None, :]),
                         -jnp.sin(w[:, None] * bands[None, :])], axis=-1)
    fr = freq.astype(f32)
    h = jnp.sin(fr * (z @ w1.astype(f32) + b1.astype(f32)))
    h = jnp.sin(fr * (h @ w2.astype(f32) + b2.astype(f32)))
    h = (h @ w3.astype(f32) + b3.astype(f32)).reshape(n, HY_ORDER, 2, HY_DIM)
    deltas = jnp.abs(jnp.linspace(HY_MIN_DECAY, HY_MAX_DECAY, HY_DIM, dtype=f32))
    h = h * jnp.exp(-t01[:, None] * deltas[None, :])[:, None, None, :]
    h_fwd, h_bwd = h[:, :, 0], h[:, :, 1]
    filt2n = jnp.concatenate([h_fwd, jnp.zeros((1, HY_ORDER, HY_DIM), f32), h_bwd[:0:-1]], axis=0)
    filt2n = filt2n * lax.rsqrt(jnp.sum(filt2n * filt2n, axis=0, keepdims=True) + EPS)
    return jnp.fft.rfft(filt2n, axis=0)

def _hyena(u, conv_w, conv_b, spec, bias):
    n = u.shape[1]
    uc = _short_conv3(u, conv_w, conv_b)
    v, x1, x2 = jnp.split(uc, HY_ORDER + 1, axis=-1)

    def long_conv(z, spec_o, b_o):
        zf = z.astype(jnp.float32)
        y = jnp.fft.irfft(jnp.fft.rfft(zf, n=2 * n, axis=1) * spec_o[None], n=2 * n, axis=1)[:, :n]
        return y + b_o.astype(jnp.float32) * zf

    z = x1.astype(jnp.float32) * long_conv(v, spec[:, 0], bias[0])
    z = x2.astype(jnp.float32) * long_conv(z, spec[:, 1], bias[1])
    return z.astype(u.dtype)

def _moe(h, router_w, router_bias, w_gate, w_up, w_down):
    b, n, d = h.shape
    x = h.reshape(b * n, d)
    scores = jax.nn.sigmoid(jnp.dot(x.astype(jnp.float32), router_w.astype(jnp.float32)))
    sel = scores + router_bias.astype(jnp.float32)
    group_score = jnp.sum(lax.top_k(sel.reshape(-1, N_GROUPS, EXPERTS_PER_GROUP), TOP_K)[0], axis=-1)
    g_best = jnp.argmax(group_score, axis=-1)
    in_group = (jnp.arange(N_EXPERTS) // EXPERTS_PER_GROUP)[None, :] == g_best[:, None]
    _, idx = lax.top_k(jnp.where(in_group, sel, -jnp.inf), TOP_K)
    wsel = jnp.take_along_axis(scores, idx, axis=-1)
    wsel = wsel / jnp.sum(wsel, axis=-1, keepdims=True)
    gates = jnp.sum(jax.nn.one_hot(idx, N_EXPERTS, dtype=jnp.float32) * wsel[..., None], axis=1)
    a = jnp.einsum('td,edf->tef', x, w_gate)
    up = jnp.einsum('td,edf->tef', x, w_up)
    mid = jax.nn.silu(a) * up * gates[:, :, None].astype(x.dtype)
    y = jnp.einsum('tef,efd->td', mid, w_down)
    return y.reshape(b, n, d)

def setup_inputs(seed: int = 0) -> dict:
    key = jax.random.key(seed)
    ks = iter(jax.random.split(key, 64))

    def nrm(shape, scale=1.0):
        return jax.random.normal(next(ks), shape, jnp.float32) * scale

    def gain(shape):
        return 1.0 + nrm(shape, 0.02)

    return {
        'x_prompt': nrm((BATCH, SEQ, D_MODEL)),
        'x_sample': nrm((DEC_BATCH, DEC_SEQ, D_MODEL)),
        'cache_gqa_k': nrm((DEC_BATCH, N_EVEN, PAST_LEN, GQA_KV_HEADS, GQA_HEAD_DIM)),
        'cache_gqa_v': nrm((DEC_BATCH, N_EVEN, PAST_LEN, GQA_KV_HEADS, GQA_HEAD_DIM)),
        'cache_mla_ckv': nrm((DEC_BATCH, N_ODD, PAST_LEN, MLA_KV_RANK)),
        'cache_mla_krope': nrm((DEC_BATCH, N_ODD, PAST_LEN, MLA_ROPE_DIM)),
        'c': nrm((DEC_BATCH, D_MODEL)),
        'c_ctx': nrm((D_MODEL,)),
        'norm_mix': gain((DEPTH, D_MODEL)),
        'norm_ffn': gain((DEPTH, D_MODEL)),
        'w_mod': nrm((DEPTH, D_MODEL, N_MOD * D_MODEL), 0.5 * D_MODEL ** -0.5),
        'b_mod': nrm((DEPTH, N_MOD * D_MODEL), 0.02),
        'ev_w_in': nrm((N_EVEN, D_MODEL, EVEN_IN), D_MODEL ** -0.5),
        'ev_conv_w': nrm((N_EVEN, 3, (HY_ORDER + 1) * HY_DIM), 0.5),
        'ev_conv_b': nrm((N_EVEN, (HY_ORDER + 1) * HY_DIM), 0.02),
        'ev_filt_w1': nrm((N_EVEN, FILT_EMB, FILT_HIDDEN), FILT_EMB ** -0.5),
        'ev_filt_b1': nrm((N_EVEN, FILT_HIDDEN), 0.02),
        'ev_filt_w2': nrm((N_EVEN, FILT_HIDDEN, FILT_HIDDEN), FILT_HIDDEN ** -0.5),
        'ev_filt_b2': nrm((N_EVEN, FILT_HIDDEN), 0.02),
        'ev_filt_w3': nrm((N_EVEN, FILT_HIDDEN, HY_ORDER * 2 * HY_DIM), FILT_HIDDEN ** -0.5),
        'ev_filt_b3': nrm((N_EVEN, HY_ORDER * 2 * HY_DIM), 0.02),
        'ev_filt_freq': gain((N_EVEN, FILT_HIDDEN)),
        'ev_hy_bias': nrm((N_EVEN, HY_ORDER, HY_DIM), 0.5),
        'ev_q_norm': gain((N_EVEN, GQA_HEAD_DIM)),
        'ev_k_norm': gain((N_EVEN, GQA_HEAD_DIM)),
        'ev_w_out': nrm((N_EVEN, EVEN_OUT, D_MODEL), EVEN_OUT ** -0.5),
        'od_w_in': nrm((N_ODD, D_MODEL, ODD_IN), D_MODEL ** -0.5),
        'od_q_lora_norm': gain((N_ODD, MLA_Q_RANK)),
        'od_kv_lora_norm': gain((N_ODD, MLA_KV_RANK)),
        'od_w_uq': nrm((N_ODD, MLA_Q_RANK, MLA_HEADS * MLA_QK_DIM), MLA_Q_RANK ** -0.5),
        'od_w_ukv': nrm((N_ODD, MLA_KV_RANK, MLA_HEADS * (MLA_NOPE_DIM + MLA_V_DIM)), MLA_KV_RANK ** -0.5),
        'od_q_norm': gain((N_ODD, MLA_QK_DIM)),
        'od_k_norm': gain((N_ODD, MLA_QK_DIM)),
        'od_w_out': nrm((N_ODD, ODD_OUT, D_MODEL), ODD_OUT ** -0.5),
        'router_w': nrm((D_MODEL, N_EXPERTS), D_MODEL ** -0.5),
        'router_bias': nrm((N_EXPERTS,), 0.01),
        'moe_w_gate': nrm((DEPTH, N_EXPERTS, D_MODEL, D_EXPERT), D_MODEL ** -0.5),
        'moe_w_up': nrm((DEPTH, N_EXPERTS, D_MODEL, D_EXPERT), D_MODEL ** -0.5),
        'moe_w_down': nrm((DEPTH, N_EXPERTS, D_EXPERT, D_MODEL), D_EXPERT ** -0.5),
    }

def reference(x_prompt, x_sample, cache_gqa_k, cache_gqa_v, cache_mla_ckv, cache_mla_krope, c,
              c_ctx, norm_mix, norm_ffn, w_mod, b_mod,
              ev_w_in, ev_conv_w, ev_conv_b, ev_filt_w1, ev_filt_b1, ev_filt_w2, ev_filt_b2,
              ev_filt_w3, ev_filt_b3, ev_filt_freq, ev_hy_bias, ev_q_norm, ev_k_norm, ev_w_out,
              od_w_in, od_q_lora_norm, od_kv_lora_norm, od_w_uq, od_w_ukv, od_q_norm, od_k_norm, od_w_out,
              router_w, router_bias, moe_w_gate, moe_w_up, moe_w_down):

    def modulation(cond, l):
        return jax.nn.silu(cond) @ w_mod[l] + b_mod[l]

    def even_mixer(h, i, ctx_k=None, ctx_v=None):
        b, n, _ = h.shape
        u = h @ ev_w_in[i]
        s0 = (HY_ORDER + 1) * HY_DIM
        u_hy, q, k, v = jnp.split(u, [s0, s0 + GQA_Q, s0 + GQA_Q + GQA_KV], axis=-1)
        spec = _hyena_spectrum(n, ev_filt_w1[i], ev_filt_b1[i], ev_filt_w2[i], ev_filt_b2[i],
                               ev_filt_w3[i], ev_filt_b3[i], ev_filt_freq[i])
        y_hy = _hyena(u_hy, ev_conv_w[i], ev_conv_b[i], spec, ev_hy_bias[i])
        q = _rmsnorm(q.reshape(b, n, GQA_HEADS, GQA_HEAD_DIM), ev_q_norm[i])
        k = _rmsnorm(k.reshape(b, n, GQA_KV_HEADS, GQA_HEAD_DIM), ev_k_norm[i])
        v = v.reshape(b, n, GQA_KV_HEADS, GQA_HEAD_DIM)
        if ctx_k is None:
            o = _attend(q, k, v)
        else:
            q = _rope_2d(q)
            k = _rope_2d(k)
            o = _attend(q, jnp.concatenate([ctx_k, k], axis=1), jnp.concatenate([ctx_v, v], axis=1))
        y = jnp.concatenate([y_hy, o.reshape(b, n, GQA_Q)], axis=-1) @ ev_w_out[i]
        return y, (k, v)

    def mla_kv(c_kv, k_rope, i):
        b, n, _ = c_kv.shape
        kv = (c_kv @ od_w_ukv[i]).reshape(b, n, MLA_HEADS, MLA_NOPE_DIM + MLA_V_DIM)
        k_nope, v = jnp.split(kv, [MLA_NOPE_DIM], axis=-1)
        k_pe = jnp.broadcast_to(k_rope[:, :, None, :], (b, n, MLA_HEADS, MLA_ROPE_DIM))
        k = _rmsnorm(jnp.concatenate([k_nope, k_pe], axis=-1), od_k_norm[i])
        return k, v

    def odd_mixer(h, i, ctx_ckv=None, ctx_krope=None):
        b, n, _ = h.shape
        u = h @ od_w_in[i]
        c_q, c_kv, k_rope = jnp.split(u, [MLA_Q_RANK, MLA_Q_RANK + MLA_KV_RANK], axis=-1)
        c_q = _rmsnorm(c_q, od_q_lora_norm[i])
        c_kv = _rmsnorm(c_kv, od_kv_lora_norm[i])
        q = _rmsnorm((c_q @ od_w_uq[i]).reshape(b, n, MLA_HEADS, MLA_QK_DIM), od_q_norm[i])
        k, v = mla_kv(c_kv, k_rope, i)
        if ctx_ckv is not None:
            q = _rope_tail(q, MLA_NOPE_DIM)
            k = _rope_tail(k, MLA_NOPE_DIM)
            k_c, v_c = mla_kv(ctx_ckv, ctx_krope, i)
            k = jnp.concatenate([k_c, k], axis=1)
            v = jnp.concatenate([v_c, v], axis=1)
        o = _attend(q, k, v)
        return o.reshape(b, n, ODD_OUT) @ od_w_out[i], (c_kv, k_rope)

    def layer(x, l, mod, mixer):
        sh1, sc1, g1, sh2, sc2, g2 = jnp.split(mod, N_MOD, axis=-1)
        y, aux = mixer(_rmsnorm(x, norm_mix[l]) * (1.0 + sc1) + sh1)
        x = x + g1 * y
        h = _rmsnorm(x, norm_ffn[l]) * (1.0 + sc2) + sh2
        x = x + g2 * _moe(h, router_w, router_bias, moe_w_gate[l], moe_w_up[l], moe_w_down[l])
        return x, aux

    xc = x_prompt
    st_k, st_v, st_ckv, st_kr = [], [], [], []
    for l in range(DEPTH):
        i = l // 2
        mod = modulation(c_ctx, l)
        if l % 2 == 0:
            xc, (k_c, v_c) = layer(xc, l, mod, functools.partial(even_mixer, i=i))
            st_k.append(k_c)
            st_v.append(v_c)
        else:
            xc, (ckv_c, kr_c) = layer(xc, l, mod, functools.partial(odd_mixer, i=i))
            st_ckv.append(ckv_c)
            st_kr.append(kr_c)
    y_prompt = xc
    state_gqa_k = jnp.stack(st_k, axis=1)
    state_gqa_v = jnp.stack(st_v, axis=1)
    state_mla_ckv = jnp.stack(st_ckv, axis=1)
    state_mla_krope = jnp.stack(st_kr, axis=1)

    xs = x_sample
    for l in range(DEPTH):
        i = l // 2
        mod = modulation(c, l)[:, None, :]
        if l % 2 == 0:
            mixer = functools.partial(even_mixer, i=i, ctx_k=cache_gqa_k[:, i], ctx_v=cache_gqa_v[:, i])
        else:
            mixer = functools.partial(odd_mixer, i=i, ctx_ckv=cache_mla_ckv[:, i], ctx_krope=cache_mla_krope[:, i])
        xs, _ = layer(xs, l, mod, mixer)
    y_sample = xs

    return (y_prompt, y_sample, state_gqa_k, state_gqa_v, state_mla_ckv, state_mla_krope)


_drawn_inputs = setup_inputs


def setup_inputs(seed=0):
    import zlib

    import numpy as np

    out = dict(_drawn_inputs(seed))
    spreads = {}
    factors = {'cache_gqa_v': 3.049,
     'cache_mla_ckv': 2.74,
     'cache_mla_krope': 7.827,
     'ev_filt_freq': 3.438,
     'ev_q_norm': 8.0,
     'od_q_lora_norm': 8.0,
     'od_kv_lora_norm': 2.849,
     'od_q_norm': 4.945,
     'od_k_norm': 8.0}
    for name, (base, spread) in spreads.items():
        noise = np.random.default_rng([zlib.crc32(name.encode()), seed]).standard_normal(out[name].shape)
        drawn = base * np.exp(spread * noise) if base else spread * noise
        out[name] = __import__('jax').numpy.asarray(drawn.astype(out[name].dtype))
    for name, factor in factors.items():
        out[name] = (out[name] * factor).astype(out[name].dtype)
    return out
```

```python
import math
from contextlib import ExitStack

import numpy as np

import concourse.bass as bass
from concourse import mybir

F32 = mybir.dt.float32
ALU = mybir.AluOpType
ACT = mybir.ActivationFunctionType
AXX = mybir.AxisListType.X

P = 128
D = 1024
KT = D // P
NPR, NSA, PAST = 128, 256, 128
T = NPR + NSA
NT = T // P
GRP = [0, 1, 1]
EPS = 1e-6
HY = D // 2
NCH = HY // P
HID, EMB = 64, 33
QH, KVH, HD = 8, 2, 64
MH, NOPE, ROPE, VD = 16, 64, 32, 64
QK = NOPE + ROPE
QR, KVR = 256, 128
ODD_IN = QR + KVR + ROPE
HG = 4
NE, DE, NG, EPG = 16, 256, 4, 4
GRID_W = 64
RING = 9
PIECE = 2048
UNROLL = 3

TWO_PI_A = 6.28125
TWO_PI_B = float(np.float32(np.round((2 * math.pi - TWO_PI_A) * 2**20) / 2**20))
TWO_PI_C = float(2 * math.pi - TWO_PI_A - TWO_PI_B)
ROUNDER = 1.5 * 2.0**23
SIN_MAX = 3.1415925

SH1, SC1, G1, SH2, SC2, G2 = range(6)


def shape_constants():
    c = {}
    c["ident"] = np.eye(P)
    sel = np.zeros((P, 2, P))
    for g in range(4):
        for r in range(2):
            sel[32 * g + r, r, :] = 1
    c["rowsel"] = sel.reshape(P, 2 * P)
    cs = np.zeros((24, 24, 2))
    for r in range(24):
        cs[r, r, :] = 1
    c["chunksel"] = cs.reshape(24, 48)

    def odd_dft(n):
        j = np.arange(n)[:, None]
        f = np.arange(n)[None, :]
        a = np.pi * ((2 * f + 1) * j % (4 * n)) / (2 * n)
        return np.cos(a), np.sin(a)

    cp, sp = odd_dft(NPR)
    cs_, ss = odd_dft(NSA)
    c["dft_p"] = np.stack([cp, sp, cp.T / NPR, sp.T / NPR], 1).reshape(P, 4 * NPR)
    two = [m.reshape(2, P, NSA).transpose(1, 0, 2) for m in (cs_, ss, cs_.T / NSA, ss.T / NSA)]
    c["dft_s"] = np.stack(two, 1).reshape(P, 8 * NSA)

    zs, ds = [], []
    lo, hi = math.log(1e-2) / 1.5, math.log(1e-2) / 0.3
    deltas = np.abs(np.linspace(lo, hi, HY))
    for n in (NPR, NSA):
        t01 = np.linspace(0.0, 1.0, n)
        w = (2 * math.pi / n) * np.arange(n)
        bands = np.linspace(1e-4, (EMB - 1) // 2 - 1, (EMB - 1) // 2)
        zs.append(np.concatenate([t01[:, None], np.cos(w[:, None] * bands), -np.sin(w[:, None] * bands)], 1))
        ds.append(np.exp(-t01[:, None] * deltas))
    c["zT"] = np.concatenate(zs, 0).T
    c["decay"] = np.concatenate(ds, 0).reshape(NT, P, HY).transpose(1, 0, 2).reshape(P, NT * HY)

    def rope(width):
        half, npair = width // 2, width // 4
        fr = 10000.0 ** (-np.arange(npair) / npair)
        t = np.arange(NSA)
        co, si = [], []
        for pos in (t // GRID_W, t % GRID_W):
            a = pos[:, None] * fr[None, :]
            co += [np.cos(a), np.cos(a)]
            si += [-np.sin(a), np.sin(a)]
        both = np.stack([np.concatenate(co, 1), np.concatenate(si, 1)], 1)
        return both.reshape(2, P, 2, width).transpose(1, 0, 2, 3).reshape(P, 4 * width)

    c["rope_q"] = rope(HD)
    c["rope_m"] = rope(ROPE)
    return {k: np.ascontiguousarray(v, np.float32) for k, v in c.items()}


class Banks:

    def __init__(self):
        self.uses = [0] * 8
        self.turn = 0
        self.jobs = {}

    def stage(self, name, count, banks=None):
        out = []
        for i in range(count):
            if banks is None:
                b = self.turn
                self.turn = (self.turn + 1) % 8
            else:
                b = banks[i % len(banks)]
            out.append((b, self.uses[b]))
            self.uses[b] += 1
        self.jobs[name] = out

    def __getitem__(self, key):
        return self.jobs[key[0]][key[1]]


def build_step(nc, d, o):
    y_prompt, y_sample, st_k, st_v, st_ckv, st_kr = o
    units_gqa = [(t, h) for t in range(NT) for h in range(QH)]
    units_mla = [(t, h) for t in range(NT) for h in range(HG)]
    NHG = MH // HG

    B = Banks()
    BANK_S, BANK_PT, BANK_O = [0, 1, 2], [3, 4, 5], [6, 7]

    def mod_stage(l, vectors):
        for v in vectors:
            for half in range(2):
                B.stage(f"mod{l}.{v}.{half}", 1)
                B.stage(f"modsel{l}.{v}.{half}", 2 if v in (G1, G2) else 1)

    def moe_stage(l):
        mod_stage(l, (SH2, SC2))
        B.stage(f"hT{l}.1", 6)
        mod_stage(l, (G2,))
        B.stage(f"router{l}", 1)
        B.jobs[f"moe{l}"] = list(B.uses)
        for b in range(4):
            B.uses[b] += NE
        for b in range(4, 7):
            B.uses[b] += 2 * NE

    B.stage("convT", 1)
    B.stage("filt1", 1)
    B.stage("filt2", 1)
    for od in range(2):
        B.stage(f"filt3.{od}", 2 * NT)
        B.stage(f"energy{od}", 2)
        B.stage(f"spec{od}", 2 * NT)
    mod_stage(0, (SH1, SC1))
    B.stage("hT0.0", 6)
    B.stage("uT", 3 * NCH)
    B.stage("qkv", 3 * NT)
    B.stage("vtok", NT)
    B.stage("x1tok", NT)
    B.stage("fwd0", 2 * NT)
    B.stage("inv0", NT)
    B.stage("fwd1", 2 * NT)
    B.stage("inv1", NCH)
    B.stage("qT", NT * KVH)
    B.stage("kT", KVH)
    B.stage("gS", len(units_gqa), BANK_S)
    B.stage("gPT", len(units_gqa), BANK_PT)
    B.stage("gO", NT, BANK_O)
    B.stage("goT", NT)
    mod_stage(0, (G1,))
    B.stage("out0", 2 * NT)
    moe_stage(0)
    mod_stage(1, (SH1, SC1))
    B.stage("hT1.0", 6)
    B.stage("um", NT)
    B.stage("cT", NT + 1)
    for g in range(NHG):
        B.stage(f"mq{g}", NT)
        B.stage(f"mkv{g}", NT + 1)
        B.stage(f"mqT{g}", NT)
        B.stage(f"mkT{g}", NT + 1)
        B.stage(f"mS{g}", len(units_mla), BANK_S)
        B.stage(f"mPT{g}", len(units_mla), BANK_PT)
        B.stage(f"mO{g}", NT, BANK_O)
    B.stage("moT", 2 * NT)
    mod_stage(1, (G1,))
    B.stage("out1", 2 * NT)
    moe_stage(1)

    pieces, at = [], {}

    def piece(name, src, *shape):
        at[name] = len(pieces)
        pieces.append((src, shape))

    def mod_pieces(l, vectors):
        for v in vectors:
            for half in range(2):
                c0 = v * D + half * 512
                for kh in range(2):
                    w = d["w_mod"][l].rearrange("(p j) n -> p j n", j=KT)
                    piece(f"mod{l}.{v}.{half}.{kh}", w[:, 4 * kh:4 * kh + 4, c0:c0 + 512], 4, 512)

    def out_pieces(l, w):
        w = w.rearrange("(j p) n -> p j n", p=P)
        for half in range(2):
            for kh in range(2):
                piece(f"out{l}.{half}.{kh}", w[:, 4 * kh:4 * kh + 4, half * 512:half * 512 + 512], 4, 512)

    def expert_piece(l, kind, e):
        w = d[{"g": "moe_w_gate", "u": "moe_w_up", "d": "moe_w_down"}[kind]][l]
        w = w[bass.ds(e, 1), :, :]
        if kind == "d":
            return w.rearrange("e (j p) n -> p (e j) n", p=P), (2, D)
        return w.rearrange("e (p j) n -> p (e j) n", j=KT), (KT, DE)

    def moe_pieces(l):
        mod_pieces(l, (SH2, SC2))
        mod_pieces(l, (G2,))
        at[f"moe{l}"] = len(pieces)
        for kind, e in [("g", 0), ("u", 0)]:
            src, shape = expert_piece(l, kind, e)
            piece(f"moe{l}.{kind}{e}", src, *shape)
        at[f"moeloop{l}"] = len(pieces)
        pieces.extend([None] * (3 * (NE - 1)))
        src, shape = expert_piece(l, "d", NE - 1)
        piece(f"moe{l}.last", src, *shape)

    mod_pieces(0, (SH1, SC1))
    ev_in = d["ev_w_in"][0].rearrange("(p j) n -> p j n", j=KT)
    for q in range(9):
        piece(f"in0.{q}", ev_in[:, :, 256 * q:256 * q + 256], KT, 256)
    mod_pieces(0, (G1,))
    out_pieces(0, d["ev_w_out"][0])
    moe_pieces(0)
    mod_pieces(1, (SH1, SC1))
    od_in = d["od_w_in"][0].rearrange("(p j) n -> p j n", j=KT)
    for kh in range(2):
        piece(f"in1.{kh}", od_in[:, 4 * kh:4 * kh + 4, :], 4, ODD_IN)
    w_uq = d["od_w_uq"][0].rearrange("(j p) n -> p j n", p=P)
    for j in range(2):
        piece(f"uq{j}", w_uq[:, j:j + 1, :], 1, MH * QK)
    piece("ukv", d["od_w_ukv"][0].rearrange("(j p) n -> p j n", j=1), 1, MH * (NOPE + VD))
    mod_pieces(1, (G1,))
    out_pieces(1, d["od_w_out"][0])
    moe_pieces(1)

    with ExitStack() as ctx:
        def sb(name, *shape):
            return ctx.enter_context(nc.sbuf_tensor(name, list(shape), F32))

        def sem(name):
            return ctx.enter_context(nc.semaphore(name))

        ring = sb("ring", P, RING * PIECE)
        x = sb("x", P, NT, D)
        hT = sb("hT", P, KT, T)
        xn = sb("xn", P, NT, D)
        gb = sb("gb", P, 2, D)
        modrow = sb("modrow", P, 512)
        ident = sb("ident", P, P)
        rowsel = sb("rowsel", P, 2, P)
        chunksel = sb("chunksel", 24, 24, 2)
        bmod = sb("bmod", 24, 512)
        condraw = sb("condraw", P, 2, KT)
        condT = sb("condT", P, KT, 32)
        modT = sb("modT", P, 2, 6, KT, 2)
        modA = sb("modA", P, 2, 2, KT, 2)
        gain = sb("gain", P, 2, 2, KT)
        routw = sb("routw", P, KT, NE)
        routb = sb("routb", P, NE)
        rank_e = sb("rank_e", P, NE)
        ssq = sb("ssq", P, 4, NT)
        gates = sb("gates", P, NT, NE)
        statA = sb("statA", P, 2, 40)
        negmax = sb("negmax", P, len(units_gqa))
        psumexp = sb("psumexp", P, len(units_gqa))
        rinv = sb("rinv", P, QH)
        ropeq = sb("ropeq", P, 2, 2, HD)
        qkgain = sb("qkgain", P, 2, HD)
        ck = sb("ck", P, KVH * HD)
        cv = sb("cv", P, KVH * HD)
        filtc = sb("filtc", HID, 3 + 2 * HID)
        convT = sb("convT", P, 4, 3 * NCH)

        arena = sb("arena", P, 20224)

        def view(off, *shape, parts=P):
            n = int(np.prod(shape))
            v = arena[0:parts, off:off + n]
            if len(shape) == 2:
                return v.rearrange("p (a b) -> p a b", b=shape[1])
            if len(shape) == 3:
                return v.rearrange("p (a b c) -> p a b c", b=shape[1], c=shape[2])
            if len(shape) == 4:
                return v.rearrange("p (a b c e) -> p a b c e", b=shape[1], c=shape[2], e=shape[3])
            return v

        H = view(0, 2, 2, NT, HY)
        uc = view(6144, 3 * NCH, T)
        dftp = view(10752, 4, NPR)
        dfts = view(11264, 4, 2, NSA)
        uT = view(13312, 3 * NCH, T)
        qkv = view(17920, NT, QH * HD + 2 * KVH * HD)
        filt = view(6144, NT, 2, HY)
        decay = view(9216, NT, HY)
        w3 = view(13312, 4, HY, parts=HID + 1)
        convraw = view(15360, P, parts=48)
        esc = view(15488, 2, HY)
        hidden = view(16512, T, parts=HID + 1)
        turns = view(16896, T, parts=HID)
        zT = view(17280, T, parts=EMB)
        sqs = view(17664, NT, HY)
        sqd = view(19200, HY)
        onesm = view(19712, P)
        Y = view(13312, NT, 2, HY)
        tmpa = view(16384, HY)
        tmpb = view(16896, HY)
        hybias = gb[:, :, 0:HY]
        vtok = xn[:, :, 0:HY]
        x1tok = xn[:, :, HY:D]
        qT = view(0, NT, QH, P, parts=HD)
        kT = view(3072, KVH, 4, P, parts=HD)
        probs = view(4096, 2, T)
        probsT = view(4864, 2, 3, P)
        scratch = gb[:, :, :].rearrange("p a b -> p (a b)")
        qsq = scratch[:, 0:(QH + KVH) * HD].rearrange("p (h e) -> p h e", e=HD)
        qrb = scratch[:, 640:640 + (QH + KVH) * HD].rearrange("p (h e) -> p h e", e=HD)
        otok = xn[:, :, 0:HY]
        um = view(0, NT, ODD_IN)
        cT = view(1248, 3, T)
        cvT = view(2400, P)
        ckv_c = view(2528, KVR)
        kr_c = view(2656, ROPE)
        lgain = view(2688, QR + KVR)
        mgain = view(3072, 2, QK)
        ropem = view(3264, 2, 2, ROPE)
        q4 = view(3392, NT, HG, QK)
        k4 = view(4544, NT + 1, HG, QK)
        v4 = view(6080, NT + 1, HG, VD)
        q4T = view(7104, NT, HG, P, parts=QK)
        k4T = view(8640, HG, NT + 1, P, parts=QK)
        mprobs = view(10688, 2, T)
        mprobsT = view(11456, 2, 3, P)
        msq = view(12224, NT + 1, HG, QK)
        mrb = view(13760, 2, HG, ROPE)
        mtok = xn
        acc = xn
        sil = view(14080, 2, T)
        mid = view(14848, UNROLL, 2, T)
        sml = view(17152, 8, 72)

        ps = [ctx.enter_context(nc.psum_tensor(f"ps{b}", [P, 512], F32)) for b in range(8)]
        filled = [sem(f"filled{b}") for b in range(8)]
        drained = [sem(f"drained{b}") for b in range(8)]
        piece_full = [sem(f"piece_full{s}") for s in range(RING)]
        piece_used = sem("piece_used")
        in_cond, in_x, in_mod, in_filt, in_dft, in_conv, in_attn, in_mla = (
            sem(n) for n in ("in_cond", "in_x", "in_mod", "in_filt", "in_dft", "in_conv", "in_attn", "in_mla"))
        cond_zero, cond_ready = sem("cond_zero"), sem("cond_ready")
        ones_set = sem("ones_set")
        modrow_used = sem("modrow_used")
        moda_ready = sem("moda_ready")
        squares = sem("squares")
        meansq = sem("meansq")
        rootsq = sem("rootsq")
        xn_ready = sem("xn_ready")
        sin_arg, sin_done = sem("sin_arg"), sem("sin_done")
        filt_ready, esq_ready, eroot, escale_ready = sem("filt_ready"), sem("esq_ready"), sem("eroot"), sem("escale_ready")
        spec_done = sem("spec_done")
        conv_copied, conv_done = sem("conv_copied"), sem("conv_done")
        y_ready = sem("y_ready")
        qsq_ready, qvar, qroot, qk_ready = sem("qsq_ready"), sem("qvar"), sem("qroot"), sem("qk_ready")
        negmax_ready = sem("negmax_ready")
        pv_done = sem("pv_done")
        x_mixed = sem("x_mixed")
        x_done = sem("x_done")
        score_ready = sem("score_ready")
        gates_ready = sem("gates_ready")
        acc_zero = sem("acc_zero")
        lora_sq, lora_var, lora_root, lora_ready = sem("lora_sq"), sem("lora_var"), sem("lora_root"), sem("lora_ready")
        stored = sem("stored")

        def ring_view(i, shape):
            s = (i % RING) * PIECE
            n = shape[0] * shape[1]
            return ring[:, s:s + n].rearrange("p (a b) -> p a b", b=shape[1])

        def filled_wait(eng, stage, i=0):
            b, n = B[stage, i]
            eng.wait_ge(filled[b], n + 1)
            return ps[b]

        def drained_wait(eng, stage, i=0):
            b, n = B[stage, i]
            eng.wait_ge(drained[b], n + 1)

        def drain_inc(ins, stage, i=0):
            ins.then_inc(drained[B[stage, i][0]], 1)

        consts_loaded = {}

        def load(eng, s, dst, src):
            eng.dma_start(dst, src).then_inc(s, 16)
            consts_loaded[s.name] = consts_loaded.get(s.name, 0) + 16

        LOADS = {"in_cond": 2, "in_x": 2, "in_mod": 9, "in_filt": 11, "in_dft": 2, "in_conv": 2, "in_attn": 6, "in_mla": 7}

        def loaded(eng, s):
            eng.wait_ge(s, 16 * LOADS[s.name])

        block = ctx.enter_context(nc.Block())

        @block.sync
        def _(sp):
            def send(i, src, shape, wait):
                if wait is not None:
                    sp.wait_ge(piece_used, wait)
                sp.dma_start(ring_view(i, shape), src).then_inc(piece_full[i % RING], 16)

            i = 0
            while i < len(pieces):
                if pieces[i] is not None:
                    src, shape = pieces[i]
                    send(i, src, shape, i - RING + 1 if i >= RING else None)
                    i += 1
                    continue
                l = 0 if i == at["moeloop0"] else 1
                with sp.Fori(0, (NE - 1) // UNROLL) as it:
                    for u in range(UNROLL):
                        for q, (kind, back) in enumerate((("g", 0), ("u", 0), ("d", 1))):
                            src, shape = expert_piece(l, kind, it * UNROLL + (u + 1 - back))
                            n = i + 3 * u + q
                            send(n, src, shape, it * RING + (n - RING + 1))
                i += 3 * (NE - 1)

        @block.gpsimd
        def _(pool):
            pool.memset(condT[:, :, :], 0.0).then_inc(cond_zero, 1)
            load(pool, in_dft, dftp, d["dft_p"].rearrange("p (a b) -> p a b", b=NPR))
            load(pool, in_dft, dfts, d["dft_s"].rearrange("p (a b c) -> p a b c", b=2, c=NSA))
            load(pool, in_attn, ropeq[:, :, :, :], d["rope_q"].rearrange("p (a b c) -> p a b c", b=2, c=HD))
            load(pool, in_attn, qkgain[:, 0, :], d["ev_q_norm"][0].partition_broadcast(P))
            load(pool, in_attn, qkgain[:, 1, :], d["ev_k_norm"][0].partition_broadcast(P))
            load(pool, in_attn, ck[:, :], d["cache_gqa_k"][0, 0].rearrange("t h e -> t (h e)"))
            load(pool, in_attn, cv[:, :], d["cache_gqa_v"][0, 0].rearrange("t h e -> t (h e)"))
            load(pool, in_attn, routb[:, :], d["router_bias"].partition_broadcast(P))
            pool.wait_ge(qk_ready, 1)
            pool.dma_start(st_k[0, 0].rearrange("t h e -> t (h e)"), qkv[:, 0, QH * HD:QH * HD + KVH * HD]).then_inc(stored, 16)
            pool.dma_start(st_v[0, 0].rearrange("t h e -> t (h e)"), qkv[:, 0, QH * HD + KVH * HD:]).then_inc(stored, 16)
            for l in range(2):
                for i in range(6):
                    drained_wait(pool, f"hT{l}.1", i)
                pool.memset(acc[:, :, :], 0.0).then_inc(acc_zero, 1)
                if l == 1:
                    break
                load(pool, in_mla, ckv_c, d["cache_mla_ckv"][0, 0])
                load(pool, in_mla, kr_c, d["cache_mla_krope"][0, 0])
                load(pool, in_mla, lgain[:, 0:QR], d["od_q_lora_norm"][0].partition_broadcast(P))
                load(pool, in_mla, lgain[:, QR:QR + KVR], d["od_kv_lora_norm"][0].partition_broadcast(P))
                load(pool, in_mla, mgain[:, 0, :], d["od_q_norm"][0].partition_broadcast(P))
                load(pool, in_mla, mgain[:, 1, :], d["od_k_norm"][0].partition_broadcast(P))
                load(pool, in_mla, ropem, d["rope_m"].rearrange("p (a b c) -> p a b c", b=2, c=ROPE))
                pool.wait_ge(lora_ready, 1)
                pool.dma_start(st_ckv[0, 0], um[:, 0, QR:QR + KVR]).then_inc(stored, 16)
                pool.dma_start(st_kr[0, 0], um[:, 0, QR + KVR:]).then_inc(stored, 16)
            pool.wait_ge(x_done, 2)
            pool.dma_start(y_prompt[0], x[:, 0, :]).then_inc(stored, 16)
            pool.dma_start(y_sample[0].rearrange("(t p) n -> p t n", p=P), x[:, 1:NT, :]).then_inc(stored, 16)
            pool.wait_ge(stored, 16 * 6)

        @block.tensor
        def _(pe):
            def claim(stage, i=0):
                b, n = B[stage, i]
                if n:
                    pe.wait_ge(drained[b], n)
                return ps[b]

            def fill_inc(ins, stage, i=0):
                ins.then_inc(filled[B[stage, i][0]], 1)

            def weights(name, shape):
                i = at[name]
                pe.wait_ge(piece_full[i % RING], 16 * (i // RING + 1))
                return ring_view(i, shape)

            due = [0]

            def piece_end(count=1):
                due[0] += count

            def product(out, lhsT, rhs, **kw):
                mm = pe.matmul(out, lhsT, rhs, **kw)
                if due[0]:
                    mm.then_inc(piece_used, due[0])
                    due[0] = 0
                return mm

            def turn(out, src):
                mm = pe.transpose(out, src, ident[:, :])
                if due[0]:
                    mm.then_inc(piece_used, due[0])
                    due[0] = 0
                return mm

            def mod_vectors(l, vectors):
                for v in vectors:
                    for half in range(2):
                        name = f"mod{l}.{v}.{half}"
                        bank = claim(name)
                        if l == 0 and v == SH1 and half == 0:
                            loaded(pe, in_mod)
                            pe.wait_ge(cond_ready, 2)
                        for kh in range(2):
                            w = weights(f"{name}.{kh}", (4, 512))
                            for g in range(4):
                                mm = product(bank[32 * g:32 * g + 32, :], condT[:, 4 * kh + g, :], w[:, g, :],
                                             start=kh == 0, stop=kh == 1)
                            if kh == 0:
                                mm.then_inc(piece_used, 1)
                                product(bank[0:2, :], chunksel[:, l * 12 + 2 * v + half, :], bmod[:, :], start=False, stop=False)
                        fill_inc(mm, name)
                        piece_end()
                        drained_wait(pe, name)
                        sel = f"modsel{l}.{v}.{half}"
                        if v in (G1, G2):
                            for c in range(2):
                                bank = claim(sel, c)
                                for n0 in (0, 256):
                                    mm = product(bank[:, n0:n0 + 256], rowsel[:, c, :], modrow[:, n0:n0 + 256], start=True, stop=True)
                                fill_inc(mm, sel, c)
                        else:
                            bank = claim(sel)
                            for j in range(KT):
                                mm = product(bank[64 * half:64 * half + 64, 2 * j:2 * j + 2],
                                               modrow[:, j::KT], rowsel[:, :, 0], start=True, stop=True)
                            fill_inc(mm, sel)

            def norm_transposes(l, which):
                stage = f"hT{l}.{which}"
                for t in range(NT):
                    pe.wait_ge(xn_ready, (2 * l + which) * NT + t + 1)
                    for q in range(2):
                        bank = claim(stage, 2 * t + q)
                        for j in range(4):
                            mm = turn(bank[:, j * P:(j + 1) * P], xn[:, t, 4 * q + j::KT])
                        fill_inc(mm, stage, 2 * t + q)

            def out_projection(l):
                for half in range(2):
                    for i in range(NT):
                        claim(f"out{l}", half * NT + i)
                    for kh in range(2):
                        w = weights(f"out{l}.{half}.{kh}", (4, 512))
                        for t in range(NT):
                            bank = ps[B[f"out{l}", half * NT + t][0]]
                            for k in range(4):
                                mm = product(bank[:, :], hT[:, 4 * kh + k, t * P:(t + 1) * P], w[:, k, :],
                                               start=kh == 0 and k == 0, stop=kh == 1 and k == 3)
                            if kh == 1:
                                fill_inc(mm, f"out{l}", half * NT + t)
                        if kh == 0:
                            mm.then_inc(piece_used, 1)
                    piece_end()

            def attention(tag, units, heads_n, lhs_q, rhs_k, v_of):
                n = len(units)
                pT = probsT if tag == "g" else mprobsT
                pr = probs if tag == "g" else mprobs
                S, PT, O = f"{tag}S", f"{tag}PT", f"{tag}O"
                if tag != "g":
                    S, PT, O = f"mS{tag}", f"mPT{tag}", f"mO{tag}"
                for i in range(n + 2):
                    if i < n:
                        t, h = units[i]
                        nk = P if t == 0 else T
                        bank = claim(S, i)
                        mm = product(bank[:, 0:nk], lhs_q(t, h), rhs_k(t, h), start=True, stop=True)
                        fill_inc(mm, S, i)
                    if 1 <= i <= n:
                        j = i - 1
                        t, h = units[j]
                        bank = claim(PT, j)
                        drained_wait(pe, S, j)
                        for kt in range(1 if t == 0 else NT):
                            mm = turn(bank[:, kt * P:(kt + 1) * P], pr[:, j % 2, kt * P:(kt + 1) * P])
                        fill_inc(mm, PT, j)
                    if i >= 2:
                        j = i - 2
                        t, h = units[j]
                        drained_wait(pe, PT, j)
                        if h == 0:
                            claim(O, t)
                        bank = ps[B[O, t][0]]
                        vs = v_of(t, h)
                        for kt, v in enumerate(vs):
                            mm = product(bank[:, h * HD:(h + 1) * HD], pT[:, j % 2, kt, :], v,
                                           start=kt == 0, stop=kt == len(vs) - 1)
                        if h == heads_n - 1:
                            fill_inc(mm, O, t)
                        else:
                            mm.then_inc(pv_done, 1)

            def experts(l):
                base = B.jobs[f"moe{l}"]
                i0 = at[f"moe{l}"]

                def gate_up(n, it):
                    for q in range(2):
                        i = (i0 + q) if n == 0 else at[f"moeloop{l}"] + 3 * (n - 1) + q
                        pe.wait_ge(piece_full[i % RING], it * 16 + 16 * (i // RING + 1))
                        w = ring_view(i, (KT, DE))
                        for ft in range(2):
                            b = 2 * q + ft
                            if base[b] + n:
                                pe.wait_ge(drained[b], it * UNROLL + base[b] + n)
                            for k in range(KT):
                                mm = product(ps[b][:, 0:T], w[:, k, ft * P:(ft + 1) * P], hT[:, k, :],
                                               start=k == 0, stop=k == KT - 1)
                            mm.then_inc(filled[b], 1)
                        piece_end()

                def down(n, it, i):
                    pe.wait_ge(piece_full[i % RING], it * 16 + 16 * (i // RING + 1))
                    for b in (2, 3):
                        pe.wait_ge(drained[b], it * UNROLL + base[b] + n + 1)
                    w = ring_view(i, (2, D))
                    for c in range(2 * NT):
                        t, half = c % NT, c // NT
                        b = 4 + c % 3
                        if base[b] + 2 * n + c // 3:
                            pe.wait_ge(drained[b], it * (2 * UNROLL) + base[b] + 2 * n + c // 3)
                        for ft in range(2):
                            mm = product(ps[b][:, :], mid[:, n % UNROLL, ft, t * P:(t + 1) * P],
                                           w[:, ft, half * 512:half * 512 + 512], start=ft == 0, stop=ft == 1)
                        mm.then_inc(filled[b], 1)
                    piece_end()

                gate_up(0, 0)
                with pe.Fori(0, (NE - 1) // UNROLL) as it:
                    for u in range(UNROLL):
                        gate_up(u + 1, it)
                        down(u, it, at[f"moeloop{l}"] + 3 * u + 2)
                down(NE - 1, 0, at[f"moe{l}.last"])

            def moe(l):
                mod_vectors(l, (SH2, SC2))
                norm_transposes(l, 1)
                mod_vectors(l, (G2,))
                for i in range(6):
                    drained_wait(pe, f"hT{l}.1", i)
                bank = claim(f"router{l}")
                for t in range(NT):
                    for k in range(KT):
                        mm = product(bank[:, t * NE:(t + 1) * NE], hT[:, k, t * P:(t + 1) * P], routw[:, k, :],
                                       start=k == 0, stop=k == KT - 1)
                fill_inc(mm, f"router{l}")
                experts(l)

            loaded(pe, in_conv)
            bank = claim("convT")
            mm = pe.transpose(bank[:, 0:48], convraw, ident[0:48, 0:48])
            fill_inc(mm, "convT")

            loaded(pe, in_filt)
            bank = claim("filt1")
            mm = product(bank[0:HID, 0:T], filtc[0:EMB, 3 + HID:3 + 2 * HID], zT, start=True, stop=True)
            fill_inc(mm, "filt1")
            pe.wait_ge(sin_done, 1)
            bank = claim("filt2")
            mm = product(bank[0:HID, 0:T], filtc[:, 3:3 + HID], hidden[0:HID, :], start=True, stop=True)
            fill_inc(mm, "filt2")
            pe.wait_ge(sin_done, 2)
            pe.wait_ge(ones_set, 1)
            for od in range(2):
                for t in range(NT):
                    for r in range(2):
                        bank = claim(f"filt3.{od}", 2 * t + r)
                        mm = product(bank[:, :], hidden[:, t * P:(t + 1) * P], w3[:, 2 * od + r, :], start=True, stop=True)
                        fill_inc(mm, f"filt3.{od}", 2 * t + r)
                for g, tiles in enumerate(([0], [1, 2])):
                    bank = claim(f"energy{od}", g)
                    for t in tiles:
                        pe.wait_ge(esq_ready, od * NT + t + 1)
                        mm = product(bank[:, :], onesm, sqs[:, t, :], start=t == tiles[0], stop=t == tiles[-1])
                    fill_inc(mm, f"energy{od}", g)
                if od == 0:
                    loaded(pe, in_dft)
                pe.wait_ge(filt_ready, (od + 1) * NT)
                for r in range(2):
                    bank = claim(f"spec{od}", r)
                    mm = product(bank[:, :], dftp[:, r, :], filt[:, 0, r, :], start=True, stop=True)
                    fill_inc(mm, f"spec{od}", r)
                for ft in range(2):
                    for r in range(2):
                        bank = claim(f"spec{od}", 2 + 2 * ft + r)
                        for k in range(2):
                            mm = product(bank[:, :], dfts[:, r, k, ft * P:(ft + 1) * P], filt[:, 1 + k, r, :],
                                           start=k == 0, stop=k == 1)
                        fill_inc(mm, f"spec{od}", 2 + 2 * ft + r)

            mod_vectors(0, (SH1, SC1))
            norm_transposes(0, 0)
            for i in range(6):
                drained_wait(pe, "hT0.0", i)
            pe.wait_ge(spec_done, 12)
            for q in range(9):
                w = weights(f"in0.{q}", (KT, 256))
                if q < 6:
                    for mt in range(2):
                        bank = claim("uT", 2 * q + mt)
                        for k in range(KT):
                            mm = product(bank[:, 0:T], w[:, k, mt * P:(mt + 1) * P], hT[:, k, :], start=k == 0, stop=k == KT - 1)
                        fill_inc(mm, "uT", 2 * q + mt)
                else:
                    for t in range(NT):
                        i = (q - 6) * NT + t
                        bank = claim("qkv", i)
                        for k in range(KT):
                            mm = product(bank[:, 0:256], hT[:, k, t * P:(t + 1) * P], w[:, k, :], start=k == 0, stop=k == KT - 1)
                        fill_inc(mm, "qkv", i)
                piece_end()

            for part, stage in enumerate(("vtok", "x1tok")):
                pe.wait_ge(conv_done, NCH * (part + 1))
                for t in range(NT):
                    bank = claim(stage, t)
                    for c in range(NCH):
                        mm = turn(bank[:, c * P:(c + 1) * P], uc[:, part * NCH + c, t * P:(t + 1) * P])
                    fill_inc(mm, stage, t)
            for od in range(2):
                if od == 0:
                    for t in range(NT):
                        drained_wait(pe, "vtok", t)
                else:
                    for t in range(NT):
                        drained_wait(pe, "inv0", t)
                for ft in range(NT):
                    for r in range(2):
                        i = 2 * ft + r
                        bank = claim(f"fwd{od}", i)
                        if ft == 0:
                            mm = product(bank[:, :], dftp[:, r, :], vtok[:, 0, :], start=True, stop=True)
                        else:
                            for k in range(2):
                                mm = product(bank[:, :], dfts[:, r, k, (ft - 1) * P:ft * P], vtok[:, 1 + k, :],
                                               start=k == 0, stop=k == 1)
                        fill_inc(mm, f"fwd{od}", i)
                if od == 0:
                    for t in range(NT):
                        pe.wait_ge(y_ready, 1 if t == 0 else NT)
                        bank = claim("inv0", t)
                        if t == 0:
                            for r in range(2):
                                mm = product(bank[:, :], dftp[:, 2 + r, :], Y[:, 0, r, :], start=r == 0, stop=r == 1)
                        else:
                            for f in range(2):
                                for r in range(2):
                                    mm = product(bank[:, :], dfts[:, 2 + r, f, (t - 1) * P:t * P], Y[:, 1 + f, r, :],
                                                   start=f + r == 0, stop=f + r == 2)
                        fill_inc(mm, "inv0", t)
                else:
                    pe.wait_ge(y_ready, 2 * NT)
                    for c in range(NCH):
                        bank = claim("inv1", c)
                        for r in range(2):
                            mm = product(bank[:, 0:NPR], Y[:, 0, r, c * P:(c + 1) * P], dftp[:, 2 + r, :],
                                           start=r == 0, stop=r == 1)
                        for f in range(2):
                            for r in range(2):
                                mm = product(bank[:, NPR:T], Y[:, 1 + f, r, c * P:(c + 1) * P], dfts[:, 2 + r, f, :],
                                               start=f + r == 0, stop=f + r == 2)
                        fill_inc(mm, "inv1", c)

            pe.wait_ge(qk_ready, NT)
            for t in range(NT):
                for g in range(KVH):
                    bank = claim("qT", KVH * t + g)
                    for h in range(4):
                        c0 = (4 * g + h) * HD
                        mm = turn(bank[0:HD, h * P:(h + 1) * P], qkv[:, t, c0:c0 + HD])
                    fill_inc(mm, "qT", KVH * t + g)
            loaded(pe, in_attn)
            for g in range(KVH):
                bank = claim("kT", g)
                c0 = QH * HD + g * HD
                srcs = [qkv[:, 0, c0:c0 + HD], ck[:, g * HD:(g + 1) * HD], qkv[:, 1, c0:c0 + HD], qkv[:, 2, c0:c0 + HD]]
                for s, src in enumerate(srcs):
                    mm = turn(bank[0:HD, s * P:(s + 1) * P], src)
                fill_inc(mm, "kT", g)
            for i in range(NT * KVH):
                drained_wait(pe, "qT", i)
            for g in range(KVH):
                drained_wait(pe, "kT", g)

            def gqa_v(t, h):
                c0 = (QH + KVH) * HD + (h // 4) * HD
                own = [qkv[:, s, c0:c0 + HD] for s in range(NT)]
                cached = cv[:, (h // 4) * HD:(h // 4 + 1) * HD]
                return [own[0]] if t == 0 else [cached, own[1], own[2]]

            attention("g", units_gqa, QH, lambda t, h: qT[:, t, h, :],
                      lambda t, h: kT[:, h // 4, 0, :] if t == 0 else kT[:, h // 4, 1:4, :].rearrange("p a b -> p (a b)"), gqa_v)
            for t in range(NT):
                drained_wait(pe, "gO", t)
                bank = claim("goT", t)
                for c in range(4):
                    mm = turn(bank[:, c * P:(c + 1) * P], otok[:, t, c * P:(c + 1) * P])
                fill_inc(mm, "goT", t)
            mod_vectors(0, (G1,))
            for c in range(NCH):
                drained_wait(pe, "inv1", c)
            for t in range(NT):
                drained_wait(pe, "goT", t)
            out_projection(0)
            moe(0)

            mod_vectors(1, (SH1, SC1))
            norm_transposes(1, 0)
            for i in range(6):
                drained_wait(pe, "hT1.0", i)
            for t in range(NT):
                claim("um", t)
            for kh in range(2):
                w = weights(f"in1.{kh}", (4, ODD_IN))
                for t in range(NT):
                    bank = ps[B["um", t][0]]
                    for k in range(4):
                        mm = product(bank[:, 0:ODD_IN], hT[:, 4 * kh + k, t * P:(t + 1) * P], w[:, k, :],
                                       start=kh == 0 and k == 0, stop=kh == 1 and k == 3)
                    if kh == 1:
                        fill_inc(mm, "um", t)
                piece_end()
            pe.wait_ge(lora_ready, NT)
            loaded(pe, in_mla)
            for t in range(NT + 1):
                bank = claim("cT", t)
                srcs = [ckv_c] if t == NT else [um[:, t, c * P:(c + 1) * P] for c in range(3)]
                for c, src in enumerate(srcs):
                    mm = turn(bank[:, c * P:(c + 1) * P], src)
                fill_inc(mm, "cT", t)
            for t in range(NT + 1):
                drained_wait(pe, "cT", t)
            wq = [weights(f"uq{j}", (1, MH * QK)) for j in range(2)]
            wkv = weights("ukv", (1, MH * (NOPE + VD)))
            for g in range(NHG):
                for t in range(NT):
                    bank = claim(f"mq{g}", t)
                    for k in range(2):
                        mm = product(bank[:, 0:HG * QK], cT[:, k, t * P:(t + 1) * P],
                                       wq[k][:, 0, g * HG * QK:(g + 1) * HG * QK], start=k == 0, stop=k == 1)
                    fill_inc(mm, f"mq{g}", t)
                for t in range(NT + 1):
                    bank = claim(f"mkv{g}", t)
                    lhs = cvT if t == NT else cT[:, 2, t * P:(t + 1) * P]
                    mm = product(bank[:, :], lhs, wkv[:, 0, g * 512:(g + 1) * 512], start=True, stop=True)
                    fill_inc(mm, f"mkv{g}", t)
                if g == NHG - 1:
                    piece_end(3)
                pe.wait_ge(qk_ready, NT + 2 * (g + 1))
                for t in range(NT):
                    bank = claim(f"mqT{g}", t)
                    for h in range(HG):
                        mm = turn(bank[0:QK, h * P:(h + 1) * P], q4[:, t, h, :])
                    fill_inc(mm, f"mqT{g}", t)
                for s, t in enumerate((0, 3, 1, 2)):
                    bank = claim(f"mkT{g}", s)
                    for h in range(HG):
                        mm = turn(bank[0:QK, h * P:(h + 1) * P], k4[:, t, h, :])
                    fill_inc(mm, f"mkT{g}", s)
                for t in range(NT):
                    drained_wait(pe, f"mqT{g}", t)
                for t in range(NT + 1):
                    drained_wait(pe, f"mkT{g}", t)
                attention(str(g), units_mla, HG, lambda t, h: q4T[:, t, h, :],
                          lambda t, h: k4T[:, h, 0, :] if t == 0 else k4T[:, h, 1:4, :].rearrange("p a b -> p (a b)"),
                          lambda t, h: [v4[:, s, h, :] for s in ((0,) if t == 0 else (3, 1, 2))])
            for g in range(NHG):
                for t in range(NT):
                    drained_wait(pe, f"mO{g}", t)
            for t in range(NT):
                for q in range(2):
                    bank = claim("moT", 2 * t + q)
                    for c in range(4):
                        mm = turn(bank[:, c * P:(c + 1) * P], mtok[:, t, (4 * q + c) * P:(4 * q + c + 1) * P])
                    fill_inc(mm, "moT", 2 * t + q)
            mod_vectors(1, (G1,))
            for i in range(2 * NT):
                drained_wait(pe, "moT", i)
            out_projection(1)
            moe(1)

        @block.scalar
        def _(act):
            load(act, in_cond, condraw[:, 0, :], d["c_ctx"].rearrange("(p j) -> p j", j=KT))
            load(act, in_cond, condraw[:, 1, :], d["c"][0].rearrange("(p j) -> p j", j=KT))
            load(act, in_filt, zT, d["zT"])
            load(act, in_filt, filtc[0:EMB, 3 + HID:3 + 2 * HID], d["ev_filt_w1"][0])
            load(act, in_filt, filtc[:, 0:1], d["ev_filt_b1"].rearrange("a n -> n a"))
            load(act, in_filt, filtc[:, 1:2], d["ev_filt_b2"].rearrange("a n -> n a"))
            load(act, in_filt, filtc[:, 2:3], d["ev_filt_freq"].rearrange("a n -> n a"))
            load(act, in_filt, filtc[:, 3:3 + HID], d["ev_filt_w2"][0])
            load(act, in_filt, w3[0:HID, :, :], d["ev_filt_w3"][0].rearrange("k (a b) -> k a b", b=HY))
            load(act, in_filt, w3[HID:HID + 1, :, :], d["ev_filt_b3"].rearrange("k (a b) -> k a b", b=HY))
            load(act, in_filt, decay, d["decay"].rearrange("p (a b) -> p a b", b=HY))
            load(act, in_filt, hybias[:, 0, :], d["ev_hy_bias"][0, 0].partition_broadcast(P))
            load(act, in_filt, hybias[:, 1, :], d["ev_hy_bias"][0, 1].partition_broadcast(P))
            load(act, in_mod, ident[:, :], d["ident"])
            load(act, in_mod, rowsel[:, :, :], d["rowsel"].rearrange("p (a b) -> p a b", b=P))
            load(act, in_mod, chunksel[:, :, :], d["chunksel"].rearrange("p (a b) -> p a b", b=2))
            load(act, in_mod, bmod[:, :], d["b_mod"].rearrange("l (c n) -> (l c) n", n=512))
            for l in range(2):
                load(act, in_mod, gain[:, l, 0, :], d["norm_mix"][l].rearrange("(p j) -> p j", j=KT))
                load(act, in_mod, gain[:, l, 1, :], d["norm_ffn"][l].rearrange("(p j) -> p j", j=KT))
            load(act, in_mod, routw[:, :, :], d["router_w"].rearrange("(p j) n -> p j n", j=KT))
            load(act, in_conv, convraw[0:36, :], d["ev_conv_w"][0].rearrange("k (c n) -> (k c) n", n=P))
            load(act, in_conv, convraw[36:48, :], d["ev_conv_b"][0].rearrange("(c n) -> c n", n=P))
            load(act, in_x, x[:, 0, :], d["x_prompt"][0])
            load(act, in_x, x[:, 1:NT, :], d["x_sample"][0].rearrange("(t p) n -> p t n", p=P))

            loaded(act, in_cond)
            act.wait_ge(cond_zero, 1)
            for c in range(2):
                act.activation(condT[:, :, c], condraw[:, c, :], ACT.Silu).then_inc(cond_ready, 1)

            def copy_out(stage, i, dst, src, **kw):
                filled_wait(act, stage, i)
                drain_inc(act.activation(dst, src, kw.pop("func", ACT.Copy), **kw), stage, i)

            def bank_of(stage, i=0):
                return ps[B[stage, i][0]]

            def mod_rows(l, vectors):
                for v in vectors:
                    for half in range(2):
                        name = f"mod{l}.{v}.{half}"
                        bank = filled_wait(act, name)
                        drain_inc(act.activation(modrow[:, :], bank[:, :], ACT.Copy), name)
                        if v in (G1, G2):
                            for c in range(2):
                                sel = f"modsel{l}.{v}.{half}"
                                copy_out(sel, c, gb[:, c, half * 512:half * 512 + 512], bank_of(sel, c)[:, :])

            def norm(l, which, x_sem, x_count):
                s = 2 * l + which
                act.wait_ge(x_sem, x_count)
                for t in range(NT):
                    ins = act.activation(xn[:, t, :], x[:, t, :], ACT.Square, accum_out=ssq[:, s, t:t + 1])
                ins.then_inc(squares, 1)
                act.wait_ge(meansq, s + 1)
                act.activation(ssq[:, s, :], ssq[:, s, :], ACT.Sqrt).then_inc(rootsq, 1)

            def modulate(l, which):
                act.wait_ge(moda_ready, 2 * l + which + 1)
                sh = 0 if which == 0 else 3
                for i in range(0, 6, 2):
                    t, q = i // 2, i % 2
                    bank = filled_wait(act, f"hT{l}.{which}", i)
                    for j in range(4):
                        k = 4 * q + j
                        ins = act.activation(hT[:, k, t * P:(t + 1) * P], bank[:, j * P:(j + 1) * P], ACT.Identity,
                                             bias=modT[:, l, sh, k, GRP[t]:GRP[t] + 1],
                                             scale=modA[:, l, which, k, GRP[t]:GRP[t] + 1])
                    drain_inc(ins, f"hT{l}.{which}", i)

            def attention(tag, units):
                S, PT = (f"{tag}S", f"{tag}PT") if tag == "g" else (f"mS{tag}", f"mPT{tag}")
                pr = probs if tag == "g" else mprobs
                first = 0 if tag == "g" else len(units_gqa) + int(tag) * len(units_mla)
                for i, (t, h) in enumerate(units):
                    nk = P if t == 0 else T
                    act.wait_ge(negmax_ready, first + i + 1)
                    if i >= 2:
                        filled_wait(act, PT, i - 2)
                    bank = bank_of(S, i)
                    ins = act.activation(pr[:, i % 2, 0:nk], bank[:, 0:nk], ACT.Exp, bias=negmax[:, i:i + 1],
                                         accum_out=psumexp[:, i:i + 1])
                    drain_inc(ins, S, i)

            def experts(l):
                base = B.jobs[f"moe{l}"]

                def silu(n, it):
                    for ft in range(2):
                        act.wait_ge(filled[ft], it * UNROLL + base[ft] + n + 1)
                        act.wait_ge(drained[2 + ft], it * UNROLL + base[2 + ft] + n)
                        act.activation(sil[:, ft, :], ps[ft][:, 0:T], ACT.Silu).then_inc(drained[ft], 1)

                silu(0, 0)
                with act.Fori(0, (NE - 1) // UNROLL) as it:
                    for u in range(UNROLL):
                        silu(u + 1, it)

            def moe(l):
                norm(l, 1, x_mixed, 2 * NT * (l + 1))
                mod_rows(l, (SH2, SC2))
                modulate(l, 1)
                mod_rows(l, (G2,))
                copy_out(f"router{l}", 0, sml[:, 0, 0:NT * NE], bank_of(f"router{l}")[:, 0:NT * NE], func=ACT.Sigmoid)
                experts(l)

            for i in range(2):
                act.wait_ge(sin_arg, i + 1)
                act.activation(hidden[0:HID, :], hidden[0:HID, :], ACT.Sin).then_inc(sin_done, 1)
            for od in range(2):
                for g in range(2):
                    act.wait_ge(eroot, 2 * od + g + 1)
                    act.activation(esc[:, g, :], esc[:, g, :], ACT.Sqrt).then_inc(escale_ready, 1)
            mod_rows(0, (SH1, SC1))
            norm(0, 0, in_x, 16 * LOADS["in_x"])
            modulate(0, 0)
            act.wait_ge(conv_copied, 1)
            for m in range(3 * NCH):
                bank = filled_wait(act, "uT", m)
                act.activation(uc[:, m, :], bank[:, 0:T], ACT.Identity, bias=convT[:, 3, m:m + 1], scale=convT[:, 1, m:m + 1])
                drain_inc(act.activation(uT[:, m, :], bank[:, 0:T], ACT.Copy), "uT", m)
            for q in range(3):
                for t in range(NT):
                    i = q * NT + t
                    copy_out("qkv", i, qkv[:, t, q * 256:(q + 1) * 256], bank_of("qkv", i)[:, 0:256])
            for t in range(NT):
                copy_out("vtok", t, vtok[:, t, :], bank_of("vtok", t)[:, :])
            for t in range(NT):
                copy_out("x1tok", t, x1tok[:, t, :], bank_of("x1tok", t)[:, :])
            act.wait_ge(qvar, 1)
            act.activation(statA[:, 1, 0:30], statA[:, 0, 0:30], ACT.Sqrt).then_inc(qroot, 1)
            for i in range(NT * KVH):
                t, g = i // KVH, i % KVH
                copy_out("qT", i, qT[:, t, 4 * g:4 * g + 4, :].rearrange("p a b -> p (a b)"), bank_of("qT", i)[0:HD, :])
            for g in range(KVH):
                copy_out("kT", g, kT[:, g, :, :].rearrange("p a b -> p (a b)"), bank_of("kT", g)[0:HD, :])
            attention("g", units_gqa)
            for t in range(NT):
                copy_out("goT", t, hT[:, 4:8, t * P:(t + 1) * P], bank_of("goT", t)[:, :].rearrange("p (a b) -> p a b", b=P))
            mod_rows(0, (G1,))
            moe(0)

            mod_rows(1, (SH1, SC1))
            norm(1, 0, x_done, 1)
            modulate(1, 0)
            for t in range(NT):
                copy_out("um", t, um[:, t, :], bank_of("um", t)[:, 0:ODD_IN])
            act.drain()
            for t in range(NT):
                act.activation(view(14080 + 256 * t, QR), um[:, t, 0:QR], ACT.Square, accum_out=statA[:, 0, t:t + 1])
                ins = act.activation(view(14848 + 128 * t, KVR), um[:, t, QR:QR + KVR], ACT.Square, accum_out=statA[:, 0, NT + t:NT + t + 1])
            ins.then_inc(lora_sq, 1)
            act.wait_ge(lora_var, 1)
            act.activation(statA[:, 1, 0:2 * NT], statA[:, 0, 0:2 * NT], ACT.Sqrt).then_inc(lora_root, 1)
            for t in range(NT + 1):
                if t < NT:
                    copy_out("cT", t, cT[:, :, t * P:(t + 1) * P], bank_of("cT", t)[:, 0:3 * P].rearrange("p (a b) -> p a b", b=P))
                else:
                    copy_out("cT", t, cvT, bank_of("cT", t)[:, 0:P])
            for g in range(NHG):
                for t in range(NT):
                    copy_out(f"mq{g}", t, q4[:, t, :, :].rearrange("p h e -> p (h e)"), bank_of(f"mq{g}", t)[:, 0:HG * QK])
                for t in range(NT + 1):
                    bank = filled_wait(act, f"mkv{g}", t)
                    b4 = bank[:, :].rearrange("p (h e) -> p h e", h=HG)
                    act.activation(v4[:, t, :, :], b4[:, :, NOPE:NOPE + VD], ACT.Copy)
                    drain_inc(act.activation(k4[:, t, :, 0:NOPE], b4[:, :, 0:NOPE], ACT.Copy), f"mkv{g}", t)
                act.wait_ge(qvar, 2 + g)
                act.activation(statA[:, 1, 0:28], statA[:, 0, 0:28], ACT.Sqrt).then_inc(qroot, 1)
                for t in range(NT):
                    copy_out(f"mqT{g}", t, q4T[:, t, :, :].rearrange("p a b -> p (a b)"), bank_of(f"mqT{g}", t)[0:QK, :])
                for s in range(NT + 1):
                    copy_out(f"mkT{g}", s, k4T[:, :, s, :], bank_of(f"mkT{g}", s)[0:QK, :].rearrange("p (a b) -> p a b", b=P))
                attention(str(g), units_mla)
            for i in range(2 * NT):
                t, q = i // 2, i % 2
                copy_out("moT", i, hT[:, 4 * q:4 * q + 4, t * P:(t + 1) * P], bank_of("moT", i)[:, :].rearrange("p (a b) -> p a b", b=P))
            mod_rows(1, (G1,))
            moe(1)

        @block.vector
        def _(dve):
            def settle():
                dve.drain()

            def bank_of(stage, i=0):
                return ps[B[stage, i][0]]

            def mod_columns(l, vectors):
                for v in vectors:
                    for half in range(2):
                        sel = f"modsel{l}.{v}.{half}"
                        bank = filled_wait(dve, sel)
                        rows = slice(64 * half, 64 * half + 64)
                        drain_inc(dve.tensor_copy(modT[rows, l, v, :, :], bank[rows, 0:2 * KT].rearrange("p (a b) -> p a b", b=2)), sel)
                which = 0 if SH1 in vectors else 1
                settle()
                A = modA[:, l, which, :, :]
                dve.tensor_scalar(A, modT[:, l, 3 * which + 1, :, :], 1.0, None, ALU.add)
                settle()
                g = gain[:, l, which, :].unsqueeze(2).broadcast_to([P, KT, 2])
                dve.tensor_tensor(A, A, g, ALU.mult).then_inc(moda_ready, 1)

            def norm(s):
                dve.wait_ge(squares, s + 1)
                dve.tensor_scalar(ssq[:, s, :], ssq[:, s, :], 1.0 / D, EPS, ALU.mult, ALU.add).then_inc(meansq, 1)
                dve.wait_ge(rootsq, s + 1)
                dve.reciprocal(ssq[:, s, :], ssq[:, s, :])
                settle()
                for t in range(NT):
                    dve.tensor_scalar(xn[:, t, :], x[:, t, :], ssq[:, s, t:t + 1], None, ALU.mult).then_inc(xn_ready, 1)

            def modulate(l, which):
                settle()
                sh = 0 if which == 0 else 3
                for i in range(1, 6, 2):
                    t, q = i // 2, i % 2
                    bank = filled_wait(dve, f"hT{l}.{which}", i)
                    for j in range(4):
                        k = 4 * q + j
                        ins = dve.tensor_scalar(hT[:, k, t * P:(t + 1) * P], bank[:, j * P:(j + 1) * P],
                                                modA[:, l, which, k, GRP[t]:GRP[t] + 1],
                                                modT[:, l, sh, k, GRP[t]:GRP[t] + 1], ALU.mult, ALU.add)
                    drain_inc(ins, f"hT{l}.{which}", i)

            def attention(tag, units, heads, o_dst):
                S, PT, O = (f"{tag}S", f"{tag}PT", f"{tag}O") if tag == "g" else (f"mS{tag}", f"mPT{tag}", f"mO{tag}")
                pT = probsT if tag == "g" else mprobsT
                pvs = 0 if tag == "g" else NT * (QH - 1) + int(tag) * NT * (HG - 1)
                n = len(units)
                for i in range(n + 2):
                    if i < n:
                        t, h = units[i]
                        nk = P if t == 0 else T
                        bank = filled_wait(dve, S, i)
                        dve.tensor_reduce(negmax[:, i:i + 1], bank[:, 0:nk], AXX, ALU.max, negate=True).then_inc(negmax_ready, 1)
                    if 1 <= i <= n:
                        j = i - 1
                        t, h = units[j]
                        nk = P if t == 0 else T
                        bank = filled_wait(dve, PT, j)
                        if j >= 2:
                            tj, hj = units[j - 2]
                            if hj == heads - 1:
                                filled_wait(dve, O, tj)
                            else:
                                dve.wait_ge(pv_done, pvs + tj * (heads - 1) + hj + 1)
                        drain_inc(dve.tensor_copy(pT[:, j % 2, :, :].rearrange("p a b -> p (a b)")[:, 0:nk], bank[:, 0:nk]), PT, j)
                    if i >= 2 and units[i - 2][1] == heads - 1:
                        t = units[i - 2][0]
                        dve.reciprocal(rinv[:, 0:heads], psumexp[:, t * heads:(t + 1) * heads])
                        settle()
                        bank = filled_wait(dve, O, t)
                        ins = dve.tensor_tensor(o_dst(t), bank[:, 0:heads * HD].rearrange("p (h e) -> p h e", e=HD),
                                                rinv[:, 0:heads].unsqueeze(2).broadcast_to([P, heads, HD]), ALU.mult)
                        drain_inc(ins, O, t)

            def rope(v, tbl, ra, rb, heads, width):
                c = width // 4
                split = lambda a: a.rearrange("p h (x y z) -> p h x y z", x=2, y=2)
                cos = tbl[:, 0, :].unsqueeze(1).broadcast_to([P, heads, width])
                sin = tbl[:, 1, :].rearrange("p (x y z) -> p x y z", x=2, y=2)
                dve.tensor_tensor(ra, v, cos, ALU.mult)
                for part in range(2):
                    s = sin[:, :, part, :].unsqueeze(1).broadcast_to([P, heads, 2, c])
                    dve.tensor_tensor(split(rb)[:, :, :, part, :], split(v)[:, :, :, 1 - part, :], s, ALU.mult)
                settle()
                return dve.tensor_tensor(v, ra, rb, ALU.add)

            def out_projection(l):
                for half in range(2):
                    cols = slice(half * 512, half * 512 + 512)
                    for t in range(NT):
                        i = half * NT + t
                        if i == 0:
                            for h2 in range(2):
                                for c in range(2):
                                    drained_wait(dve, f"modsel{l}.{G1}.{h2}", c)
                        bank = filled_wait(dve, f"out{l}", i)
                        tmp = tmpa if i % 2 == 0 else tmpb
                        drain_inc(dve.tensor_tensor(tmp, bank[:, :], gb[:, GRP[t], cols], ALU.mult), f"out{l}", i)
                        settle()
                        dve.tensor_tensor(x[:, t, cols], x[:, t, cols], tmp, ALU.add).then_inc(x_mixed, 1)

            def route(l):
                drained_wait(dve, f"router{l}")
                col = lambda i, n: sml[:, i, 0:n]
                by = lambda a, n: a.rearrange("p (a b) -> p a b", b=n)
                wide = lambda a, n, m: a.unsqueeze(2).broadcast_to([P, n, m])
                every = lambda a, n: a.unsqueeze(1).broadcast_to([P, NT, n])
                scores, sel, pairs, t3, t4 = col(0, 48), col(1, 48), col(2, 72), col(3, 48), col(4, 48)
                gmask, hot = col(5, 12), col(6, 48)
                small = col(7, 72)
                dve.tensor_tensor(by(sel, NE), by(scores, NE), every(routb[:, :], NE), ALU.add)
                settle()
                s4, p6 = by(sel, EPG), by(pairs, 6)
                dve.tensor_tensor(p6[:, :, 0:3], s4[:, :, 0:3], s4[:, :, 1:4], ALU.add)
                dve.tensor_tensor(p6[:, :, 3:5], s4[:, :, 0:2], s4[:, :, 2:4], ALU.add)
                dve.tensor_tensor(p6[:, :, 5:6], s4[:, :, 0:1], s4[:, :, 3:4], ALU.add)
                settle()
                dve.tensor_reduce(small[:, 0:12], p6, AXX, ALU.max)
                settle()

                def first_best(out, v, n, rank, best):
                    dve.tensor_reduce(best, by(v, n), AXX, ALU.max)
                    settle()
                    dve.tensor_tensor(by(out, n), by(v, n), wide(best, NT, n), ALU.is_equal)
                    settle()
                    dve.tensor_tensor(by(out, n), by(out, n), every(rank, n), ALU.mult)
                    settle()
                    dve.tensor_reduce(best, by(out, n), AXX, ALU.max)
                    settle()
                    dve.tensor_tensor(by(out, n), by(out, n), wide(best, NT, n), ALU.is_equal)
                    settle()

                first_best(gmask, small[:, 0:12], NG, rank_e[:, NE - NG:], small[:, 12:15])
                dve.tensor_scalar(small[:, 16:28], gmask, 1e30, -1e30, ALU.mult, ALU.add)
                dve.tensor_tensor(by(t3, EPG), by(sel, EPG), wide(gmask, NT * NG, EPG), ALU.mult)
                settle()
                dve.tensor_tensor(by(t3, EPG), by(t3, EPG), wide(small[:, 16:28], NT * NG, EPG), ALU.add)
                settle()
                first_best(hot, t3, NE, rank_e[:, :], small[:, 12:15])
                dve.scalar_tensor_tensor(out=t3, in0=hot, scalar=-2e30, in1=t3, op0=ALU.mult, op1=ALU.add)
                settle()
                first_best(t4, t3, NE, rank_e[:, :], small[:, 12:15])
                dve.tensor_tensor(hot, hot, t4, ALU.add)
                settle()
                dve.tensor_tensor(t3, hot, scores, ALU.mult)
                settle()
                dve.tensor_reduce(small[:, 12:15], by(t3, NE), AXX, ALU.add)
                settle()
                dve.reciprocal(small[:, 12:15], small[:, 12:15])
                settle()
                dve.tensor_tensor(gates[:, :, :], by(t3, NE), wide(small[:, 12:15], NT, NE), ALU.mult)
                settle()

            def experts(l):
                base = B.jobs[f"moe{l}"]

                def gated(n, it):
                    for ft in range(2):
                        b = 2 + ft
                        dve.wait_ge(drained[ft], it * UNROLL + base[ft] + n + 1)
                        dve.wait_ge(filled[b], it * UNROLL + base[b] + n + 1)
                        dve.tensor_tensor(mid[:, n % UNROLL, ft, :], sil[:, ft, :], ps[b][:, 0:T], ALU.mult).then_inc(drained[b], 1)

                def add_up(n, it):
                    settle()
                    for c in range(2 * NT):
                        t, half = c % NT, c // NT
                        b = 4 + c % 3
                        dve.wait_ge(filled[b], it * (2 * UNROLL) + base[b] + 2 * n + c // 3 + 1)
                        dst = acc[:, t, half * 512:half * 512 + 512]
                        dve.scalar_tensor_tensor(out=dst, in0=ps[b][:, :], scalar=gates[:, t, bass.ds(it * UNROLL + n, 1)], in1=dst,
                                                 op0=ALU.mult, op1=ALU.add).then_inc(drained[b], 1)

                gated(0, 0)
                with dve.Fori(0, (NE - 1) // UNROLL) as it:
                    for u in range(UNROLL):
                        gated(u + 1, it)
                        add_up(u, it)
                add_up(NE - 1, 0)
                settle()
                for h2 in range(2):
                    for c in range(2):
                        drained_wait(dve, f"modsel{l}.{G2}.{h2}", c)
                for t in range(NT):
                    dve.tensor_tensor(acc[:, t, :], acc[:, t, :], gb[:, GRP[t], :], ALU.mult)
                settle()
                for t in range(NT):
                    ins = dve.tensor_tensor(x[:, t, :], x[:, t, :], acc[:, t, :], ALU.add)
                ins.then_inc(x_done, 1)

            def moe(l):
                norm(2 * l + 1)
                mod_columns(l, (SH2, SC2))
                modulate(l, 1)
                route(l)
                dve.wait_ge(acc_zero, l + 1)
                experts(l)

            dve.memset(hidden[HID:HID + 1, :], 1.0)
            dve.memset(onesm, 1.0).then_inc(ones_set, 1)
            for e in range(NE):
                dve.memset(rank_e[:, e:e + 1], float(NE - e))
            bank = filled_wait(dve, "convT")
            ins = dve.tensor_copy(convT[:, :, :], bank[:, 0:48].rearrange("p (a b) -> p a b", b=3 * NCH))
            drain_inc(ins, "convT")
            dve.drain().then_inc(conv_copied, 1)

            hid = hidden[0:HID, :]
            loaded(dve, in_filt)
            for i in range(2):
                bank = filled_wait(dve, f"filt{i + 1}")
                drain_inc(dve.tensor_scalar(hid, bank[0:HID, 0:T], filtc[:, i:i + 1], filtc[:, 2:3], ALU.add, ALU.mult), f"filt{i + 1}")
                settle()
                dve.tensor_scalar(turns, hid, 1.0 / (2 * math.pi), ROUNDER, ALU.mult, ALU.add)
                settle()
                dve.tensor_scalar(turns, turns, ROUNDER, None, ALU.subtract)
                for part in (TWO_PI_A, TWO_PI_B, TWO_PI_C):
                    settle()
                    dve.scalar_tensor_tensor(out=hid, in0=turns, scalar=-part, in1=hid, op0=ALU.mult, op1=ALU.add)
                settle()
                dve.tensor_scalar(hid, hid, SIN_MAX, -SIN_MAX, ALU.min, ALU.max).then_inc(sin_arg, 1)

            for od in range(2):
                for t in range(NT):
                    for r in range(2):
                        bank = filled_wait(dve, f"filt3.{od}", 2 * t + r)
                        drain_inc(dve.tensor_tensor(filt[:, t, r, :], bank[:, :], decay[:, t, :], ALU.mult), f"filt3.{od}", 2 * t + r)
                    settle()
                    if t < 2:
                        dve.memset(filt[0:1, t, 1, :], 0.0)
                        settle()
                    dve.tensor_tensor(sqd, filt[:, t, 0, :], filt[:, t, 1, :], ALU.add)
                    dve.tensor_tensor(filt[:, t, 1, :], filt[:, t, 0, :], filt[:, t, 1, :], ALU.subtract)
                    settle()
                    dve.tensor_copy(filt[:, t, 0, :], sqd).then_inc(filt_ready, 1)
                    dve.tensor_tensor(sqs[:, t, :], filt[:, t, 1, :], filt[:, t, 1, :], ALU.mult)
                    dve.tensor_tensor(sqd, sqd, sqd, ALU.mult)
                    settle()
                    dve.tensor_tensor(sqs[:, t, :], sqs[:, t, :], sqd, ALU.add).then_inc(esq_ready, 1)
                for g in range(2):
                    bank = filled_wait(dve, f"energy{od}", g)
                    drain_inc(dve.tensor_scalar(esc[:, g, :], bank[:, :], 0.5, EPS, ALU.mult, ALU.add), f"energy{od}", g)
                    dve.drain().then_inc(eroot, 1)
                for g in range(2):
                    dve.wait_ge(escale_ready, 2 * od + g + 1)
                    dve.reciprocal(esc[:, g, :], esc[:, g, :])
                settle()
                for i in range(2 * NT):
                    ft, r = i // 2, i % 2
                    bank = filled_wait(dve, f"spec{od}", i)
                    ins = dve.tensor_tensor(H[:, od, r, ft, :], bank[:, :], esc[:, GRP[ft], :], ALU.mult)
                    drain_inc(ins, f"spec{od}", i)
                settle()
                for ft in range(NT):
                    dve.tensor_tensor(H[:, od, 0, ft, :], H[:, od, 0, ft, :], hybias[:, od, :], ALU.add)
                dve.drain().then_inc(spec_done, 6)

            loaded(dve, in_mod)
            mod_columns(0, (SH1, SC1))
            norm(0)
            modulate(0, 0)

            for m in range(3 * NCH):
                drained_wait(dve, "uT", m)
                for a, b in ((0, NPR), (NPR, T)):
                    dve.scalar_tensor_tensor(out=uc[:, m, a + 1:b], in0=uT[:, m, a:b - 1], scalar=convT[:, 0, m:m + 1],
                                             in1=uc[:, m, a + 1:b], op0=ALU.mult, op1=ALU.add)
                settle()
                for a, b in ((0, NPR), (NPR, T)):
                    ins = dve.scalar_tensor_tensor(out=uc[:, m, a:b - 1], in0=uT[:, m, a + 1:b], scalar=convT[:, 2, m:m + 1],
                                                   in1=uc[:, m, a:b - 1], op0=ALU.mult, op1=ALU.add)
                ins.then_inc(conv_done, 1)

            for od in range(2):
                for ft in range(NT):
                    Hr, Hi = H[:, od, 0, ft, :], H[:, od, 1, ft, :]
                    settle()
                    bank = filled_wait(dve, f"fwd{od}", 2 * ft)
                    dve.tensor_tensor(Y[:, ft, 0, :], bank[:, :], Hr, ALU.mult)
                    drain_inc(dve.tensor_tensor(Y[:, ft, 1, :], bank[:, :], Hi, ALU.mult), f"fwd{od}", 2 * ft)
                    bank = filled_wait(dve, f"fwd{od}", 2 * ft + 1)
                    dve.tensor_tensor(tmpa, bank[:, :], Hi, ALU.mult)
                    drain_inc(dve.tensor_tensor(tmpb, bank[:, :], Hr, ALU.mult), f"fwd{od}", 2 * ft + 1)
                    settle()
                    dve.tensor_tensor(Y[:, ft, 0, :], Y[:, ft, 0, :], tmpa, ALU.subtract)
                    dve.tensor_tensor(Y[:, ft, 1, :], Y[:, ft, 1, :], tmpb, ALU.add).then_inc(y_ready, 1)
                if od == 0:
                    for t in range(NT):
                        drained_wait(dve, "x1tok", t)
                        bank = filled_wait(dve, "inv0", t)
                        drain_inc(dve.tensor_tensor(vtok[:, t, :], bank[:, :], x1tok[:, t, :], ALU.mult), "inv0", t)
                else:
                    for c in range(NCH):
                        bank = filled_wait(dve, "inv1", c)
                        drain_inc(dve.tensor_tensor(hT[:, c, :], bank[:, 0:T], uc[:, 2 * NCH + c, :], ALU.mult), "inv1", c)

            loaded(dve, in_attn)
            dve.tensor_scalar(qkgain[:, 0, :], qkgain[:, 0, :], HD ** -0.5, None, ALU.mult)
            QKH = QH + KVH
            for t in range(NT):
                for q in range(3):
                    drained_wait(dve, "qkv", q * NT + t)
                v = qkv[:, t, 0:QKH * HD].rearrange("p (h e) -> p h e", e=HD)
                dve.tensor_tensor(qsq, v, v, ALU.mult)
                settle()
                dve.tensor_reduce(statA[:, 0, QKH * t:QKH * (t + 1)], qsq, AXX, ALU.add)
                settle()
            dve.tensor_scalar(statA[:, 0, 0:30], statA[:, 0, 0:30], 1.0 / HD, EPS, ALU.mult, ALU.add).then_inc(qvar, 1)
            dve.wait_ge(qroot, 1)
            dve.reciprocal(statA[:, 1, 0:30], statA[:, 1, 0:30])
            settle()
            for t in range(NT):
                v = qkv[:, t, 0:QKH * HD].rearrange("p (h e) -> p h e", e=HD)
                dve.tensor_tensor(v, v, statA[:, 1, QKH * t:QKH * (t + 1)].unsqueeze(2).broadcast_to([P, QKH, HD]), ALU.mult)
                settle()
                dve.tensor_tensor(v[:, 0:QH, :], v[:, 0:QH, :], qkgain[:, 0, :].unsqueeze(1).broadcast_to([P, QH, HD]), ALU.mult)
                ins = dve.tensor_tensor(v[:, QH:QKH, :], v[:, QH:QKH, :], qkgain[:, 1, :].unsqueeze(1).broadcast_to([P, KVH, HD]), ALU.mult)
                if t:
                    settle()
                    ins = rope(v, ropeq[:, t - 1, :, :], qsq, qrb, QKH, HD)
                ins.then_inc(qk_ready, 1)
            attention("g", units_gqa, QH, lambda t: otok[:, t, :].rearrange("p (h e) -> p h e", e=HD))
            out_projection(0)
            moe(0)

            mod_columns(1, (SH1, SC1))
            norm(2)
            modulate(1, 0)
            loaded(dve, in_mla)
            dve.wait_ge(lora_sq, 1)
            dve.tensor_scalar(statA[:, 0, 0:NT], statA[:, 0, 0:NT], 1.0 / QR, EPS, ALU.mult, ALU.add)
            dve.tensor_scalar(statA[:, 0, NT:2 * NT], statA[:, 0, NT:2 * NT], 1.0 / KVR, EPS, ALU.mult, ALU.add).then_inc(lora_var, 1)
            dve.tensor_scalar(mgain[:, 0, :], mgain[:, 0, :], QK ** -0.5, None, ALU.mult)
            dve.wait_ge(lora_root, 1)
            dve.reciprocal(statA[:, 1, 0:2 * NT], statA[:, 1, 0:2 * NT])
            settle()
            for t in range(NT):
                for c0, c1, i in ((0, QR, t), (QR, QR + KVR, NT + t)):
                    ins = dve.scalar_tensor_tensor(out=um[:, t, c0:c1], in0=um[:, t, c0:c1], scalar=statA[:, 1, i:i + 1],
                                                   in1=lgain[:, c0:c1], op0=ALU.mult, op1=ALU.mult)
                ins.then_inc(lora_ready, 1)
            for g in range(NHG):
                nq, nkk = NT * HG, (NT + 1) * HG
                flat = lambda a: a.rearrange("p t h e -> p (t h) e")
                if g:
                    for s_ in range(NT + 1):
                        filled_wait(dve, f"mkT{g - 1}", s_)
                for t in range(NT + 1):
                    kr = kr_c if t == NT else um[:, t, QR + KVR:ODD_IN]
                    dve.tensor_copy(k4[:, t, :, NOPE:QK], kr.unsqueeze(1).broadcast_to([P, HG, ROPE]))
                for t in range(NT):
                    drained_wait(dve, f"mq{g}", t)
                dve.tensor_tensor(flat(msq)[:, 0:nq, :], flat(q4), flat(q4), ALU.mult)
                settle()
                dve.tensor_reduce(statA[:, 0, 0:nq], flat(msq)[:, 0:nq, :], AXX, ALU.add)
                settle()
                for t in range(NT + 1):
                    drained_wait(dve, f"mkv{g}", t)
                dve.tensor_tensor(flat(msq), flat(k4), flat(k4), ALU.mult)
                settle()
                dve.tensor_reduce(statA[:, 0, nq:nq + nkk], flat(msq), AXX, ALU.add)
                settle()
                dve.tensor_scalar(statA[:, 0, 0:28], statA[:, 0, 0:28], 1.0 / QK, EPS, ALU.mult, ALU.add).then_inc(qvar, 1)
                dve.wait_ge(qroot, 2 + g)
                dve.reciprocal(statA[:, 1, 0:28], statA[:, 1, 0:28])
                settle()
                for v, a, m, which in ((q4, 0, nq, 0), (k4, nq, nkk, 1)):
                    dve.tensor_tensor(flat(v), flat(v), statA[:, 1, a:a + m].unsqueeze(2).broadcast_to([P, m, QK]), ALU.mult)
                    settle()
                    dve.tensor_tensor(flat(v), flat(v), mgain[:, which, :].unsqueeze(1).broadcast_to([P, m, QK]), ALU.mult)
                    settle()
                    for t in range(1, NT):
                        rope(v[:, t, :, NOPE:QK], ropem[:, t - 1, :, :], mrb[:, 0, :, :], mrb[:, 1, :, :], HG, ROPE)
                        settle()
                    dve.drain().then_inc(qk_ready, 1)
                attention(str(g), units_mla, HG,
                          lambda t, g=g: mtok[:, t, g * HG * VD:(g + 1) * HG * VD].rearrange("p (h e) -> p h e", e=VD))
            out_projection(1)
            moe(1)


_OUTS = [(1, NPR, D), (1, NSA, D), (1, 1, NPR, KVH, HD), (1, 1, NPR, KVH, HD), (1, 1, NPR, KVR), (1, 1, NPR, ROPE)]


def kernel(**inputs):
    import concourse.bacc as _bacc
    from concourse.bass_utils import run_bass_kernel_spmd as _run

    nc = _bacc.Bacc("TRN2", target_bir_lowering=False, num_devices=1)
    arrays, dram = {}, {}
    for name, a in list(inputs.items()) + list(shape_constants().items()):
        a = np.ascontiguousarray(a)
        arrays[f"in_{name}_dram"] = a
        dram[name] = nc.dram_tensor(f"in_{name}_dram", a.shape, mybir.dt.from_np(a.dtype), kind="ExternalInput").ap()
    outs = [nc.dram_tensor(f"out_{i}_dram", shape, F32, kind="ExternalOutput").ap() for i, shape in enumerate(_OUTS)]
    build_step(nc, dram, outs)
    r = _run(nc, [arrays], core_ids=[0])
    return tuple(r.results[0][f"out_{i}_dram"] for i in range(len(_OUTS)))
```

```python
import math
from contextlib import ExitStack

import numpy as np

import concourse.bass as bass
from concourse import mybir

F32 = mybir.dt.float32
ALU = mybir.AluOpType
ACT = mybir.ActivationFunctionType
AXX = mybir.AxisListType.X

P = 128
D = 1024
KT = D // P
NPR, NSA, PAST = 128, 256, 128
T = NPR + NSA
NT = T // P
GRP = [0, 1, 1]
EPS = 1e-6
HY = D // 2
NCH = HY // P
HID, EMB = 64, 33
QH, KVH, HD = 8, 2, 64
MH, NOPE, ROPE, VD = 16, 64, 32, 64
QK = NOPE + ROPE
QR, KVR = 256, 128
ODD_IN = QR + KVR + ROPE
HG = 4
NE, DE, NG, EPG = 16, 256, 4, 4
GRID_W = 64
RING = 9
PIECE = 2048
NBLK = (T + NG * (P - 1)) // P

TWO_PI_A = 6.28125
TWO_PI_B = float(np.float32(np.round((2 * math.pi - TWO_PI_A) * 2**20) / 2**20))
TWO_PI_C = float(2 * math.pi - TWO_PI_A - TWO_PI_B)
ROUNDER = 1.5 * 2.0**23
SIN_MAX = 3.1415925

SH1, SC1, G1, SH2, SC2, G2 = range(6)


def shape_constants():
    c = {}
    c["ident"] = np.eye(P)
    c["before"] = np.triu(np.ones((P, P)), 1)
    c["slots"] = np.tile(np.arange(P), (P, 1))
    sel = np.zeros((P, 2, P))
    for g in range(4):
        for r in range(2):
            sel[32 * g + r, r, :] = 1
    c["rowsel"] = sel.reshape(P, 2 * P)
    cs = np.zeros((24, 24, 2))
    for r in range(24):
        cs[r, r, :] = 1
    c["chunksel"] = cs.reshape(24, 48)

    def odd_dft(n):
        j = np.arange(n)[:, None]
        f = np.arange(n)[None, :]
        a = np.pi * ((2 * f + 1) * j % (4 * n)) / (2 * n)
        return np.cos(a), np.sin(a)

    cp, sp = odd_dft(NPR)
    cs_, ss = odd_dft(NSA)
    c["dft_p"] = np.stack([cp, sp, cp.T / NPR, sp.T / NPR], 1).reshape(P, 4 * NPR)
    two = [m.reshape(2, P, NSA).transpose(1, 0, 2) for m in (cs_, ss, cs_.T / NSA, ss.T / NSA)]
    c["dft_s"] = np.stack(two, 1).reshape(P, 8 * NSA)

    zs, ds = [], []
    lo, hi = math.log(1e-2) / 1.5, math.log(1e-2) / 0.3
    deltas = np.abs(np.linspace(lo, hi, HY))
    for n in (NPR, NSA):
        t01 = np.linspace(0.0, 1.0, n)
        w = (2 * math.pi / n) * np.arange(n)
        bands = np.linspace(1e-4, (EMB - 1) // 2 - 1, (EMB - 1) // 2)
        zs.append(np.concatenate([t01[:, None], np.cos(w[:, None] * bands), -np.sin(w[:, None] * bands)], 1))
        ds.append(np.exp(-t01[:, None] * deltas))
    c["zT"] = np.concatenate(zs, 0).T
    c["decay"] = np.concatenate(ds, 0).reshape(NT, P, HY).transpose(1, 0, 2).reshape(P, NT * HY)

    def rope(width):
        half, npair = width // 2, width // 4
        fr = 10000.0 ** (-np.arange(npair) / npair)
        t = np.arange(NSA)
        co, si = [], []
        for pos in (t // GRID_W, t % GRID_W):
            a = pos[:, None] * fr[None, :]
            co += [np.cos(a), np.cos(a)]
            si += [-np.sin(a), np.sin(a)]
        both = np.stack([np.concatenate(co, 1), np.concatenate(si, 1)], 1)
        return both.reshape(2, P, 2, width).transpose(1, 0, 2, 3).reshape(P, 4 * width)

    c["rope_q"] = rope(HD)
    c["rope_m"] = rope(ROPE)
    return {k: np.ascontiguousarray(v, np.float32) for k, v in c.items()}


class Banks:

    def __init__(self):
        self.uses = [0] * 8
        self.turn = 0
        self.jobs = {}

    def stage(self, name, count, banks=None):
        out = []
        for i in range(count):
            if banks is None:
                b = self.turn
                self.turn = (self.turn + 1) % 8
            else:
                b = banks[i % len(banks)]
            out.append((b, self.uses[b]))
            self.uses[b] += 1
        self.jobs[name] = out

    def __getitem__(self, key):
        return self.jobs[key[0]][key[1]]


def build_step(nc, d, o):
    y_prompt, y_sample, st_k, st_v, st_ckv, st_kr = o
    units_gqa = [(t, h) for t in range(NT) for h in range(QH)]
    units_mla = [(t, h) for t in range(NT) for h in range(HG)]
    NHG = MH // HG

    B = Banks()
    BANK_S, BANK_PT, BANK_O = [0, 1, 2], [3, 4, 5], [6, 7]

    def mod_stage(l, vectors):
        for v in vectors:
            for half in range(2):
                B.stage(f"mod{l}.{v}.{half}", 1)
                B.stage(f"modsel{l}.{v}.{half}", 2 if v in (G1, G2) else 1)

    def moe_stage(l):
        mod_stage(l, (SH2, SC2))
        B.stage(f"hT{l}.1", 6)
        B.stage(f"router{l}", 1)
        B.stage(f"htok{l}", 6)
        mod_stage(l, (G2,))
        B.stage(f"rank{l}", 1)
        if l == 0:
            mod_stage(1, (SH1, SC1))
        B.jobs[f"moe{l}"] = list(B.uses)

    B.stage("convT", 1)
    B.stage("filt1", 1)
    B.stage("filt2", 1)
    for od in range(2):
        B.stage(f"filt3.{od}", 2 * NT)
        B.stage(f"energy{od}", 2)
        B.stage(f"spec{od}", 2 * NT)
    mod_stage(0, (SH1, SC1))
    B.stage("hT0.0", 6)
    B.stage("uT", 3 * NCH)
    B.stage("qkv", 3 * NT)
    B.stage("vtok", NT)
    B.stage("x1tok", NT)
    B.stage("fwd0", 2 * NT)
    B.stage("inv0", NT)
    B.stage("fwd1", 2 * NT)
    B.stage("inv1", NCH)
    B.stage("qT", NT * KVH)
    B.stage("kT", KVH)
    B.stage("gS", len(units_gqa), BANK_S)
    B.stage("gPT", len(units_gqa), BANK_PT)
    B.stage("gO", NT, BANK_O)
    B.stage("goT", NT)
    mod_stage(0, (G1,))
    B.stage("out0", 2 * NT)
    moe_stage(0)
    B.stage("hT1.0", 6)
    B.stage("um", NT)
    B.stage("cT", NT + 1)
    for g in range(NHG):
        B.stage(f"mq{g}", NT)
        B.stage(f"mkv{g}", NT + 1)
        B.stage(f"mqT{g}", NT)
        B.stage(f"mkT{g}", NT + 1)
        B.stage(f"mS{g}", len(units_mla), BANK_S)
        B.stage(f"mPT{g}", len(units_mla), BANK_PT)
        B.stage(f"mO{g}", NT, BANK_O)
    B.stage("moT", 2 * NT)
    mod_stage(1, (G1,))
    B.stage("out1", 2 * NT)
    moe_stage(1)

    pieces, at = [], {}

    def piece(name, src, *shape):
        at[name] = len([q for q in pieces if q is not None])
        pieces.append((src, shape))

    def mod_pieces(l, vectors):
        for v in vectors:
            for half in range(2):
                c0 = v * D + half * 512
                for kh in range(2):
                    w = d["w_mod"][l].rearrange("(p j) n -> p j n", j=KT)
                    piece(f"mod{l}.{v}.{half}.{kh}", w[:, 4 * kh:4 * kh + 4, c0:c0 + 512], 4, 512)

    def out_pieces(l, w):
        w = w.rearrange("(j p) n -> p j n", p=P)
        for half in range(2):
            for kh in range(2):
                piece(f"out{l}.{half}.{kh}", w[:, 4 * kh:4 * kh + 4, half * 512:half * 512 + 512], 4, 512)

    def moe_pieces(l):
        mod_pieces(l, (SH2, SC2))
        mod_pieces(l, (G2,))
        if l == 0:
            mod_pieces(1, (SH1, SC1))
        pieces.append(None)
        at[f"moe{l}"] = len([q for q in pieces if q is not None])

    mod_pieces(0, (SH1, SC1))
    ev_in = d["ev_w_in"][0].rearrange("(p j) n -> p j n", j=KT)
    for q in range(9):
        piece(f"in0.{q}", ev_in[:, :, 256 * q:256 * q + 256], KT, 256)
    mod_pieces(0, (G1,))
    out_pieces(0, d["ev_w_out"][0])
    moe_pieces(0)
    od_in = d["od_w_in"][0].rearrange("(p j) n -> p j n", j=KT)
    for kh in range(2):
        piece(f"in1.{kh}", od_in[:, 4 * kh:4 * kh + 4, :], 4, ODD_IN)
    w_uq = d["od_w_uq"][0].rearrange("(j p) n -> p j n", p=P)
    for j in range(2):
        piece(f"uq{j}", w_uq[:, j:j + 1, :], 1, MH * QK)
    piece("ukv", d["od_w_ukv"][0].rearrange("(j p) n -> p j n", j=1), 1, MH * (NOPE + VD))
    mod_pieces(1, (G1,))
    out_pieces(1, d["od_w_out"][0])
    moe_pieces(1)

    with ExitStack() as ctx:
        def sb(name, *shape):
            return ctx.enter_context(nc.sbuf_tensor(name, list(shape), F32))

        def sem(name):
            return ctx.enter_context(nc.semaphore(name))

        ring = sb("ring", P, RING * PIECE)
        x = sb("x", P, NT, D)
        hT = sb("hT", P, KT, T)
        xn = sb("xn", P, NT, D)
        gb = sb("gb", P, 2, D)
        modrow = sb("modrow", P, 512)
        ident = sb("ident", P, P)
        rowsel = sb("rowsel", P, 2, P)
        chunksel = sb("chunksel", 24, 24, 2)
        bmod = sb("bmod", 24, 512)
        condraw = sb("condraw", P, 2, KT)
        condT = sb("condT", P, KT, 32)
        modT = sb("modT", P, 2, 6, KT, 2)
        modA = sb("modA", P, 2, 2, KT, 2)
        gain = sb("gain", P, 2, 2, KT)
        routw = sb("routw", P, KT, NE)
        routb = sb("routb", P, NE)
        rank_e = sb("rank_e", P, NE)
        ssq = sb("ssq", P, 4, NT)
        gates = sb("gates", P, NT, NE)
        meta = ctx.enter_context(nc.sbuf_tensor("meta", [1, 2, 8], mybir.dt.int32))
        statA = sb("statA", P, 2, 40)
        negmax = sb("negmax", P, len(units_gqa))
        psumexp = sb("psumexp", P, len(units_gqa))
        rinv = sb("rinv", P, QH)
        ropeq = sb("ropeq", P, 2, 2, HD)
        qkgain = sb("qkgain", P, 2, HD)
        ck = sb("ck", P, KVH * HD)
        cv = sb("cv", P, KVH * HD)
        filtc = sb("filtc", HID, 3 + 2 * HID)
        convT = sb("convT", P, 4, 3 * NCH)

        arena = sb("arena", P, 20224)

        def view(off, *shape, parts=P):
            n = int(np.prod(shape))
            v = arena[0:parts, off:off + n]
            if len(shape) == 2:
                return v.rearrange("p (a b) -> p a b", b=shape[1])
            if len(shape) == 3:
                return v.rearrange("p (a b c) -> p a b c", b=shape[1], c=shape[2])
            if len(shape) == 4:
                return v.rearrange("p (a b c e) -> p a b c e", b=shape[1], c=shape[2], e=shape[3])
            return v

        H = view(0, 2, 2, NT, HY)
        uc = view(6144, 3 * NCH, T)
        dftp = view(10752, 4, NPR)
        dfts = view(11264, 4, 2, NSA)
        uT = view(13312, 3 * NCH, T)
        qkv = view(17920, NT, QH * HD + 2 * KVH * HD)
        filt = view(6144, NT, 2, HY)
        decay = view(9216, NT, HY)
        w3 = view(13312, 4, HY, parts=HID + 1)
        convraw = view(15360, P, parts=48)
        esc = view(15488, 2, HY)
        hidden = view(16512, T, parts=HID + 1)
        turns = view(16896, T, parts=HID)
        zT = view(17280, T, parts=EMB)
        sqs = view(17664, NT, HY)
        sqd = view(19200, HY)
        onesm = view(19712, P)
        Y = view(13312, NT, 2, HY)
        tmpa = view(16384, HY)
        tmpb = view(16896, HY)
        hybias = gb[:, :, 0:HY]
        vtok = xn[:, :, 0:HY]
        x1tok = xn[:, :, HY:D]
        qT = view(0, NT, QH, P, parts=HD)
        kT = view(3072, KVH, 4, P, parts=HD)
        probs = view(4096, 2, T)
        probsT = view(4864, 2, 3, P)
        scratch = gb[:, :, :].rearrange("p a b -> p (a b)")
        qsq = scratch[:, 0:(QH + KVH) * HD].rearrange("p (h e) -> p h e", e=HD)
        qrb = scratch[:, 640:640 + (QH + KVH) * HD].rearrange("p (h e) -> p h e", e=HD)
        otok = xn[:, :, 0:HY]
        um = view(0, NT, ODD_IN)
        cT = view(1248, 3, T)
        cvT = view(2400, P)
        ckv_c = view(14100, KVR)
        kr_c = view(14228, ROPE)
        lgain = view(14260, QR + KVR)
        mgain = view(14644, 2, QK)
        ropem = view(14836, 2, 2, ROPE)
        q4 = view(3392, NT, HG, QK)
        k4 = view(4544, NT + 1, HG, QK)
        v4 = view(6080, NT + 1, HG, VD)
        q4T = view(7104, NT, HG, P, parts=QK)
        k4T = view(8640, HG, NT + 1, P, parts=QK)
        mprobs = view(10688, 2, T)
        mprobsT = view(11456, 2, 3, P)
        msq = view(12224, NT + 1, HG, QK)
        mrb = view(13760, 2, HG, ROPE)
        mtok = xn
        ysb = view(6144, D)
        hTs = view(7168, KT, P)
        before = view(8192, P)
        slots = view(8320, P)
        onesr = view(8448, P)
        sml = view(8576, 8, 72)
        plan = view(9152, 128)
        sil = view(9280, 2, DE)
        mid = view(9792, 2, DE)
        midT = view(10304, 2, 2, P)
        perm = view(10816, NT, P)
        permT = view(11200, NT, P)
        gtmp = view(15104, 2 * NT, 512)
        htok = xn
        junk = view(12000, 2 * NT, QR)

        ps = [ctx.enter_context(nc.psum_tensor(f"ps{b}", [P, 512], F32)) for b in range(8)]
        filled = [sem(f"filled{b}") for b in range(8)]
        drained = [sem(f"drained{b}") for b in range(8)]
        piece_full = [sem(f"piece_full{s}") for s in range(RING)]
        piece_used = sem("piece_used")
        in_cond, in_x, in_mod, in_filt, in_dft, in_conv, in_attn, in_mla = (
            sem(n) for n in ("in_cond", "in_x", "in_mod", "in_filt", "in_dft", "in_conv", "in_attn", "in_mla"))
        cond_zero, cond_ready = sem("cond_zero"), sem("cond_ready")
        ones_set = sem("ones_set")
        modrow_used = sem("modrow_used")
        moda_ready = sem("moda_ready")
        squares = sem("squares")
        meansq = sem("meansq")
        rootsq = sem("rootsq")
        xn_ready = sem("xn_ready")
        sin_arg, sin_done = sem("sin_arg"), sem("sin_done")
        filt_ready, esq_ready, eroot, escale_ready = sem("filt_ready"), sem("esq_ready"), sem("eroot"), sem("escale_ready")
        spec_done = sem("spec_done")
        conv_copied, conv_done = sem("conv_copied"), sem("conv_done")
        y_ready = sem("y_ready")
        qsq_ready, qvar, qroot, qk_ready = sem("qsq_ready"), sem("qvar"), sem("qroot"), sem("qk_ready")
        negmax_ready = sem("negmax_ready")
        pv_done = sem("pv_done")
        x_mixed = sem("x_mixed")
        x_done = sem("x_done")
        score_ready = sem("score_ready")
        gates_ready = sem("gates_ready")
        in_route = sem("in_route")
        per_layer = lambda name: [sem(f"{name}{l}") for l in range(2)]
        plan_sums, plan_ready, perm_ready = per_layer("plan_sums"), per_layer("plan_ready"), per_layer("perm_ready")
        gather_full, hts_ready, aux_read = per_layer("gather_full"), per_layer("hts_ready"), per_layer("aux_read")
        gu_full, silu_ready, mid_ready = per_layer("gu_full"), per_layer("silu_ready"), per_layer("mid_ready")
        mt_full, mt_read, y_full, y_read = per_layer("mt_full"), per_layer("mt_read"), per_layer("y_full"), per_layer("y_read")
        scatter_full, scatter_read = per_layer("scatter_full"), per_layer("scatter_read")
        expert_used = per_layer("expert_used")
        gu_loaded = [[sem(f"gu_loaded{l}{j}") for j in range(EPG)] for l in range(2)]
        down_loaded = [[sem(f"down_loaded{l}{j}") for j in range(EPG)] for l in range(2)]
        lora_sq, lora_var, lora_root, lora_ready = sem("lora_sq"), sem("lora_var"), sem("lora_root"), sem("lora_ready")
        stored = sem("stored")

        def place(j):
            w = ring[:, 3 * j * PIECE:3 * (j + 1) * PIECE] if j < 3 else arena[:, 0:3 * PIECE]
            gu = w[:, 0:2 * PIECE].rearrange("p (w k n) -> p w k n", w=2, n=DE)
            return gu, w[:, 2 * PIECE:3 * PIECE].rearrange("p (k n) -> p k n", n=D)

        def blocks_of(eng, l):
            eng.wait_ge(plan_ready[l], 1)
            return eng.value_load(meta[0:1, l, 0:1], min_val=1, max_val=NBLK)

        def ring_view(i, shape):
            s = (i % RING) * PIECE
            n = shape[0] * shape[1]
            return ring[:, s:s + n].rearrange("p (a b) -> p a b", b=shape[1])

        def filled_wait(eng, stage, i=0):
            b, n = B[stage, i]
            eng.wait_ge(filled[b], n + 1)
            return ps[b]

        def drained_wait(eng, stage, i=0):
            b, n = B[stage, i]
            eng.wait_ge(drained[b], n + 1)

        def drain_inc(ins, stage, i=0):
            ins.then_inc(drained[B[stage, i][0]], 1)

        consts_loaded = {}

        def load(eng, s, dst, src):
            eng.dma_start(dst, src).then_inc(s, 16)
            consts_loaded[s.name] = consts_loaded.get(s.name, 0) + 16

        LOADS = {"in_cond": 2, "in_x": 2, "in_mod": 9, "in_filt": 11, "in_dft": 2, "in_conv": 2, "in_attn": 6, "in_mla": 7}

        def loaded(eng, s):
            eng.wait_ge(s, 16 * LOADS[s.name])

        block = ctx.enter_context(nc.Block())

        @block.sync
        def _(sp):
            def send(i, src, shape, wait):
                if wait is not None:
                    sp.wait_ge(piece_used, wait)
                sp.dma_start(ring_view(i, shape), src).then_inc(piece_full[i % RING], 16)

            def send_experts(l):
                nb = blocks_of(sp, l)
                with sp.Fori(0, nb) as b:
                    g = sp.value_load(meta[0:1, l, bass.ds(b + 1, 1)], min_val=0, max_val=NG - 1)
                    for j in range(EPG):
                        gu, dn = place(j)
                        e = g * EPG + j
                        sp.wait_ge(expert_used[l], b * EPG + (j + 1))
                        for w, name in enumerate(("moe_w_gate", "moe_w_up")):
                            src = d[name][l][bass.ds(e, 1), :, :].rearrange("e (p j) n -> p (e j) n", j=KT)
                            sp.dma_start(gu[:, w, :, :], src).then_inc(gu_loaded[l][j], 16)
                        src = d["moe_w_down"][l][bass.ds(e, 1), :, :].rearrange("e (j p) n -> p (e j) n", p=P)
                        sp.dma_start(dn, src).then_inc(down_loaded[l][j], 16)
                return nb

            i, l, nb = 0, 0, None
            for entry in pieces:
                if entry is None:
                    nb = send_experts(l)
                    l += 1
                    continue
                if l == 1 and i - at["moe0"] < RING:
                    sp.wait_ge(expert_used[0], nb * EPG + ((i % RING) // 3 + 1))
                    send(i, *entry, None)
                else:
                    send(i, *entry, i - RING + 1 if i >= RING else None)
                i += 1

        @block.gpsimd
        def _(pool):
            pool.memset(condT[:, :, :], 0.0).then_inc(cond_zero, 1)
            load(pool, in_dft, dftp, d["dft_p"].rearrange("p (a b) -> p a b", b=NPR))
            load(pool, in_dft, dfts, d["dft_s"].rearrange("p (a b c) -> p a b c", b=2, c=NSA))
            load(pool, in_attn, ropeq[:, :, :, :], d["rope_q"].rearrange("p (a b c) -> p a b c", b=2, c=HD))
            load(pool, in_attn, qkgain[:, 0, :], d["ev_q_norm"][0].partition_broadcast(P))
            load(pool, in_attn, qkgain[:, 1, :], d["ev_k_norm"][0].partition_broadcast(P))
            load(pool, in_attn, ck[:, :], d["cache_gqa_k"][0, 0].rearrange("t h e -> t (h e)"))
            load(pool, in_attn, cv[:, :], d["cache_gqa_v"][0, 0].rearrange("t h e -> t (h e)"))
            load(pool, in_attn, routb[:, :], d["router_bias"].partition_broadcast(P))
            pool.wait_ge(qk_ready, 1)
            pool.dma_start(st_k[0, 0].rearrange("t h e -> t (h e)"), qkv[:, 0, QH * HD:QH * HD + KVH * HD]).then_inc(stored, 16)
            pool.dma_start(st_v[0, 0].rearrange("t h e -> t (h e)"), qkv[:, 0, QH * HD + KVH * HD:]).then_inc(stored, 16)
            for l in range(2):
                for i in range(6):
                    drained_wait(pool, f"hT{l}.1", i)
                load(pool, in_route, before, d["before"])
                load(pool, in_route, slots, d["slots"])
                if l == 1:
                    break
                load(pool, in_mla, ckv_c, d["cache_mla_ckv"][0, 0])
                load(pool, in_mla, kr_c, d["cache_mla_krope"][0, 0])
                load(pool, in_mla, lgain[:, 0:QR], d["od_q_lora_norm"][0].partition_broadcast(P))
                load(pool, in_mla, lgain[:, QR:QR + KVR], d["od_kv_lora_norm"][0].partition_broadcast(P))
                load(pool, in_mla, mgain[:, 0, :], d["od_q_norm"][0].partition_broadcast(P))
                load(pool, in_mla, mgain[:, 1, :], d["od_k_norm"][0].partition_broadcast(P))
                load(pool, in_mla, ropem, d["rope_m"].rearrange("p (a b c) -> p a b c", b=2, c=ROPE))
                pool.wait_ge(lora_ready, 1)
                pool.dma_start(st_ckv[0, 0], um[:, 0, QR:QR + KVR]).then_inc(stored, 16)
                pool.dma_start(st_kr[0, 0], um[:, 0, QR + KVR:]).then_inc(stored, 16)
            pool.wait_ge(x_done, 2)
            pool.dma_start(y_prompt[0], x[:, 0, :]).then_inc(stored, 16)
            pool.dma_start(y_sample[0].rearrange("(t p) n -> p t n", p=P), x[:, 1:NT, :]).then_inc(stored, 16)
            pool.wait_ge(stored, 16 * 6)

        @block.tensor
        def _(pe):
            def claim(stage, i=0):
                b, n = B[stage, i]
                if n:
                    pe.wait_ge(drained[b], n)
                return ps[b]

            def fill_inc(ins, stage, i=0):
                ins.then_inc(filled[B[stage, i][0]], 1)

            def weights(name, shape):
                i = at[name]
                pe.wait_ge(piece_full[i % RING], 16 * (i // RING + 1))
                return ring_view(i, shape)

            due = [0, piece_used]

            def piece_end(count=1):
                due[0] += count

            def product(out, lhsT, rhs, **kw):
                mm = pe.matmul(out, lhsT, rhs, **kw)
                if due[0]:
                    mm.then_inc(due[1], due[0])
                    due[:] = [0, piece_used]
                return mm

            def turn(out, src):
                mm = pe.transpose(out, src, ident[:, :])
                if due[0]:
                    mm.then_inc(due[1], due[0])
                    due[:] = [0, piece_used]
                return mm

            def mod_vectors(l, vectors):
                for v in vectors:
                    for half in range(2):
                        name = f"mod{l}.{v}.{half}"
                        bank = claim(name)
                        if l == 0 and v == SH1 and half == 0:
                            loaded(pe, in_mod)
                            pe.wait_ge(cond_ready, 2)
                        for kh in range(2):
                            w = weights(f"{name}.{kh}", (4, 512))
                            for g in range(4):
                                mm = product(bank[32 * g:32 * g + 32, :], condT[:, 4 * kh + g, :], w[:, g, :],
                                             start=kh == 0, stop=kh == 1)
                            if kh == 0:
                                mm.then_inc(piece_used, 1)
                                product(bank[0:2, :], chunksel[:, l * 12 + 2 * v + half, :], bmod[:, :], start=False, stop=False)
                        fill_inc(mm, name)
                        piece_end()
                        drained_wait(pe, name)
                        sel = f"modsel{l}.{v}.{half}"
                        if v in (G1, G2):
                            for c in range(2):
                                bank = claim(sel, c)
                                for n0 in (0, 256):
                                    mm = product(bank[:, n0:n0 + 256], rowsel[:, c, :], modrow[:, n0:n0 + 256], start=True, stop=True)
                                fill_inc(mm, sel, c)
                        else:
                            bank = claim(sel)
                            for j in range(KT):
                                mm = product(bank[64 * half:64 * half + 64, 2 * j:2 * j + 2],
                                               modrow[:, j::KT], rowsel[:, :, 0], start=True, stop=True)
                            fill_inc(mm, sel)

            def norm_transposes(l, which):
                stage = f"hT{l}.{which}"
                for t in range(NT):
                    pe.wait_ge(xn_ready, (2 * l + which) * NT + t + 1)
                    for q in range(2):
                        bank = claim(stage, 2 * t + q)
                        for j in range(4):
                            mm = turn(bank[:, j * P:(j + 1) * P], xn[:, t, 4 * q + j::KT])
                        fill_inc(mm, stage, 2 * t + q)

            def out_projection(l):
                for half in range(2):
                    for i in range(NT):
                        claim(f"out{l}", half * NT + i)
                    for kh in range(2):
                        w = weights(f"out{l}.{half}.{kh}", (4, 512))
                        for t in range(NT):
                            bank = ps[B[f"out{l}", half * NT + t][0]]
                            for k in range(4):
                                mm = product(bank[:, :], hT[:, 4 * kh + k, t * P:(t + 1) * P], w[:, k, :],
                                               start=kh == 0 and k == 0, stop=kh == 1 and k == 3)
                            if kh == 1:
                                fill_inc(mm, f"out{l}", half * NT + t)
                        if kh == 0:
                            mm.then_inc(piece_used, 1)
                    piece_end()

            def attention(tag, units, heads_n, lhs_q, rhs_k, v_of):
                n = len(units)
                pT = probsT if tag == "g" else mprobsT
                pr = probs if tag == "g" else mprobs
                S, PT, O = f"{tag}S", f"{tag}PT", f"{tag}O"
                if tag != "g":
                    S, PT, O = f"mS{tag}", f"mPT{tag}", f"mO{tag}"
                for i in range(n + 2):
                    if i < n:
                        t, h = units[i]
                        nk = P if t == 0 else T
                        bank = claim(S, i)
                        mm = product(bank[:, 0:nk], lhs_q(t, h), rhs_k(t, h), start=True, stop=True)
                        fill_inc(mm, S, i)
                    if 1 <= i <= n:
                        j = i - 1
                        t, h = units[j]
                        bank = claim(PT, j)
                        drained_wait(pe, S, j)
                        for kt in range(1 if t == 0 else NT):
                            mm = turn(bank[:, kt * P:(kt + 1) * P], pr[:, j % 2, kt * P:(kt + 1) * P])
                        fill_inc(mm, PT, j)
                    if i >= 2:
                        j = i - 2
                        t, h = units[j]
                        drained_wait(pe, PT, j)
                        if h == 0:
                            claim(O, t)
                        bank = ps[B[O, t][0]]
                        vs = v_of(t, h)
                        for kt, v in enumerate(vs):
                            mm = product(bank[:, h * HD:(h + 1) * HD], pT[:, j % 2, kt, :], v,
                                           start=kt == 0, stop=kt == len(vs) - 1)
                        if h == heads_n - 1:
                            fill_inc(mm, O, t)
                        else:
                            mm.then_inc(pv_done, 1)

            def experts(l):
                nb = blocks_of(pe, l)
                for b, n in enumerate(B.jobs[f"moe{l}"]):
                    pe.wait_ge(drained[b], n)
                for i in range(6):
                    drained_wait(pe, f"htok{l}", i)

                def gather_tables(b1):
                    pe.wait_ge(perm_ready[l], b1)
                    for t in range(NT):
                        turn(ps[5][:, t * P:(t + 1) * P], perm[:, t, :])
                    for t in range(NT):
                        mm = product(ps[5][:, T:T + EPG], perm[:, t, :], plan[:, 64 + 4 * t:68 + 4 * t], start=t == 0, stop=t == 2)
                    mm.then_inc(gather_full[l], 1)

                def gather(half):
                    for q in range(4):
                        k = 4 * half + q
                        for t in range(NT):
                            mm = product(ps[6 + half][:, q * P:(q + 1) * P], htok[:, t, k * P:(k + 1) * P], perm[:, t, :],
                                         start=t == 0, stop=t == 2)
                    mm.then_inc(gather_full[l], 1)

                def gate_up(b, j, k0, k1):
                    gu, _ = place(j)
                    bank = ps[2 + j % 2]
                    if k0 == 0:
                        pe.wait_ge(gu_loaded[l][j], b * 32 + 32)
                        if j < 2:
                            if j == 0:
                                pe.wait_ge(hts_ready[l], b * 2 + 2)
                                pe.wait_ge(scatter_read[l], b * 6 + 6)
                        else:
                            pe.wait_ge(mid_ready[l], b * EPG + (j - 1))
                    for k in range(k0, k1):
                        mm = product(bank[:, :], hTs[:, k, :], gu[:, :, k, :], start=k == 0, stop=k == KT - 1)
                    if k1 == KT:
                        mm.then_inc(gu_full[l], 1)

                def turn_mid(b, j):
                    pe.wait_ge(mid_ready[l], b * EPG + (j + 1))
                    for ft in range(2):
                        mm = turn(ps[4][:, ft * P:(ft + 1) * P], mid[:, j % 2, ft * P:(ft + 1) * P])
                    mm.then_inc(mt_full[l], 1)

                def down(b, j):
                    _, dn = place(j)
                    pe.wait_ge(down_loaded[l][j], b * 16 + 16)
                    pe.wait_ge(mt_read[l], b * EPG + (j + 1))
                    for half in range(2):
                        for ft in range(2):
                            mm = product(ps[half][:, :], midT[:, j % 2, ft, :], dn[:, ft, half * 512:half * 512 + 512],
                                         start=j == 0 and ft == 0, stop=j == EPG - 1 and ft == 1)
                    if j < EPG - 1:
                        mm.then_inc(expert_used[l], 1)
                    else:
                        mm.then_inc(y_full[l], 1)
                        due[:] = [1, expert_used[l]]

                def scatter(b):
                    pe.wait_ge(y_read[l], b + 1)
                    pe.wait_ge(aux_read[l], b + 1)
                    pe.wait_ge(mid_ready[l], b * EPG + EPG)
                    for c in range(2 * NT):
                        if c >= 4:
                            pe.wait_ge(scatter_read[l], b * 6 + 6 + (c - 3))
                        t, half = c // 2, c % 2
                        mm = product(ps[(2, 3, 0, 1, 2, 3)[c]][:, :], permT[:, t, :], ysb[:, half * 512:half * 512 + 512],
                                     start=True, stop=True)
                        mm.then_inc(scatter_full[l], 1)

                if due[0]:
                    turn(ps[5][:, 0:P], ident[:, :])
                turn(ps[5][:, 0:P], ident[:, :]).then_inc(expert_used[l], EPG)
                gather_tables(1)
                gather(0)
                gather(1)
                with pe.Fori(0, nb) as b:
                    gate_up(b, 0, 0, KT)
                    for j in range(1, EPG):
                        gate_up(b, j, 0, KT // 2)
                        turn_mid(b, j - 1)
                        gate_up(b, j, KT // 2, KT)
                        down(b, j - 1)
                    pe.wait_ge(aux_read[l], b + 1)
                    gather_tables(b + 2)
                    gather(0)
                    turn_mid(b, EPG - 1)
                    down(b, EPG - 1)
                    gather(1)
                    scatter(b)
                pe.wait_ge(scatter_read[l], nb * 6 + 6)
                pe.wait_ge(hts_ready[l], nb * 2 + 2)
                pe.wait_ge(aux_read[l], nb + 1)

            def moe(l):
                mod_vectors(l, (SH2, SC2))
                norm_transposes(l, 1)
                for i in range(6):
                    drained_wait(pe, f"hT{l}.1", i)
                bank = claim(f"router{l}")
                for t in range(NT):
                    for k in range(KT):
                        mm = product(bank[:, t * NE:(t + 1) * NE], hT[:, k, t * P:(t + 1) * P], routw[:, k, :],
                                       start=k == 0, stop=k == KT - 1)
                fill_inc(mm, f"router{l}")
                for t in range(NT):
                    for q in range(2):
                        bank = claim(f"htok{l}", 2 * t + q)
                        for j in range(4):
                            mm = turn(bank[:, j * P:(j + 1) * P], hT[:, 4 * q + j, t * P:(t + 1) * P])
                        fill_inc(mm, f"htok{l}", 2 * t + q)
                mod_vectors(l, (G2,))
                bank = claim(f"rank{l}")
                pe.wait_ge(in_route, 32 * (l + 1))
                pe.wait_ge(plan_sums[l], 1)
                product(bank[:, 0:12], before, sml[:, 5, 0:12], start=True, stop=False)
                product(bank[:, 0:12], onesr, plan[:, 0:12], start=False, stop=True)
                mm = product(bank[:, 12:16], onesr, plan[:, 12:16], start=True, stop=True)
                fill_inc(mm, f"rank{l}")
                if l == 0:
                    mod_vectors(1, (SH1, SC1))
                experts(l)

            loaded(pe, in_conv)
            bank = claim("convT")
            mm = pe.transpose(bank[:, 0:48], convraw, ident[0:48, 0:48])
            fill_inc(mm, "convT")

            loaded(pe, in_filt)
            bank = claim("filt1")
            mm = product(bank[0:HID, 0:T], filtc[0:EMB, 3 + HID:3 + 2 * HID], zT, start=True, stop=True)
            fill_inc(mm, "filt1")
            pe.wait_ge(sin_done, 1)
            bank = claim("filt2")
            mm = product(bank[0:HID, 0:T], filtc[:, 3:3 + HID], hidden[0:HID, :], start=True, stop=True)
            fill_inc(mm, "filt2")
            pe.wait_ge(sin_done, 2)
            pe.wait_ge(ones_set, 1)
            for od in range(2):
                for t in range(NT):
                    for r in range(2):
                        bank = claim(f"filt3.{od}", 2 * t + r)
                        mm = product(bank[:, :], hidden[:, t * P:(t + 1) * P], w3[:, 2 * od + r, :], start=True, stop=True)
                        fill_inc(mm, f"filt3.{od}", 2 * t + r)
                for g, tiles in enumerate(([0], [1, 2])):
                    bank = claim(f"energy{od}", g)
                    for t in tiles:
                        pe.wait_ge(esq_ready, od * NT + t + 1)
                        mm = product(bank[:, :], onesm, sqs[:, t, :], start=t == tiles[0], stop=t == tiles[-1])
                    fill_inc(mm, f"energy{od}", g)
                if od == 0:
                    loaded(pe, in_dft)
                pe.wait_ge(filt_ready, (od + 1) * NT)
                for r in range(2):
                    bank = claim(f"spec{od}", r)
                    mm = product(bank[:, :], dftp[:, r, :], filt[:, 0, r, :], start=True, stop=True)
                    fill_inc(mm, f"spec{od}", r)
                for ft in range(2):
                    for r in range(2):
                        bank = claim(f"spec{od}", 2 + 2 * ft + r)
                        for k in range(2):
                            mm = product(bank[:, :], dfts[:, r, k, ft * P:(ft + 1) * P], filt[:, 1 + k, r, :],
                                           start=k == 0, stop=k == 1)
                        fill_inc(mm, f"spec{od}", 2 + 2 * ft + r)

            mod_vectors(0, (SH1, SC1))
            norm_transposes(0, 0)
            for i in range(6):
                drained_wait(pe, "hT0.0", i)
            pe.wait_ge(spec_done, 12)
            for q in range(9):
                w = weights(f"in0.{q}", (KT, 256))
                if q < 6:
                    for mt in range(2):
                        bank = claim("uT", 2 * q + mt)
                        for k in range(KT):
                            mm = product(bank[:, 0:T], w[:, k, mt * P:(mt + 1) * P], hT[:, k, :], start=k == 0, stop=k == KT - 1)
                        fill_inc(mm, "uT", 2 * q + mt)
                else:
                    for t in range(NT):
                        i = (q - 6) * NT + t
                        bank = claim("qkv", i)
                        for k in range(KT):
                            mm = product(bank[:, 0:256], hT[:, k, t * P:(t + 1) * P], w[:, k, :], start=k == 0, stop=k == KT - 1)
                        fill_inc(mm, "qkv", i)
                piece_end()

            for part, stage in enumerate(("vtok", "x1tok")):
                pe.wait_ge(conv_done, NCH * (part + 1))
                for t in range(NT):
                    bank = claim(stage, t)
                    for c in range(NCH):
                        mm = turn(bank[:, c * P:(c + 1) * P], uc[:, part * NCH + c, t * P:(t + 1) * P])
                    fill_inc(mm, stage, t)
            for od in range(2):
                if od == 0:
                    for t in range(NT):
                        drained_wait(pe, "vtok", t)
                else:
                    for t in range(NT):
                        drained_wait(pe, "inv0", t)
                for ft in range(NT):
                    for r in range(2):
                        i = 2 * ft + r
                        bank = claim(f"fwd{od}", i)
                        if ft == 0:
                            mm = product(bank[:, :], dftp[:, r, :], vtok[:, 0, :], start=True, stop=True)
                        else:
                            for k in range(2):
                                mm = product(bank[:, :], dfts[:, r, k, (ft - 1) * P:ft * P], vtok[:, 1 + k, :],
                                               start=k == 0, stop=k == 1)
                        fill_inc(mm, f"fwd{od}", i)
                if od == 0:
                    for t in range(NT):
                        pe.wait_ge(y_ready, 1 if t == 0 else NT)
                        bank = claim("inv0", t)
                        if t == 0:
                            for r in range(2):
                                mm = product(bank[:, :], dftp[:, 2 + r, :], Y[:, 0, r, :], start=r == 0, stop=r == 1)
                        else:
                            for f in range(2):
                                for r in range(2):
                                    mm = product(bank[:, :], dfts[:, 2 + r, f, (t - 1) * P:t * P], Y[:, 1 + f, r, :],
                                                   start=f + r == 0, stop=f + r == 2)
                        fill_inc(mm, "inv0", t)
                else:
                    pe.wait_ge(y_ready, 2 * NT)
                    for c in range(NCH):
                        bank = claim("inv1", c)
                        for r in range(2):
                            mm = product(bank[:, 0:NPR], Y[:, 0, r, c * P:(c + 1) * P], dftp[:, 2 + r, :],
                                           start=r == 0, stop=r == 1)
                        for f in range(2):
                            for r in range(2):
                                mm = product(bank[:, NPR:T], Y[:, 1 + f, r, c * P:(c + 1) * P], dfts[:, 2 + r, f, :],
                                               start=f + r == 0, stop=f + r == 2)
                        fill_inc(mm, "inv1", c)

            pe.wait_ge(qk_ready, NT)
            for t in range(NT):
                for g in range(KVH):
                    bank = claim("qT", KVH * t + g)
                    for h in range(4):
                        c0 = (4 * g + h) * HD
                        mm = turn(bank[0:HD, h * P:(h + 1) * P], qkv[:, t, c0:c0 + HD])
                    fill_inc(mm, "qT", KVH * t + g)
            loaded(pe, in_attn)
            for g in range(KVH):
                bank = claim("kT", g)
                c0 = QH * HD + g * HD
                srcs = [qkv[:, 0, c0:c0 + HD], ck[:, g * HD:(g + 1) * HD], qkv[:, 1, c0:c0 + HD], qkv[:, 2, c0:c0 + HD]]
                for s, src in enumerate(srcs):
                    mm = turn(bank[0:HD, s * P:(s + 1) * P], src)
                fill_inc(mm, "kT", g)
            for i in range(NT * KVH):
                drained_wait(pe, "qT", i)
            for g in range(KVH):
                drained_wait(pe, "kT", g)

            def gqa_v(t, h):
                c0 = (QH + KVH) * HD + (h // 4) * HD
                own = [qkv[:, s, c0:c0 + HD] for s in range(NT)]
                cached = cv[:, (h // 4) * HD:(h // 4 + 1) * HD]
                return [own[0]] if t == 0 else [cached, own[1], own[2]]

            attention("g", units_gqa, QH, lambda t, h: qT[:, t, h, :],
                      lambda t, h: kT[:, h // 4, 0, :] if t == 0 else kT[:, h // 4, 1:4, :].rearrange("p a b -> p (a b)"), gqa_v)
            for t in range(NT):
                drained_wait(pe, "gO", t)
                bank = claim("goT", t)
                for c in range(4):
                    mm = turn(bank[:, c * P:(c + 1) * P], otok[:, t, c * P:(c + 1) * P])
                fill_inc(mm, "goT", t)
            mod_vectors(0, (G1,))
            for c in range(NCH):
                drained_wait(pe, "inv1", c)
            for t in range(NT):
                drained_wait(pe, "goT", t)
            out_projection(0)
            moe(0)

            norm_transposes(1, 0)
            for i in range(6):
                drained_wait(pe, "hT1.0", i)
            for t in range(NT):
                claim("um", t)
            for kh in range(2):
                w = weights(f"in1.{kh}", (4, ODD_IN))
                for t in range(NT):
                    bank = ps[B["um", t][0]]
                    for k in range(4):
                        mm = product(bank[:, 0:ODD_IN], hT[:, 4 * kh + k, t * P:(t + 1) * P], w[:, k, :],
                                       start=kh == 0 and k == 0, stop=kh == 1 and k == 3)
                    if kh == 1:
                        fill_inc(mm, "um", t)
                piece_end()
            pe.wait_ge(lora_ready, NT)
            loaded(pe, in_mla)
            for t in range(NT + 1):
                bank = claim("cT", t)
                srcs = [ckv_c] if t == NT else [um[:, t, c * P:(c + 1) * P] for c in range(3)]
                for c, src in enumerate(srcs):
                    mm = turn(bank[:, c * P:(c + 1) * P], src)
                fill_inc(mm, "cT", t)
            for t in range(NT + 1):
                drained_wait(pe, "cT", t)
            wq = [weights(f"uq{j}", (1, MH * QK)) for j in range(2)]
            wkv = weights("ukv", (1, MH * (NOPE + VD)))
            for g in range(NHG):
                for t in range(NT):
                    bank = claim(f"mq{g}", t)
                    for k in range(2):
                        mm = product(bank[:, 0:HG * QK], cT[:, k, t * P:(t + 1) * P],
                                       wq[k][:, 0, g * HG * QK:(g + 1) * HG * QK], start=k == 0, stop=k == 1)
                    fill_inc(mm, f"mq{g}", t)
                for t in range(NT + 1):
                    bank = claim(f"mkv{g}", t)
                    lhs = cvT if t == NT else cT[:, 2, t * P:(t + 1) * P]
                    mm = product(bank[:, :], lhs, wkv[:, 0, g * 512:(g + 1) * 512], start=True, stop=True)
                    fill_inc(mm, f"mkv{g}", t)
                if g == NHG - 1:
                    piece_end(3)
                pe.wait_ge(qk_ready, NT + 2 * (g + 1))
                for t in range(NT):
                    bank = claim(f"mqT{g}", t)
                    for h in range(HG):
                        mm = turn(bank[0:QK, h * P:(h + 1) * P], q4[:, t, h, :])
                    fill_inc(mm, f"mqT{g}", t)
                for s, t in enumerate((0, 3, 1, 2)):
                    bank = claim(f"mkT{g}", s)
                    for h in range(HG):
                        mm = turn(bank[0:QK, h * P:(h + 1) * P], k4[:, t, h, :])
                    fill_inc(mm, f"mkT{g}", s)
                for t in range(NT):
                    drained_wait(pe, f"mqT{g}", t)
                for t in range(NT + 1):
                    drained_wait(pe, f"mkT{g}", t)
                attention(str(g), units_mla, HG, lambda t, h: q4T[:, t, h, :],
                          lambda t, h: k4T[:, h, 0, :] if t == 0 else k4T[:, h, 1:4, :].rearrange("p a b -> p (a b)"),
                          lambda t, h: [v4[:, s, h, :] for s in ((0,) if t == 0 else (3, 1, 2))])
            for g in range(NHG):
                for t in range(NT):
                    drained_wait(pe, f"mO{g}", t)
            for t in range(NT):
                for q in range(2):
                    bank = claim("moT", 2 * t + q)
                    for c in range(4):
                        mm = turn(bank[:, c * P:(c + 1) * P], mtok[:, t, (4 * q + c) * P:(4 * q + c + 1) * P])
                    fill_inc(mm, "moT", 2 * t + q)
            mod_vectors(1, (G1,))
            for i in range(2 * NT):
                drained_wait(pe, "moT", i)
            out_projection(1)
            moe(1)

        @block.scalar
        def _(act):
            load(act, in_cond, condraw[:, 0, :], d["c_ctx"].rearrange("(p j) -> p j", j=KT))
            load(act, in_cond, condraw[:, 1, :], d["c"][0].rearrange("(p j) -> p j", j=KT))
            load(act, in_filt, zT, d["zT"])
            load(act, in_filt, filtc[0:EMB, 3 + HID:3 + 2 * HID], d["ev_filt_w1"][0])
            load(act, in_filt, filtc[:, 0:1], d["ev_filt_b1"].rearrange("a n -> n a"))
            load(act, in_filt, filtc[:, 1:2], d["ev_filt_b2"].rearrange("a n -> n a"))
            load(act, in_filt, filtc[:, 2:3], d["ev_filt_freq"].rearrange("a n -> n a"))
            load(act, in_filt, filtc[:, 3:3 + HID], d["ev_filt_w2"][0])
            load(act, in_filt, w3[0:HID, :, :], d["ev_filt_w3"][0].rearrange("k (a b) -> k a b", b=HY))
            load(act, in_filt, w3[HID:HID + 1, :, :], d["ev_filt_b3"].rearrange("k (a b) -> k a b", b=HY))
            load(act, in_filt, decay, d["decay"].rearrange("p (a b) -> p a b", b=HY))
            load(act, in_filt, hybias[:, 0, :], d["ev_hy_bias"][0, 0].partition_broadcast(P))
            load(act, in_filt, hybias[:, 1, :], d["ev_hy_bias"][0, 1].partition_broadcast(P))
            load(act, in_mod, ident[:, :], d["ident"])
            load(act, in_mod, rowsel[:, :, :], d["rowsel"].rearrange("p (a b) -> p a b", b=P))
            load(act, in_mod, chunksel[:, :, :], d["chunksel"].rearrange("p (a b) -> p a b", b=2))
            load(act, in_mod, bmod[:, :], d["b_mod"].rearrange("l (c n) -> (l c) n", n=512))
            for l in range(2):
                load(act, in_mod, gain[:, l, 0, :], d["norm_mix"][l].rearrange("(p j) -> p j", j=KT))
                load(act, in_mod, gain[:, l, 1, :], d["norm_ffn"][l].rearrange("(p j) -> p j", j=KT))
            load(act, in_mod, routw[:, :, :], d["router_w"].rearrange("(p j) n -> p j n", j=KT))
            load(act, in_conv, convraw[0:36, :], d["ev_conv_w"][0].rearrange("k (c n) -> (k c) n", n=P))
            load(act, in_conv, convraw[36:48, :], d["ev_conv_b"][0].rearrange("(c n) -> c n", n=P))
            load(act, in_x, x[:, 0, :], d["x_prompt"][0])
            load(act, in_x, x[:, 1:NT, :], d["x_sample"][0].rearrange("(t p) n -> p t n", p=P))

            loaded(act, in_cond)
            act.wait_ge(cond_zero, 1)
            for c in range(2):
                act.activation(condT[:, :, c], condraw[:, c, :], ACT.Silu).then_inc(cond_ready, 1)

            def copy_out(stage, i, dst, src, **kw):
                filled_wait(act, stage, i)
                drain_inc(act.activation(dst, src, kw.pop("func", ACT.Copy), **kw), stage, i)

            def bank_of(stage, i=0):
                return ps[B[stage, i][0]]

            def mod_rows(l, vectors):
                for v in vectors:
                    for half in range(2):
                        name = f"mod{l}.{v}.{half}"
                        bank = filled_wait(act, name)
                        drain_inc(act.activation(modrow[:, :], bank[:, :], ACT.Copy), name)
                        if v in (G1, G2):
                            for c in range(2):
                                sel = f"modsel{l}.{v}.{half}"
                                copy_out(sel, c, gb[:, c, half * 512:half * 512 + 512], bank_of(sel, c)[:, :])

            def norm(l, which, x_sem, x_count):
                s = 2 * l + which
                act.wait_ge(x_sem, x_count)
                for t in range(NT):
                    ins = act.activation(xn[:, t, :], x[:, t, :], ACT.Square, accum_out=ssq[:, s, t:t + 1])
                ins.then_inc(squares, 1)
                act.wait_ge(meansq, s + 1)
                act.activation(ssq[:, s, :], ssq[:, s, :], ACT.Sqrt).then_inc(rootsq, 1)

            def modulate(l, which):
                act.wait_ge(moda_ready, 2 * l + which + 1)
                sh = 0 if which == 0 else 3
                for i in range(0, 6, 2):
                    t, q = i // 2, i % 2
                    bank = filled_wait(act, f"hT{l}.{which}", i)
                    for j in range(4):
                        k = 4 * q + j
                        ins = act.activation(hT[:, k, t * P:(t + 1) * P], bank[:, j * P:(j + 1) * P], ACT.Identity,
                                             bias=modT[:, l, sh, k, GRP[t]:GRP[t] + 1],
                                             scale=modA[:, l, which, k, GRP[t]:GRP[t] + 1])
                    drain_inc(ins, f"hT{l}.{which}", i)

            def attention(tag, units):
                S, PT = (f"{tag}S", f"{tag}PT") if tag == "g" else (f"mS{tag}", f"mPT{tag}")
                pr = probs if tag == "g" else mprobs
                first = 0 if tag == "g" else len(units_gqa) + int(tag) * len(units_mla)
                for i, (t, h) in enumerate(units):
                    nk = P if t == 0 else T
                    act.wait_ge(negmax_ready, first + i + 1)
                    if i >= 2:
                        filled_wait(act, PT, i - 2)
                    bank = bank_of(S, i)
                    ins = act.activation(pr[:, i % 2, 0:nk], bank[:, 0:nk], ACT.Exp, bias=negmax[:, i:i + 1],
                                         accum_out=psumexp[:, i:i + 1])
                    drain_inc(ins, S, i)

            def experts(l):
                nb = blocks_of(act, l)

                def inputs(half):
                    return act.activation(hTs[:, 4 * half:4 * half + 4, :].rearrange("p a b -> p (a b)"), ps[6 + half][:, :], ACT.Copy)

                act.wait_ge(gather_full[l], 2)
                inputs(0).then_inc(hts_ready[l], 1)
                act.wait_ge(gather_full[l], 3)
                inputs(1).then_inc(hts_ready[l], 1)
                with act.Fori(0, nb) as b:
                    for j in range(EPG):
                        act.wait_ge(gu_full[l], b * EPG + (j + 1))
                        if j >= 2:
                            act.wait_ge(mid_ready[l], b * EPG + (j - 1))
                        act.activation(sil[:, j % 2, :], ps[2 + j % 2][:, 0:DE], ACT.Silu).then_inc(silu_ready[l], 1)
                    act.wait_ge(gather_full[l], b * 3 + 5)
                    inputs(0).then_inc(hts_ready[l], 1)
                    act.wait_ge(y_full[l], b + 1)
                    for half in range(2):
                        ins = act.activation(ysb[:, half * 512:half * 512 + 512], ps[half][:, :], ACT.Copy)
                    ins.then_inc(y_read[l], 1)
                    act.wait_ge(gather_full[l], b * 3 + 6)
                    inputs(1).then_inc(hts_ready[l], 1)

            def moe(l):
                norm(l, 1, x_mixed, 2 * NT * (l + 1))
                mod_rows(l, (SH2, SC2))
                modulate(l, 1)
                copy_out(f"router{l}", 0, sml[:, 0, 0:NT * NE], bank_of(f"router{l}")[:, 0:NT * NE], func=ACT.Sigmoid)
                for i in range(6):
                    t, q = i // 2, i % 2
                    copy_out(f"htok{l}", i, htok[:, t, q * 512:q * 512 + 512], bank_of(f"htok{l}", i)[:, :])
                mod_rows(l, (G2,))
                if l == 0:
                    mod_rows(1, (SH1, SC1))
                experts(l)

            for i in range(2):
                act.wait_ge(sin_arg, i + 1)
                act.activation(hidden[0:HID, :], hidden[0:HID, :], ACT.Sin).then_inc(sin_done, 1)
            for od in range(2):
                for g in range(2):
                    act.wait_ge(eroot, 2 * od + g + 1)
                    act.activation(esc[:, g, :], esc[:, g, :], ACT.Sqrt).then_inc(escale_ready, 1)
            mod_rows(0, (SH1, SC1))
            norm(0, 0, in_x, 16 * LOADS["in_x"])
            modulate(0, 0)
            act.wait_ge(conv_copied, 1)
            for m in range(3 * NCH):
                bank = filled_wait(act, "uT", m)
                act.activation(uc[:, m, :], bank[:, 0:T], ACT.Identity, bias=convT[:, 3, m:m + 1], scale=convT[:, 1, m:m + 1])
                drain_inc(act.activation(uT[:, m, :], bank[:, 0:T], ACT.Copy), "uT", m)
            for q in range(3):
                for t in range(NT):
                    i = q * NT + t
                    copy_out("qkv", i, qkv[:, t, q * 256:(q + 1) * 256], bank_of("qkv", i)[:, 0:256])
            for t in range(NT):
                copy_out("vtok", t, vtok[:, t, :], bank_of("vtok", t)[:, :])
            for t in range(NT):
                copy_out("x1tok", t, x1tok[:, t, :], bank_of("x1tok", t)[:, :])
            act.wait_ge(qvar, 1)
            act.activation(statA[:, 1, 0:30], statA[:, 0, 0:30], ACT.Sqrt).then_inc(qroot, 1)
            for i in range(NT * KVH):
                t, g = i // KVH, i % KVH
                copy_out("qT", i, qT[:, t, 4 * g:4 * g + 4, :].rearrange("p a b -> p (a b)"), bank_of("qT", i)[0:HD, :])
            for g in range(KVH):
                copy_out("kT", g, kT[:, g, :, :].rearrange("p a b -> p (a b)"), bank_of("kT", g)[0:HD, :])
            attention("g", units_gqa)
            for t in range(NT):
                copy_out("goT", t, hT[:, 4:8, t * P:(t + 1) * P], bank_of("goT", t)[:, :].rearrange("p (a b) -> p a b", b=P))
            mod_rows(0, (G1,))
            moe(0)

            norm(1, 0, x_done, 1)
            modulate(1, 0)
            for t in range(NT):
                copy_out("um", t, um[:, t, :], bank_of("um", t)[:, 0:ODD_IN])
            act.drain()
            for t in range(NT):
                act.activation(junk[:, t, 0:QR], um[:, t, 0:QR], ACT.Square, accum_out=statA[:, 0, t:t + 1])
                ins = act.activation(junk[:, NT + t, 0:KVR], um[:, t, QR:QR + KVR], ACT.Square, accum_out=statA[:, 0, NT + t:NT + t + 1])
            ins.then_inc(lora_sq, 1)
            act.wait_ge(lora_var, 1)
            act.activation(statA[:, 1, 0:2 * NT], statA[:, 0, 0:2 * NT], ACT.Sqrt).then_inc(lora_root, 1)
            for t in range(NT + 1):
                if t < NT:
                    copy_out("cT", t, cT[:, :, t * P:(t + 1) * P], bank_of("cT", t)[:, 0:3 * P].rearrange("p (a b) -> p a b", b=P))
                else:
                    copy_out("cT", t, cvT, bank_of("cT", t)[:, 0:P])
            for g in range(NHG):
                for t in range(NT):
                    copy_out(f"mq{g}", t, q4[:, t, :, :].rearrange("p h e -> p (h e)"), bank_of(f"mq{g}", t)[:, 0:HG * QK])
                for t in range(NT + 1):
                    bank = filled_wait(act, f"mkv{g}", t)
                    b4 = bank[:, :].rearrange("p (h e) -> p h e", h=HG)
                    act.activation(v4[:, t, :, :], b4[:, :, NOPE:NOPE + VD], ACT.Copy)
                    drain_inc(act.activation(k4[:, t, :, 0:NOPE], b4[:, :, 0:NOPE], ACT.Copy), f"mkv{g}", t)
                act.wait_ge(qvar, 2 + g)
                act.activation(statA[:, 1, 0:28], statA[:, 0, 0:28], ACT.Sqrt).then_inc(qroot, 1)
                for t in range(NT):
                    copy_out(f"mqT{g}", t, q4T[:, t, :, :].rearrange("p a b -> p (a b)"), bank_of(f"mqT{g}", t)[0:QK, :])
                for s in range(NT + 1):
                    copy_out(f"mkT{g}", s, k4T[:, :, s, :], bank_of(f"mkT{g}", s)[0:QK, :].rearrange("p (a b) -> p a b", b=P))
                attention(str(g), units_mla)
            for i in range(2 * NT):
                t, q = i // 2, i % 2
                copy_out("moT", i, hT[:, 4 * q:4 * q + 4, t * P:(t + 1) * P], bank_of("moT", i)[:, :].rearrange("p (a b) -> p a b", b=P))
            mod_rows(1, (G1,))
            moe(1)

        @block.vector
        def _(dve):
            def settle():
                dve.drain()

            def bank_of(stage, i=0):
                return ps[B[stage, i][0]]

            def mod_columns(l, vectors):
                for v in vectors:
                    for half in range(2):
                        sel = f"modsel{l}.{v}.{half}"
                        bank = filled_wait(dve, sel)
                        rows = slice(64 * half, 64 * half + 64)
                        drain_inc(dve.tensor_copy(modT[rows, l, v, :, :], bank[rows, 0:2 * KT].rearrange("p (a b) -> p a b", b=2)), sel)
                which = 0 if SH1 in vectors else 1
                settle()
                A = modA[:, l, which, :, :]
                dve.tensor_scalar(A, modT[:, l, 3 * which + 1, :, :], 1.0, None, ALU.add)
                settle()
                g = gain[:, l, which, :].unsqueeze(2).broadcast_to([P, KT, 2])
                dve.tensor_tensor(A, A, g, ALU.mult).then_inc(moda_ready, 1)

            def norm(s):
                dve.wait_ge(squares, s + 1)
                dve.tensor_scalar(ssq[:, s, :], ssq[:, s, :], 1.0 / D, EPS, ALU.mult, ALU.add).then_inc(meansq, 1)
                dve.wait_ge(rootsq, s + 1)
                dve.reciprocal(ssq[:, s, :], ssq[:, s, :])
                settle()
                for t in range(NT):
                    dve.tensor_scalar(xn[:, t, :], x[:, t, :], ssq[:, s, t:t + 1], None, ALU.mult).then_inc(xn_ready, 1)

            def modulate(l, which):
                settle()
                sh = 0 if which == 0 else 3
                for i in range(1, 6, 2):
                    t, q = i // 2, i % 2
                    bank = filled_wait(dve, f"hT{l}.{which}", i)
                    for j in range(4):
                        k = 4 * q + j
                        ins = dve.tensor_scalar(hT[:, k, t * P:(t + 1) * P], bank[:, j * P:(j + 1) * P],
                                                modA[:, l, which, k, GRP[t]:GRP[t] + 1],
                                                modT[:, l, sh, k, GRP[t]:GRP[t] + 1], ALU.mult, ALU.add)
                    drain_inc(ins, f"hT{l}.{which}", i)

            def attention(tag, units, heads, o_dst):
                S, PT, O = (f"{tag}S", f"{tag}PT", f"{tag}O") if tag == "g" else (f"mS{tag}", f"mPT{tag}", f"mO{tag}")
                pT = probsT if tag == "g" else mprobsT
                pvs = 0 if tag == "g" else NT * (QH - 1) + int(tag) * NT * (HG - 1)
                n = len(units)
                for i in range(n + 2):
                    if i < n:
                        t, h = units[i]
                        nk = P if t == 0 else T
                        bank = filled_wait(dve, S, i)
                        dve.tensor_reduce(negmax[:, i:i + 1], bank[:, 0:nk], AXX, ALU.max, negate=True).then_inc(negmax_ready, 1)
                    if 1 <= i <= n:
                        j = i - 1
                        t, h = units[j]
                        nk = P if t == 0 else T
                        bank = filled_wait(dve, PT, j)
                        if j >= 2:
                            tj, hj = units[j - 2]
                            if hj == heads - 1:
                                filled_wait(dve, O, tj)
                            else:
                                dve.wait_ge(pv_done, pvs + tj * (heads - 1) + hj + 1)
                        drain_inc(dve.tensor_copy(pT[:, j % 2, :, :].rearrange("p a b -> p (a b)")[:, 0:nk], bank[:, 0:nk]), PT, j)
                    if i >= 2 and units[i - 2][1] == heads - 1:
                        t = units[i - 2][0]
                        dve.reciprocal(rinv[:, 0:heads], psumexp[:, t * heads:(t + 1) * heads])
                        settle()
                        bank = filled_wait(dve, O, t)
                        ins = dve.tensor_tensor(o_dst(t), bank[:, 0:heads * HD].rearrange("p (h e) -> p h e", e=HD),
                                                rinv[:, 0:heads].unsqueeze(2).broadcast_to([P, heads, HD]), ALU.mult)
                        drain_inc(ins, O, t)

            def rope(v, tbl, ra, rb, heads, width):
                c = width // 4
                split = lambda a: a.rearrange("p h (x y z) -> p h x y z", x=2, y=2)
                cos = tbl[:, 0, :].unsqueeze(1).broadcast_to([P, heads, width])
                sin = tbl[:, 1, :].rearrange("p (x y z) -> p x y z", x=2, y=2)
                dve.tensor_tensor(ra, v, cos, ALU.mult)
                for part in range(2):
                    s = sin[:, :, part, :].unsqueeze(1).broadcast_to([P, heads, 2, c])
                    dve.tensor_tensor(split(rb)[:, :, :, part, :], split(v)[:, :, :, 1 - part, :], s, ALU.mult)
                settle()
                return dve.tensor_tensor(v, ra, rb, ALU.add)

            def out_projection(l):
                for half in range(2):
                    cols = slice(half * 512, half * 512 + 512)
                    for t in range(NT):
                        i = half * NT + t
                        if i == 0:
                            for h2 in range(2):
                                for c in range(2):
                                    drained_wait(dve, f"modsel{l}.{G1}.{h2}", c)
                        bank = filled_wait(dve, f"out{l}", i)
                        tmp = tmpa if i % 2 == 0 else tmpb
                        drain_inc(dve.tensor_tensor(tmp, bank[:, :], gb[:, GRP[t], cols], ALU.mult), f"out{l}", i)
                        settle()
                        dve.tensor_tensor(x[:, t, cols], x[:, t, cols], tmp, ALU.add).then_inc(x_mixed, 1)

            def route(l):
                drained_wait(dve, f"router{l}")
                col = lambda i, n: sml[:, i, 0:n]
                by = lambda a, n: a.rearrange("p (a b) -> p a b", b=n)
                wide = lambda a, n, m: a.unsqueeze(2).broadcast_to([P, n, m])
                every = lambda a, n: a.unsqueeze(1).broadcast_to([P, NT, n])
                scores, sel, pairs, t3, t4 = col(0, 48), col(1, 48), col(2, 72), col(3, 48), col(4, 48)
                gmask, hot = col(5, 12), col(6, 48)
                small = col(7, 72)
                dve.tensor_tensor(by(sel, NE), by(scores, NE), every(routb[:, :], NE), ALU.add)
                settle()
                s4, p6 = by(sel, EPG), by(pairs, 6)
                dve.tensor_tensor(p6[:, :, 0:3], s4[:, :, 0:3], s4[:, :, 1:4], ALU.add)
                dve.tensor_tensor(p6[:, :, 3:5], s4[:, :, 0:2], s4[:, :, 2:4], ALU.add)
                dve.tensor_tensor(p6[:, :, 5:6], s4[:, :, 0:1], s4[:, :, 3:4], ALU.add)
                settle()
                dve.tensor_reduce(small[:, 0:12], p6, AXX, ALU.max)
                settle()

                def first_best(out, v, n, rank, best):
                    dve.tensor_reduce(best, by(v, n), AXX, ALU.max)
                    settle()
                    dve.tensor_tensor(by(out, n), by(v, n), wide(best, NT, n), ALU.is_equal)
                    settle()
                    dve.tensor_tensor(by(out, n), by(out, n), every(rank, n), ALU.mult)
                    settle()
                    dve.tensor_reduce(best, by(out, n), AXX, ALU.max)
                    settle()
                    dve.tensor_tensor(by(out, n), by(out, n), wide(best, NT, n), ALU.is_equal)
                    settle()

                first_best(gmask, small[:, 0:12], NG, rank_e[:, NE - NG:], small[:, 12:15])
                dve.tensor_scalar(small[:, 16:28], gmask, 1e30, -1e30, ALU.mult, ALU.add)
                dve.tensor_tensor(by(t3, EPG), by(sel, EPG), wide(gmask, NT * NG, EPG), ALU.mult)
                settle()
                dve.tensor_tensor(by(t3, EPG), by(t3, EPG), wide(small[:, 16:28], NT * NG, EPG), ALU.add)
                settle()
                first_best(hot, t3, NE, rank_e[:, :], small[:, 12:15])
                dve.scalar_tensor_tensor(out=t3, in0=hot, scalar=-2e30, in1=t3, op0=ALU.mult, op1=ALU.add)
                settle()
                first_best(t4, t3, NE, rank_e[:, :], small[:, 12:15])
                dve.tensor_tensor(hot, hot, t4, ALU.add)
                settle()
                dve.tensor_tensor(t3, hot, scores, ALU.mult)
                settle()
                dve.tensor_reduce(small[:, 12:15], by(t3, NE), AXX, ALU.add)
                settle()
                dve.reciprocal(small[:, 12:15], small[:, 12:15])
                settle()
                dve.tensor_tensor(gates[:, :, :], by(t3, NE), wide(small[:, 12:15], NT, NE), ALU.mult)
                settle()

            def make_plan(l):
                gm = sml[:, 5, 0:12]
                small = sml[:, 7, :]
                cum, tot, rank, size, nblk, end, first, slot, grp = (
                    plan[:, 0:12], plan[:, 12:16], plan[:, 16:28], plan[:, 28:32], plan[:, 32:36],
                    plan[:, 36:40], plan[:, 40:44], plan[:, 44:47], plan[:, 48:54])
                tile = lambda t: gm[:, 4 * t:4 * t + 4]
                dve.memset(onesr, 1.0)
                dve.memset(cum[:, 0:4], 0.0)
                dve.tensor_copy(cum[:, 4:8], tile(0))
                dve.tensor_tensor(cum[:, 8:12], tile(0), tile(1), ALU.add)
                settle()
                dve.tensor_tensor(tot, cum[:, 8:12], tile(2), ALU.add).then_inc(plan_sums[l], 1)
                g4 = gates[:, :, :].rearrange("p t (g e) -> p t g e", e=EPG)
                gsum = plan[:, 64:76].rearrange("p (t e) -> p t e", e=EPG)
                dve.tensor_tensor(gsum, g4[:, :, 0, :], g4[:, :, 1, :], ALU.add)
                for g in (2, 3):
                    settle()
                    dve.tensor_tensor(gsum, gsum, g4[:, :, g, :], ALU.add)
                bank = filled_wait(dve, f"rank{l}")
                drain_inc(dve.tensor_copy(plan[:, 16:32], bank[:, 0:16]), f"rank{l}")
                settle()
                dve.tensor_scalar(nblk, size, 0.0, None, ALU.is_gt)
                for m in (1, 2):
                    settle()
                    dve.scalar_tensor_tensor(out=nblk, in0=size, scalar=float(m * P), in1=nblk, op0=ALU.is_gt, op1=ALU.add)
                settle()
                dve.tensor_copy(end, nblk)
                for g in range(1, NG):
                    settle()
                    dve.tensor_tensor(end[:, g:g + 1], end[:, g - 1:g], nblk[:, g:g + 1], ALU.add)
                settle()
                dve.tensor_tensor(first, end, nblk, ALU.subtract)
                dve.tensor_scalar(grp, slots[:, 0:NBLK], end[:, 0:1], None, ALU.is_ge)
                for g in (1, 2):
                    settle()
                    dve.scalar_tensor_tensor(out=grp, in0=slots[:, 0:NBLK], scalar=end[:, g:g + 1], in1=grp, op0=ALU.is_ge, op1=ALU.add)
                settle()
                dve.tensor_copy(meta[0:1, l, 0:1], end[0:1, 3:4])
                dve.tensor_copy(meta[0:1, l, 1:1 + NBLK], grp[0:1, :]).then_inc(plan_ready[l], 1)
                dve.tensor_scalar(first, first, float(P), None, ALU.mult)
                settle()
                by = lambda a: a.rearrange("p (t g) -> p t g", g=NG)
                dve.tensor_tensor(by(rank), by(rank), first.unsqueeze(1).broadcast_to([P, NT, NG]), ALU.add)
                settle()
                dve.tensor_tensor(rank, rank, gm, ALU.mult)
                settle()
                dve.tensor_reduce(slot, by(rank), AXX, ALU.add)
                settle()

            def experts(l):
                slot, gslot = plan[:, 44:47], plan[:, 80:84]
                nb = blocks_of(dve, l)

                def permute():
                    for t in range(NT):
                        ins = dve.tensor_scalar(perm[:, t, :], slots, slot[:, t:t + 1], None, ALU.is_equal)
                    ins.then_inc(perm_ready[l], 1)
                    settle()
                    dve.tensor_scalar(slot, slot, float(-P), None, ALU.add)
                    settle()

                def tables(count):
                    dve.wait_ge(gather_full[l], count)
                    dve.tensor_copy(gslot, ps[5][:, T:T + EPG])
                    dve.tensor_copy(permT.rearrange("p a b -> p (a b)"), ps[5][:, 0:T]).then_inc(aux_read[l], 1)
                    settle()

                def turned(b, j):
                    dve.wait_ge(mt_full[l], b * EPG + (j + 1))
                    dve.tensor_copy(midT[:, j % 2, :, :].rearrange("p a b -> p (a b)"), ps[4][:, 0:DE]).then_inc(mt_read[l], 1)

                for h2 in range(2):
                    for c in range(2):
                        drained_wait(dve, f"modsel{l}.{G2}.{h2}", c)
                permute()
                tables(1)
                dve.drain().then_inc(scatter_read[l], 6)
                with dve.Fori(0, nb) as b:
                    for j in range(EPG):
                        if j:
                            turned(b, j - 1)
                        dve.wait_ge(silu_ready[l], b * EPG + (j + 1))
                        dve.scalar_tensor_tensor(out=mid[:, j % 2, :], in0=sil[:, j % 2, :], scalar=gslot[:, j:j + 1],
                                                 in1=ps[2 + j % 2][:, DE:2 * DE], op0=ALU.mult, op1=ALU.mult).then_inc(mid_ready[l], 1)
                        if j == 0:
                            dve.wait_ge(gather_full[l], b * 3 + 3)
                            permute()
                    turned(b, EPG - 1)
                    for c in range(2 * NT):
                        t, half = c // 2, c % 2
                        dve.wait_ge(scatter_full[l], b * 6 + (c + 1))
                        dve.tensor_tensor(gtmp[:, c, :], ps[(2, 3, 0, 1, 2, 3)[c]][:, :], gb[:, GRP[t], half * 512:half * 512 + 512],
                                          ALU.mult).then_inc(scatter_read[l], 1)
                    tables(b * 3 + 4)
                    for t in range(NT):
                        dve.tensor_tensor(x[:, t, :], x[:, t, :], gtmp[:, 2 * t:2 * t + 2, :].rearrange("p a b -> p (a b)"), ALU.add)
                    settle()
                dve.drain().then_inc(x_done, 1)

            def moe(l):
                norm(2 * l + 1)
                mod_columns(l, (SH2, SC2))
                modulate(l, 1)
                route(l)
                dve.wait_ge(in_route, 32 * (l + 1))
                make_plan(l)
                if l == 0:
                    mod_columns(1, (SH1, SC1))
                experts(l)

            dve.memset(hidden[HID:HID + 1, :], 1.0)
            dve.memset(onesm, 1.0).then_inc(ones_set, 1)
            for e in range(NE):
                dve.memset(rank_e[:, e:e + 1], float(NE - e))
            bank = filled_wait(dve, "convT")
            ins = dve.tensor_copy(convT[:, :, :], bank[:, 0:48].rearrange("p (a b) -> p a b", b=3 * NCH))
            drain_inc(ins, "convT")
            dve.drain().then_inc(conv_copied, 1)

            hid = hidden[0:HID, :]
            loaded(dve, in_filt)
            for i in range(2):
                bank = filled_wait(dve, f"filt{i + 1}")
                drain_inc(dve.tensor_scalar(hid, bank[0:HID, 0:T], filtc[:, i:i + 1], filtc[:, 2:3], ALU.add, ALU.mult), f"filt{i + 1}")
                settle()
                dve.tensor_scalar(turns, hid, 1.0 / (2 * math.pi), ROUNDER, ALU.mult, ALU.add)
                settle()
                dve.tensor_scalar(turns, turns, ROUNDER, None, ALU.subtract)
                for part in (TWO_PI_A, TWO_PI_B, TWO_PI_C):
                    settle()
                    dve.scalar_tensor_tensor(out=hid, in0=turns, scalar=-part, in1=hid, op0=ALU.mult, op1=ALU.add)
                settle()
                dve.tensor_scalar(hid, hid, SIN_MAX, -SIN_MAX, ALU.min, ALU.max).then_inc(sin_arg, 1)

            for od in range(2):
                for t in range(NT):
                    for r in range(2):
                        bank = filled_wait(dve, f"filt3.{od}", 2 * t + r)
                        drain_inc(dve.tensor_tensor(filt[:, t, r, :], bank[:, :], decay[:, t, :], ALU.mult), f"filt3.{od}", 2 * t + r)
                    settle()
                    if t < 2:
                        dve.memset(filt[0:1, t, 1, :], 0.0)
                        settle()
                    dve.tensor_tensor(sqd, filt[:, t, 0, :], filt[:, t, 1, :], ALU.add)
                    dve.tensor_tensor(filt[:, t, 1, :], filt[:, t, 0, :], filt[:, t, 1, :], ALU.subtract)
                    settle()
                    dve.tensor_copy(filt[:, t, 0, :], sqd).then_inc(filt_ready, 1)
                    dve.tensor_tensor(sqs[:, t, :], filt[:, t, 1, :], filt[:, t, 1, :], ALU.mult)
                    dve.tensor_tensor(sqd, sqd, sqd, ALU.mult)
                    settle()
                    dve.tensor_tensor(sqs[:, t, :], sqs[:, t, :], sqd, ALU.add).then_inc(esq_ready, 1)
                for g in range(2):
                    bank = filled_wait(dve, f"energy{od}", g)
                    drain_inc(dve.tensor_scalar(esc[:, g, :], bank[:, :], 0.5, EPS, ALU.mult, ALU.add), f"energy{od}", g)
                    dve.drain().then_inc(eroot, 1)
                for g in range(2):
                    dve.wait_ge(escale_ready, 2 * od + g + 1)
                    dve.reciprocal(esc[:, g, :], esc[:, g, :])
                settle()
                for i in range(2 * NT):
                    ft, r = i // 2, i % 2
                    bank = filled_wait(dve, f"spec{od}", i)
                    ins = dve.tensor_tensor(H[:, od, r, ft, :], bank[:, :], esc[:, GRP[ft], :], ALU.mult)
                    drain_inc(ins, f"spec{od}", i)
                settle()
                for ft in range(NT):
                    dve.tensor_tensor(H[:, od, 0, ft, :], H[:, od, 0, ft, :], hybias[:, od, :], ALU.add)
                dve.drain().then_inc(spec_done, 6)

            loaded(dve, in_mod)
            mod_columns(0, (SH1, SC1))
            norm(0)
            modulate(0, 0)

            for m in range(3 * NCH):
                drained_wait(dve, "uT", m)
                for a, b in ((0, NPR), (NPR, T)):
                    dve.scalar_tensor_tensor(out=uc[:, m, a + 1:b], in0=uT[:, m, a:b - 1], scalar=convT[:, 0, m:m + 1],
                                             in1=uc[:, m, a + 1:b], op0=ALU.mult, op1=ALU.add)
                settle()
                for a, b in ((0, NPR), (NPR, T)):
                    ins = dve.scalar_tensor_tensor(out=uc[:, m, a:b - 1], in0=uT[:, m, a + 1:b], scalar=convT[:, 2, m:m + 1],
                                                   in1=uc[:, m, a:b - 1], op0=ALU.mult, op1=ALU.add)
                ins.then_inc(conv_done, 1)

            for od in range(2):
                for ft in range(NT):
                    Hr, Hi = H[:, od, 0, ft, :], H[:, od, 1, ft, :]
                    settle()
                    bank = filled_wait(dve, f"fwd{od}", 2 * ft)
                    dve.tensor_tensor(Y[:, ft, 0, :], bank[:, :], Hr, ALU.mult)
                    drain_inc(dve.tensor_tensor(Y[:, ft, 1, :], bank[:, :], Hi, ALU.mult), f"fwd{od}", 2 * ft)
                    bank = filled_wait(dve, f"fwd{od}", 2 * ft + 1)
                    dve.tensor_tensor(tmpa, bank[:, :], Hi, ALU.mult)
                    drain_inc(dve.tensor_tensor(tmpb, bank[:, :], Hr, ALU.mult), f"fwd{od}", 2 * ft + 1)
                    settle()
                    dve.tensor_tensor(Y[:, ft, 0, :], Y[:, ft, 0, :], tmpa, ALU.subtract)
                    dve.tensor_tensor(Y[:, ft, 1, :], Y[:, ft, 1, :], tmpb, ALU.add).then_inc(y_ready, 1)
                if od == 0:
                    for t in range(NT):
                        drained_wait(dve, "x1tok", t)
                        bank = filled_wait(dve, "inv0", t)
                        drain_inc(dve.tensor_tensor(vtok[:, t, :], bank[:, :], x1tok[:, t, :], ALU.mult), "inv0", t)
                else:
                    for c in range(NCH):
                        bank = filled_wait(dve, "inv1", c)
                        drain_inc(dve.tensor_tensor(hT[:, c, :], bank[:, 0:T], uc[:, 2 * NCH + c, :], ALU.mult), "inv1", c)

            loaded(dve, in_attn)
            dve.tensor_scalar(qkgain[:, 0, :], qkgain[:, 0, :], HD ** -0.5, None, ALU.mult)
            QKH = QH + KVH
            for t in range(NT):
                for q in range(3):
                    drained_wait(dve, "qkv", q * NT + t)
                v = qkv[:, t, 0:QKH * HD].rearrange("p (h e) -> p h e", e=HD)
                dve.tensor_tensor(qsq, v, v, ALU.mult)
                settle()
                dve.tensor_reduce(statA[:, 0, QKH * t:QKH * (t + 1)], qsq, AXX, ALU.add)
                settle()
            dve.tensor_scalar(statA[:, 0, 0:30], statA[:, 0, 0:30], 1.0 / HD, EPS, ALU.mult, ALU.add).then_inc(qvar, 1)
            dve.wait_ge(qroot, 1)
            dve.reciprocal(statA[:, 1, 0:30], statA[:, 1, 0:30])
            settle()
            for t in range(NT):
                v = qkv[:, t, 0:QKH * HD].rearrange("p (h e) -> p h e", e=HD)
                dve.tensor_tensor(v, v, statA[:, 1, QKH * t:QKH * (t + 1)].unsqueeze(2).broadcast_to([P, QKH, HD]), ALU.mult)
                settle()
                dve.tensor_tensor(v[:, 0:QH, :], v[:, 0:QH, :], qkgain[:, 0, :].unsqueeze(1).broadcast_to([P, QH, HD]), ALU.mult)
                ins = dve.tensor_tensor(v[:, QH:QKH, :], v[:, QH:QKH, :], qkgain[:, 1, :].unsqueeze(1).broadcast_to([P, KVH, HD]), ALU.mult)
                if t:
                    settle()
                    ins = rope(v, ropeq[:, t - 1, :, :], qsq, qrb, QKH, HD)
                ins.then_inc(qk_ready, 1)
            attention("g", units_gqa, QH, lambda t: otok[:, t, :].rearrange("p (h e) -> p h e", e=HD))
            out_projection(0)
            moe(0)

            norm(2)
            modulate(1, 0)
            loaded(dve, in_mla)
            dve.wait_ge(lora_sq, 1)
            dve.tensor_scalar(statA[:, 0, 0:NT], statA[:, 0, 0:NT], 1.0 / QR, EPS, ALU.mult, ALU.add)
            dve.tensor_scalar(statA[:, 0, NT:2 * NT], statA[:, 0, NT:2 * NT], 1.0 / KVR, EPS, ALU.mult, ALU.add).then_inc(lora_var, 1)
            dve.tensor_scalar(mgain[:, 0, :], mgain[:, 0, :], QK ** -0.5, None, ALU.mult)
            dve.wait_ge(lora_root, 1)
            dve.reciprocal(statA[:, 1, 0:2 * NT], statA[:, 1, 0:2 * NT])
            settle()
            for t in range(NT):
                for c0, c1, i in ((0, QR, t), (QR, QR + KVR, NT + t)):
                    ins = dve.scalar_tensor_tensor(out=um[:, t, c0:c1], in0=um[:, t, c0:c1], scalar=statA[:, 1, i:i + 1],
                                                   in1=lgain[:, c0:c1], op0=ALU.mult, op1=ALU.mult)
                ins.then_inc(lora_ready, 1)
            for g in range(NHG):
                nq, nkk = NT * HG, (NT + 1) * HG
                flat = lambda a: a.rearrange("p t h e -> p (t h) e")
                if g:
                    for s_ in range(NT + 1):
                        filled_wait(dve, f"mkT{g - 1}", s_)
                for t in range(NT + 1):
                    kr = kr_c if t == NT else um[:, t, QR + KVR:ODD_IN]
                    dve.tensor_copy(k4[:, t, :, NOPE:QK], kr.unsqueeze(1).broadcast_to([P, HG, ROPE]))
                for t in range(NT):
                    drained_wait(dve, f"mq{g}", t)
                dve.tensor_tensor(flat(msq)[:, 0:nq, :], flat(q4), flat(q4), ALU.mult)
                settle()
                dve.tensor_reduce(statA[:, 0, 0:nq], flat(msq)[:, 0:nq, :], AXX, ALU.add)
                settle()
                for t in range(NT + 1):
                    drained_wait(dve, f"mkv{g}", t)
                dve.tensor_tensor(flat(msq), flat(k4), flat(k4), ALU.mult)
                settle()
                dve.tensor_reduce(statA[:, 0, nq:nq + nkk], flat(msq), AXX, ALU.add)
                settle()
                dve.tensor_scalar(statA[:, 0, 0:28], statA[:, 0, 0:28], 1.0 / QK, EPS, ALU.mult, ALU.add).then_inc(qvar, 1)
                dve.wait_ge(qroot, 2 + g)
                dve.reciprocal(statA[:, 1, 0:28], statA[:, 1, 0:28])
                settle()
                for v, a, m, which in ((q4, 0, nq, 0), (k4, nq, nkk, 1)):
                    dve.tensor_tensor(flat(v), flat(v), statA[:, 1, a:a + m].unsqueeze(2).broadcast_to([P, m, QK]), ALU.mult)
                    settle()
                    dve.tensor_tensor(flat(v), flat(v), mgain[:, which, :].unsqueeze(1).broadcast_to([P, m, QK]), ALU.mult)
                    settle()
                    for t in range(1, NT):
                        rope(v[:, t, :, NOPE:QK], ropem[:, t - 1, :, :], mrb[:, 0, :, :], mrb[:, 1, :, :], HG, ROPE)
                        settle()
                    dve.drain().then_inc(qk_ready, 1)
                attention(str(g), units_mla, HG,
                          lambda t, g=g: mtok[:, t, g * HG * VD:(g + 1) * HG * VD].rearrange("p (h e) -> p h e", e=VD))
            out_projection(1)
            moe(1)


_OUTS = [(1, NPR, D), (1, NSA, D), (1, 1, NPR, KVH, HD), (1, 1, NPR, KVH, HD), (1, 1, NPR, KVR), (1, 1, NPR, ROPE)]


def kernel(**inputs):
    import concourse.bacc as _bacc
    from concourse.bass_utils import run_bass_kernel_spmd as _run

    nc = _bacc.Bacc("TRN2", target_bir_lowering=False, num_devices=1)
    arrays, dram = {}, {}
    for name, a in list(inputs.items()) + list(shape_constants().items()):
        a = np.ascontiguousarray(a)
        arrays[f"in_{name}_dram"] = a
        dram[name] = nc.dram_tensor(f"in_{name}_dram", a.shape, mybir.dt.from_np(a.dtype), kind="ExternalInput").ap()
    outs = [nc.dram_tensor(f"out_{i}_dram", shape, F32, kind="ExternalOutput").ap() for i, shape in enumerate(_OUTS)]
    build_step(nc, dram, outs)
    r = _run(nc, [arrays], core_ids=[0])
    return tuple(r.results[0][f"out_{i}_dram"] for i in range(len(_OUTS)))
```

```python
import math
from contextlib import ExitStack

import numpy as np

import concourse.bass as bass
from concourse import mybir

F32 = mybir.dt.float32
F32R = mybir.dt.float32r
ALU = mybir.AluOpType
ACT = mybir.ActivationFunctionType
AXX = mybir.AxisListType.X

P = 128
D = 1024
KT = D // P
NPR, NSA, PAST = 128, 256, 128
T = NPR + NSA
NT = T // P
GRP = [0, 1, 1]
EPS = 1e-6
HY = D // 2
NCH = HY // P
HID, EMB = 64, 33
QH, KVH, HD = 8, 2, 64
MH, NOPE, ROPE, VD = 16, 64, 32, 64
QK = NOPE + ROPE
QR, KVR = 256, 128
ODD_IN = QR + KVR + ROPE
HG = 4
NE, DE, NG, EPG = 16, 256, 4, 4
GRID_W = 64
RING = 9
PIECE = 2048
NBLK = (T + NG * (P - 1)) // P

TWO_PI_A = 6.28125
TWO_PI_B = float(np.float32(np.round((2 * math.pi - TWO_PI_A) * 2**20) / 2**20))
TWO_PI_C = float(2 * math.pi - TWO_PI_A - TWO_PI_B)
ROUNDER = 1.5 * 2.0**23
SIN_MAX = 3.1415925

SH1, SC1, G1, SH2, SC2, G2 = range(6)


def halves(*vectors):
    return [(l, v, half) for l, v in vectors for half in range(2)]


CHUNKS = {
    "start": halves((0, SH1), (0, SC1)),
    "gqa": halves((0, G1), (0, SH2), (0, SC2), (1, SH1), (1, SC1)),
    "ffn0": halves((0, G2)),
    "mla": halves((1, G1), (1, SH2), (1, SC2)),
    "ffn1": halves((1, G2)),
}
MODA_ORDER = [(0, 0), (0, 1), (1, 0), (1, 1)]
MLA_NORM_STEPS = 12
MLA_NORM_AT = {1: (0,), 2: (1,), 3: (2,), 4: (3,), 7: (4,), 8: (8,), 9: (9,), 10: (10,), 11: (11,)}
GQA_AHEAD, MLA_AHEAD = 4, 3
GQA_AT = {3 + 3 * (i - GQA_AHEAD): i for i in range(GQA_AHEAD, len(CHUNKS["gqa"]) + 1)}
MLA_AT = {(i - MLA_AHEAD, 3): i for i in range(MLA_AHEAD, len(CHUNKS["mla"]) + 1)}


def order(kind, e):
    return 3 * e + {"A": 0, "B": 1, "C": 5}[kind]


FIRST_PIECES = (("A", 0), ("B", 0), ("A", 1), ("B", 1), ("C", 0))


def shape_constants():
    c = {}
    c["ident"] = np.eye(P)
    c["before"] = np.triu(np.ones((P, P)), 1)
    c["slots"] = np.tile(np.arange(P), (P, 1))
    sel = np.zeros((P, 2, P))
    for g in range(4):
        for r in range(2):
            sel[32 * g + r, r, :] = 1
    c["rowsel"] = sel.reshape(P, 2 * P)
    cs = np.zeros((24, 24, 2))
    for r in range(24):
        cs[r, r, :] = 1
    c["chunksel"] = cs.reshape(24, 48)

    def odd_dft(n):
        j = np.arange(n)[:, None]
        f = np.arange(n)[None, :]
        a = np.pi * ((2 * f + 1) * j % (4 * n)) / (2 * n)
        return np.cos(a), np.sin(a)

    cp, sp = odd_dft(NPR)
    cs_, ss = odd_dft(NSA)
    c["dft_p"] = np.stack([cp, sp, cp.T / NPR, sp.T / NPR], 1).reshape(P, 4 * NPR)
    two = [m.reshape(2, P, NSA).transpose(1, 0, 2) for m in (cs_, ss, cs_.T / NSA, ss.T / NSA)]
    c["dft_s"] = np.stack(two, 1).reshape(P, 8 * NSA)

    zs, ds = [], []
    lo, hi = math.log(1e-2) / 1.5, math.log(1e-2) / 0.3
    deltas = np.abs(np.linspace(lo, hi, HY))
    for n in (NPR, NSA):
        t01 = np.linspace(0.0, 1.0, n)
        w = (2 * math.pi / n) * np.arange(n)
        bands = np.linspace(1e-4, (EMB - 1) // 2 - 1, (EMB - 1) // 2)
        zs.append(np.concatenate([t01[:, None], np.cos(w[:, None] * bands), -np.sin(w[:, None] * bands)], 1))
        ds.append(np.exp(-t01[:, None] * deltas))
    c["zT"] = np.concatenate(zs, 0).T
    c["decay"] = np.concatenate(ds, 0).reshape(NT, P, HY).transpose(1, 0, 2).reshape(P, NT * HY)

    def rope(width):
        half, npair = width // 2, width // 4
        fr = 10000.0 ** (-np.arange(npair) / npair)
        t = np.arange(NSA)
        co, si = [], []
        for pos in (t // GRID_W, t % GRID_W):
            a = pos[:, None] * fr[None, :]
            co += [np.cos(a), np.cos(a)]
            si += [-np.sin(a), np.sin(a)]
        both = np.stack([np.concatenate(co, 1), np.concatenate(si, 1)], 1)
        return both.reshape(2, P, 2, width).transpose(1, 0, 2, 3).reshape(P, 4 * width)

    c["rope_q"] = rope(HD)
    c["rope_m"] = rope(ROPE)
    return {k: np.ascontiguousarray(v, np.float32) for k, v in c.items()}


class Banks:

    def __init__(self):
        self.uses = [0] * 8
        self.turn = 0
        self.jobs = {}

    def stage(self, name, count, banks=None):
        out = []
        for i in range(count):
            if banks is None:
                b = self.turn
                self.turn = (self.turn + 1) % 8
            else:
                b = banks[i % len(banks)]
            out.append((b, self.uses[b]))
            self.uses[b] += 1
        self.jobs[name] = out

    def __getitem__(self, key):
        return self.jobs[key[0]][key[1]]


def build_step(nc, d, o):
    y_prompt, y_sample, st_k, st_v, st_ckv, st_kr = o
    units_gqa = [(t, h) for t in range(NT) for h in range(QH)]
    units_mla = [(t, h) for t in range(NT) for h in range(HG)]
    NHG = MH // HG

    B = Banks()
    BANK_S, BANK_PT, BANK_O, BANK_M = [0, 1], [2, 3], [4, 5], [6, 7]
    SCATTER_BANKS = (4, 6, 7, 0, 1, 2)

    def mod_stage(where, i, banks=None):
        chunks = CHUNKS[where]
        if i < len(chunks):
            l, v, half = chunks[i]
            B.stage(f"mod{l}.{v}.{half}", 1, banks and [banks[i % 2]])
        if 1 <= i <= len(chunks):
            l, v, half = chunks[i - 1]
            turn = banks and [banks[(i - 1) % 2], banks[i % 2]]
            B.stage(f"modsel{l}.{v}.{half}", 2 if v in (G1, G2) else 1, turn)

    def moe_stage(l):
        B.stage(f"hT{l}.1", 6)
        B.stage(f"routerT{l}", 1)
        B.stage(f"router{l}", 1)
        B.stage(f"htok{l}", 6)
        for i in range(len(CHUNKS[f"ffn{l}"]) + 1):
            mod_stage(f"ffn{l}", i)
        B.stage(f"rank{l}", 1)
        B.jobs[f"moe{l}"] = list(B.uses)

    B.stage("filt1", 1)
    mod_stage("start", 0)
    B.stage("filt2", 1)
    mod_stage("start", 1)
    for od in range(2):
        B.stage(f"filt3.{od}", 2 * NT)
        if od == 0:
            mod_stage("start", 2)
        else:
            B.stage("hT0.0", 6)
        B.stage(f"energy{od}", 2)
        if od == 0:
            mod_stage("start", 3)
        if od == 0:
            B.stage(f"spec{od}", 2 * NT)
            mod_stage("start", 4)
            B.stage("convT", 1)
    B.stage("qkv", 2 * NT)
    B.stage("spec1", 2 * NT)
    B.stage("qkv2", NT)
    B.stage("uT", 3 * NCH)
    B.stage("vtok", NT)
    B.stage("x1tok", NT)
    for i, (stage, count) in enumerate((("fwd0", 2 * NT), ("inv0", NT), ("fwd1", 2 * NT), ("inv1", NCH))):
        B.stage(stage, count)
        mod_stage("gqa", i, BANK_M)
    B.stage("qT", NT * KVH)
    B.stage("kT", KVH)
    B.stage("gS", len(units_gqa), BANK_S)
    B.stage("gPT", len(units_gqa), BANK_PT)
    B.stage("gO", NT, BANK_O)
    for i in GQA_AT.values():
        mod_stage("gqa", i, BANK_M)
    B.stage("goT", NT)
    B.stage("out0", 2 * NT)
    moe_stage(0)
    B.stage("hT1.0", 6)
    B.stage("um", NT)
    B.stage("cT", NT + 1)
    B.stage("mq0", NT)
    B.stage("mk0", NT + 1)
    for i in range(MLA_AHEAD):
        mod_stage("mla", i, BANK_M)
    for g in range(NHG):
        B.stage(f"mv{g}", NT + 1)
        B.stage(f"mqT{g}", NT)
        B.stage(f"mkT{g}", NT + 1)
        if g + 1 < NHG:
            B.stage(f"mq{g + 1}", NT)
            B.stage(f"mk{g + 1}", NT + 1)
        B.stage(f"mS{g}", len(units_mla), BANK_S)
        B.stage(f"mPT{g}", len(units_mla), BANK_PT)
        B.stage(f"mO{g}", NT, BANK_O)
        for (group, _), i in MLA_AT.items():
            if group == g:
                mod_stage("mla", i, BANK_M)
    B.stage("moT", 2 * NT)
    B.stage("out1", 2 * NT)
    moe_stage(1)

    pieces, at = [], {}

    def piece(name, src, *shape):
        at[name] = len([q for q in pieces if q is not None])
        pieces.append((src, shape))

    def mod_pieces(where):
        for l, v, half in CHUNKS[where]:
            c0 = v * D + half * 512
            for kh in range(2):
                w = d["w_mod"][l].rearrange("(p j) n -> p j n", j=KT)
                piece(f"mod{l}.{v}.{half}.{kh}", w[:, 4 * kh:4 * kh + 4, c0:c0 + 512], 4, 512)

    def out_pieces(l, w):
        w = w.rearrange("(j p) n -> p j n", p=P)
        for half in range(2):
            for kh in range(2):
                piece(f"out{l}.{half}.{kh}", w[:, 4 * kh:4 * kh + 4, half * 512:half * 512 + 512], 4, 512)

    def moe_pieces(l):
        mod_pieces(f"ffn{l}")
        pieces.append(None)
        at[f"moe{l}"] = len([q for q in pieces if q is not None])

    mod_pieces("start")
    ev_in = d["ev_w_in"][0].rearrange("(p j) n -> p j n", j=KT)
    for q in (6, 7, 8, 0, 1, 2, 3, 4, 5):
        piece(f"in0.{q}", ev_in[:, :, 256 * q:256 * q + 256], KT, 256)
    mod_pieces("gqa")
    out_pieces(0, d["ev_w_out"][0])
    moe_pieces(0)
    od_in = d["od_w_in"][0].rearrange("(p j) n -> p j n", j=KT)
    for kh in range(2):
        piece(f"in1.{kh}", od_in[:, 4 * kh:4 * kh + 4, :], 4, ODD_IN)
    mod_pieces("mla")
    out_pieces(1, d["od_w_out"][0])
    moe_pieces(1)

    with ExitStack() as ctx:
        def sb(name, *shape):
            return ctx.enter_context(nc.sbuf_tensor(name, list(shape), F32))

        def sem(name):
            return ctx.enter_context(nc.semaphore(name))

        x = sb("x", P, NT, D)
        hT = sb("hT", P, KT, T)
        xn = sb("xn", P, NT, D)
        gb = sb("gb", P, 2, D)
        modrow = sb("modrow", P, 512)
        ident = sb("ident", P, P)
        rowsel = sb("rowsel", P, 2, P)
        chunksel = sb("chunksel", 24, 24, 2)
        bmod = sb("bmod", 24, 512)
        zero2 = sb("zero2", 24, 2)
        condraw = sb("condraw", P, 2, KT)
        condT = sb("condT", P, KT, 32)
        modT = sb("modT", P, 2, 6, KT, 2)
        modA = sb("modA", P, 2, 2, KT, 2)
        gain = sb("gain", P, 2, 2, KT)
        routw = sb("routw", P, KT, NE)
        routb = sb("routb", P, NE)
        rank_e = sb("rank_e", P, NE)
        ssq = sb("ssq", P, 4, NT)
        gates = sb("gates", P, NT, NE)
        meta = ctx.enter_context(nc.sbuf_tensor("meta", [1, 2, 8], mybir.dt.int32))
        statA = sb("statA", P, 2, 40)
        negmax = sb("negmax", P, len(units_gqa))
        psumexp = sb("psumexp", P, len(units_gqa))
        rinv = sb("rinv", P, QH)
        ropeq = sb("ropeq", P, 2, 2, HD)
        qkgain = sb("qkgain", P, 2, HD)
        ck = sb("ck", P, KVH * HD)
        cv = sb("cv", P, KVH * HD)
        filtc = sb("filtc", HID, 3 + 2 * HID)
        convT = sb("convT", P, 4, 3 * NCH)

        with ExitStack() as mixer:
            ring = mixer.enter_context(nc.sbuf_tensor("ring", [P, RING * PIECE], F32))
            arena = mixer.enter_context(nc.sbuf_tensor("arena", [P, 20224], F32))
        lows = ctx.enter_context(nc.sbuf_tensor("lows", [P, RING * PIECE], F32R))
        parts = ctx.enter_context(nc.sbuf_tensor("parts", [P, 17792], F32R))
        scratch_e = sb("scratch_e", P, 2432)

        hTs = parts[:, 12288:14336].rearrange("p (h k n) -> p h k n", h=2, n=P)
        midT = parts[:, 14336:15360].rearrange("p (b h f n) -> p b h f n", b=2, h=2, n=P)
        ysb = parts[:, 15360:17408].rearrange("p (h n) -> p h n", h=2)
        permT = parts[:, 17408:17792].rearrange("p (t n) -> p t n", n=P)
        before, slots, onesr = (scratch_e[:, P * i:P * (i + 1)] for i in range(3))
        plan = scratch_e[:, 384:512]
        perm = scratch_e[:, 512:896].rearrange("p (t n) -> p t n", n=P)
        sil = scratch_e[:, 896:1408].rearrange("p (b n) -> p b n", n=DE)
        mid = scratch_e[:, 1408:1920].rearrange("p (b n) -> p b n", n=DE)
        sml = scratch_e[:, 896:1472].rearrange("p (a b) -> p a b", b=72)

        def view(off, *shape, parts=P):
            n = int(np.prod(shape))
            v = arena[0:parts, off:off + n]
            if len(shape) == 2:
                return v.rearrange("p (a b) -> p a b", b=shape[1])
            if len(shape) == 3:
                return v.rearrange("p (a b c) -> p a b c", b=shape[1], c=shape[2])
            if len(shape) == 4:
                return v.rearrange("p (a b c e) -> p a b c e", b=shape[1], c=shape[2], e=shape[3])
            return v

        H = view(0, 2, 2, NT, HY)
        uc = view(6144, 3 * NCH, T)
        dftp = view(10752, 4, NPR)
        dfts = view(11264, 4, 2, NSA)
        uT = view(13312, 3 * NCH, T)
        qkv = view(17920, NT, QH * HD + 2 * KVH * HD)
        filt = view(6144, NT, 2, HY)
        decay = view(9216, NT, HY)
        w3 = view(13312, 4, HY, parts=HID + 1)
        convraw = view(15360, P, parts=48)
        esc = view(15488, 2, HY)
        hidden = view(16512, T, parts=HID + 1)
        turns = view(16896, T, parts=HID)
        zT = view(17280, T, parts=EMB)
        sqs = view(17152, 2, 2, HY)
        sqd = view(19200, HY)
        onesm = view(19712, P)
        modbias = view(19840, 2, 6, KT)
        Y = view(13312, NT, 2, HY)
        tmpa = view(16384, HY)
        tmpb = view(16896, HY)
        hybias = gb[:, :, 0:HY]
        vtok = xn[:, :, 0:HY]
        x1tok = xn[:, :, HY:D]
        qT = view(0, NT, QH, P, parts=HD)
        kT = view(3072, KVH, 4, P, parts=HD)
        probs = view(4096, 2, T)
        probsT = view(4864, 2, 3, P)
        scratch = gb[:, :, :].rearrange("p a b -> p (a b)")
        qsq = scratch[:, 0:(QH + KVH) * HD].rearrange("p (h e) -> p h e", e=HD)
        qrb = scratch[:, 640:640 + (QH + KVH) * HD].rearrange("p (h e) -> p h e", e=HD)
        otok = xn[:, :, 0:HY]
        um = view(0, NT, ODD_IN)
        cT = view(1248, 3, T)
        cvT = view(2400, P)
        ckv_c = view(14100, KVR)
        kr_c = view(14228, ROPE)
        lgain = view(2528, QR + KVR)
        mgain = view(2912, 2, QK)
        ropem = view(14260, 2, 2, ROPE)
        w_q = view(14388, 2, MH * QK)
        w_kv = view(17460, MH * (NOPE + VD))
        flat_hT = hT[:, :, :].rearrange("p a b -> p (a b)")
        in_heads = lambda a: a.rearrange("p (t h e) -> p t h e", h=HG, e=QK)
        q4s = [view(3392, NT, HG, QK), in_heads(flat_hT[:, 0:NT * HG * QK])]
        k4s = [view(4544, NT + 1, HG, QK), in_heads(flat_hT[:, NT * HG * QK:(2 * NT + 1) * HG * QK])]
        v4 = view(6080, NT + 1, HG, VD)
        q4T = view(7104, NT, HG, P, parts=QK)
        k4T = view(8640, HG, NT + 1, P, parts=QK)
        mprobs = view(10688, 2, T)
        mprobsT = view(11456, 2, 3, P)
        msq = view(12224, NT + 1, HG, QK)
        mrb = view(13760, 2, HG, ROPE)
        mtok = xn
        junk = view(12300, NT, QR + KVR)
        htok = xn
        gtmp = hT[:, :, :].rearrange("p a b -> p (a b)").rearrange("p (a b) -> p a b", b=512)

        other_row = {"start": hT[:, :, :].rearrange("p a b -> p (a b)")[:, 0:512], "gqa": view(6144, 512),
                     "ffn0": view(6144, 512), "mla": view(19508, 512), "ffn1": view(6144, 512)}

        def modrow_of(where, i):
            return modrow[:, :] if i % 2 == 0 else other_row[where]

        ps = [ctx.enter_context(nc.psum_tensor(f"ps{b}", [P, 512], F32)) for b in range(8)]
        filled = [sem(f"filled{b}") for b in range(8)]
        drained = [sem(f"drained{b}") for b in range(8)]
        piece_full = [sem(f"piece_full{s}") for s in range(RING)]
        piece_used = sem("piece_used")
        ring_free = sem("ring_free")
        in_cond, in_x, in_mod, in_filt, in_filt3, in_dft, in_conv, in_attn, in_mla, in_mla_w = (
            sem(n) for n in ("in_cond", "in_x", "in_mod", "in_filt", "in_filt3", "in_dft", "in_conv", "in_attn", "in_mla", "in_mla_w"))
        cond_zero, cond_ready = sem("cond_zero"), sem("cond_ready")
        ones_set = sem("ones_set")
        modrow_used = sem("modrow_used")
        moda_ready = sem("moda_ready")
        squares = sem("squares")
        meansq = sem("meansq")
        rootsq = sem("rootsq")
        xn_ready = sem("xn_ready")
        sin_arg, sin_done = sem("sin_arg"), sem("sin_done")
        esq_ready, eroot, escale_ready = sem("esq_ready"), sem("eroot"), sem("escale_ready")
        sum_ready, esq_used = sem("sum_ready"), sem("esq_used")
        spec_done = sem("spec_done")
        conv_copied, conv_done = sem("conv_copied"), sem("conv_done")
        y_ready = sem("y_ready")
        qsq_ready, qvar, qroot, qk_ready = sem("qsq_ready"), sem("qvar"), sem("qroot"), sem("qk_ready")
        negmax_ready = sem("negmax_ready")
        inv_root, qk_turned = sem("inv_root"), sem("qk_turned")
        pv_done = sem("pv_done")
        x_mixed = sem("x_mixed")
        x_done = sem("x_done")
        score_ready = sem("score_ready")
        gates_ready = sem("gates_ready")
        in_route = sem("in_route")
        per_layer = lambda name: [sem(f"{name}{l}") for l in range(2)]
        plan_sums, plan_ready, perm_ready = per_layer("plan_sums"), per_layer("plan_ready"), per_layer("perm_ready")
        gather_full, hts_ready, aux_read = per_layer("gather_full"), per_layer("hts_ready"), per_layer("aux_read")
        gu_full, silu_ready, mid_ready = per_layer("gu_full"), per_layer("silu_ready"), per_layer("mid_ready")
        mt_full, mt_read, y_full, y_read = per_layer("mt_full"), per_layer("mt_read"), per_layer("y_full"), per_layer("y_read")
        scatter_full, scatter_read = per_layer("scatter_full"), per_layer("scatter_read")
        hi_ready, split_ready, parts_used = per_layer("hi_ready"), per_layer("split_ready"), per_layer("parts_used")
        hts_hi, mt_hi, y_hi, x_added = per_layer("hts_hi"), per_layer("mt_hi"), per_layer("y_hi"), per_layer("x_added")
        loaded_w = [{k + str(j): sem(f"w{k}{j}_{l}") for k in "ABC" for j in range(2)} for l in range(2)]
        lora_sq, lora_var, lora_root, lora_ready = sem("lora_sq"), sem("lora_var"), sem("lora_root"), sem("lora_ready")
        stored = sem("stored")

        def raw(kind, e):
            s = "ABC".index(kind) + 3 * (e % 2)
            return ring[:, s * PIECE:(s + 1) * PIECE]

        def low_of(kind, e):
            s = "ABC".index(kind) + 3 * (e % 2)
            return lows[:, s * PIECE:(s + 1) * PIECE]

        def high_of(kind, e):
            s = "ABC".index(kind) + 3 * (e % 2)
            return parts[:, s * PIECE:(s + 1) * PIECE]

        def blocks_of(eng, l):
            eng.wait_ge(plan_ready[l], 1)
            return eng.value_load(meta[0:1, l, 0:1], min_val=1, max_val=NBLK)

        def ring_view(i, shape):
            s = (i % RING) * PIECE
            n = shape[0] * shape[1]
            return ring[:, s:s + n].rearrange("p (a b) -> p a b", b=shape[1])

        def filled_wait(eng, stage, i=0):
            b, n = B[stage, i]
            eng.wait_ge(filled[b], n + 1)
            return ps[b]

        def drained_wait(eng, stage, i=0):
            b, n = B[stage, i]
            eng.wait_ge(drained[b], n + 1)

        def drain_inc(ins, stage, i=0):
            ins.then_inc(drained[B[stage, i][0]], 1)

        def rope(eng, v, tbl, ra, rb, heads, width):
            c = width // 4
            split = lambda a: a.rearrange("p h (x y z) -> p h x y z", x=2, y=2)
            cos = tbl[:, 0, :].unsqueeze(1).broadcast_to([P, heads, width])
            sin = tbl[:, 1, :].rearrange("p (x y z) -> p x y z", x=2, y=2)
            eng.tensor_tensor(ra, v, cos, ALU.mult)
            for part in range(2):
                s = sin[:, :, part, :].unsqueeze(1).broadcast_to([P, heads, 2, c])
                eng.tensor_tensor(split(rb)[:, :, :, part, :], split(v)[:, :, :, 1 - part, :], s, ALU.mult)
            eng.drain()
            return eng.tensor_tensor(v, ra, rb, ALU.add)

        def mla_turn(eng, g, step, scr):
            nq, nkk = NT * HG, (NT + 1) * HG
            flat = lambda a: a.rearrange("p t h e -> p (t h) e")
            which, part = divmod(step - 4, 4)
            v, a, m = ((q4s[g % 2], 0, nq), (k4s[g % 2], nq, nkk))[which]
            if part == 0:
                return eng.tensor_tensor(flat(v), flat(v), statA[:, 1, a:a + m].unsqueeze(2).broadcast_to([P, m, QK]), ALU.mult)
            if part == 1:
                return eng.tensor_tensor(flat(v), flat(v), mgain[:, which, :].unsqueeze(1).broadcast_to([P, m, QK]), ALU.mult)
            t = part - 1
            return rope(eng, v[:, t, :, NOPE:QK], ropem[:, t - 1, :, :], scr[0], scr[1], HG, ROPE)

        consts_loaded = {}

        def load(eng, s, dst, src):
            eng.dma_start(dst, src).then_inc(s, 16)
            consts_loaded[s.name] = consts_loaded.get(s.name, 0) + 16

        LOADS = {"in_cond": 2, "in_x": 2, "in_mod": 11, "in_filt": 6, "in_filt3": 5, "in_mla_w": 3, "in_dft": 2, "in_conv": 2, "in_attn": 6, "in_mla": 7}

        def loaded(eng, s):
            eng.wait_ge(s, 16 * LOADS[s.name])

        block = ctx.enter_context(nc.Block())

        @block.sync
        def _(sp):
            def send(i, src, shape, wait):
                if wait is not None:
                    sp.wait_ge(piece_used, wait)
                sp.dma_start(ring_view(i, shape), src).then_inc(piece_full[i % RING], 16)

            def send_experts(l):
                def send_piece(kind, e, g, count):
                    expert = g * EPG + e % EPG
                    sp.wait_ge(parts_used[l], count)
                    dst, s = raw(kind, e), loaded_w[l][kind + str(e % 2)]
                    if kind == "C":
                        src = d["moe_w_down"][l][bass.ds(expert, 1), :, :].rearrange("e (j p) n -> p (e j) n", p=P)
                        sp.dma_start(dst.rearrange("p (j n) -> p j n", n=D), src).then_inc(s, 16)
                        return
                    k0 = 0 if kind == "A" else 4
                    for w, which in enumerate(("moe_w_gate", "moe_w_up")):
                        src = d[which][l][bass.ds(expert, 1), :, :].rearrange("e (p j) n -> p (e j) n", j=KT)[:, k0:k0 + 4, :]
                        sp.dma_start(dst.rearrange("p (w j n) -> p w j n", w=2, n=DE)[:, w, :, :], src).then_inc(s, 16)

                nb = blocks_of(sp, l)
                g = sp.value_load(meta[0:1, l, 1:2], min_val=0, max_val=NG - 1)
                for kind, e in FIRST_PIECES:
                    send_piece(kind, e, g, 1)
                with sp.Fori(0, nb) as b:
                    own = sp.value_load(meta[0:1, l, bass.ds(b + 1, 1)], min_val=0, max_val=NG - 1)
                    after = sp.value_load(meta[0:1, l, bass.ds(b + 2, 1)], min_val=0, max_val=NG - 1)
                    for e in range(1, EPG + 1):
                        send_piece("A", e + 1, own if e + 1 < EPG else after, b * 12 + (1 + max(3 * e - 3, 1)))
                        send_piece("B", e + 1, own if e + 1 < EPG else after, b * 12 + (1 + max(3 * e - 2, 2)))
                        send_piece("C", e, own if e < EPG else after, b * 12 + (1 + (3 * e - 1 if e > 1 else 1)))
                return nb

            i, l = 0, 0
            for entry in pieces:
                if entry is None:
                    send_experts(l)
                    l += 1
                    continue
                if l == 1 and i == at["moe0"]:
                    sp.wait_ge(ring_free, 1)
                if l == 1 and i == at["moe0"] + 2:
                    for j in range(2):
                        load(sp, in_mla_w, w_q[:, j, :], d["od_w_uq"][0, j * P:(j + 1) * P, :])
                    load(sp, in_mla_w, w_kv, d["od_w_ukv"][0])
                if i == 0:
                    load(sp, in_filt3, w3[0:HID, :, :], d["ev_filt_w3"][0].rearrange("k (a b) -> k a b", b=HY))
                    load(sp, in_filt3, w3[HID:HID + 1, :, :], d["ev_filt_b3"].rearrange("k (a b) -> k a b", b=HY))
                if i == 1:
                    loaded(sp, in_filt)
                    loaded(sp, in_mod)
                if i == 2:
                    load(sp, in_filt3, decay, d["decay"].rearrange("p (a b) -> p a b", b=HY))
                    load(sp, in_filt3, hybias[:, 0, :], d["ev_hy_bias"][0, 0].partition_broadcast(P))
                    load(sp, in_filt3, hybias[:, 1, :], d["ev_hy_bias"][0, 1].partition_broadcast(P))
                if i == 4:
                    load(sp, in_x, x[:, 0, :], d["x_prompt"][0])
                    load(sp, in_x, x[:, 1:NT, :], d["x_sample"][0].rearrange("(t p) n -> p t n", p=P))
                if l == 1 and i - at["moe0"] < RING:
                    send(i, *entry, None)
                else:
                    send(i, *entry, i - RING + 1 if i >= RING else None)
                i += 1

        @block.gpsimd
        def _(pool):
            pool.memset(condT[:, :, :], 0.0).then_inc(cond_zero, 1)
            load(pool, in_dft, dftp, d["dft_p"].rearrange("p (a b) -> p a b", b=NPR))
            load(pool, in_dft, dfts, d["dft_s"].rearrange("p (a b c) -> p a b c", b=2, c=NSA))
            load(pool, in_attn, ropeq[:, :, :, :], d["rope_q"].rearrange("p (a b c) -> p a b c", b=2, c=HD))
            load(pool, in_attn, qkgain[:, 0, :], d["ev_q_norm"][0].partition_broadcast(P))
            load(pool, in_attn, qkgain[:, 1, :], d["ev_k_norm"][0].partition_broadcast(P))
            load(pool, in_attn, ck[:, :], d["cache_gqa_k"][0, 0].rearrange("t h e -> t (h e)"))
            load(pool, in_attn, cv[:, :], d["cache_gqa_v"][0, 0].rearrange("t h e -> t (h e)"))
            load(pool, in_attn, routb[:, :], d["router_bias"].partition_broadcast(P))
            pool.wait_ge(qk_ready, 1)
            pool.dma_start(st_k[0, 0].rearrange("t h e -> t (h e)"), qkv[:, 0, QH * HD:QH * HD + KVH * HD]).then_inc(stored, 16)
            pool.dma_start(st_v[0, 0].rearrange("t h e -> t (h e)"), qkv[:, 0, QH * HD + KVH * HD:]).then_inc(stored, 16)
            for l in range(2):
                for i in range(6):
                    drained_wait(pool, f"hT{l}.1", i)
                load(pool, in_route, before, d["before"])
                load(pool, in_route, slots, d["slots"])
                nb = blocks_of(pool, l)
                pool.drain().then_inc(x_added[l], 1)
                with pool.Fori(0, nb) as b:
                    for t in range(NT):
                        pool.wait_ge(scatter_read[l], b * 6 + (2 * t + 8))
                        ins = pool.tensor_tensor(x[:, t, :], x[:, t, :], gtmp[:, 2 * t:2 * t + 2, :].rearrange("p a b -> p (a b)"), ALU.add)
                    ins.then_inc(x_added[l], 1)
                pool.wait_ge(x_added[l], nb + 1)
                pool.tensor_tensor(gtmp[:, 0, 0:1], gtmp[:, 1, 0:1], gtmp[:, 1, 0:1], ALU.add).then_inc(x_done, 1)
                if l == 1:
                    break
                load(pool, in_mla, ckv_c, d["cache_mla_ckv"][0, 0])
                load(pool, in_mla, kr_c, d["cache_mla_krope"][0, 0])
                load(pool, in_mla, lgain[:, 0:QR], d["od_q_lora_norm"][0].partition_broadcast(P))
                load(pool, in_mla, lgain[:, QR:QR + KVR], d["od_kv_lora_norm"][0].partition_broadcast(P))
                load(pool, in_mla, mgain[:, 0, :], d["od_q_norm"][0].partition_broadcast(P))
                load(pool, in_mla, mgain[:, 1, :], d["od_k_norm"][0].partition_broadcast(P))
                load(pool, in_mla, ropem, d["rope_m"].rearrange("p (a b c) -> p a b c", b=2, c=ROPE))
                pool.wait_ge(lora_ready, 1)
                pool.dma_start(st_ckv[0, 0], um[:, 0, QR:QR + KVR]).then_inc(stored, 16)
                pool.dma_start(st_kr[0, 0], um[:, 0, QR + KVR:]).then_inc(stored, 16)
                for g in range(NHG):
                    pool.wait_ge(inv_root, g + 1)
                    for step in range(4, 8):
                        mla_turn(pool, g, step, (msq[:, 0, :, 0:ROPE], msq[:, 1, :, 0:ROPE]))
                        if step == 7:
                            pool.drain().then_inc(qk_turned, 1)
                        else:
                            pool.drain()
            pool.wait_ge(x_done, 2)
            pool.dma_start(y_prompt[0], x[:, 0, :]).then_inc(stored, 16)
            pool.dma_start(y_sample[0].rearrange("(t p) n -> p t n", p=P), x[:, 1:NT, :]).then_inc(stored, 16)
            pool.wait_ge(stored, 16 * 6)

        @block.tensor
        def _(pe):
            def claim(stage, i=0):
                b, n = B[stage, i]
                if n:
                    pe.wait_ge(drained[b], n)
                return ps[b]

            def fill_inc(ins, stage, i=0):
                ins.then_inc(filled[B[stage, i][0]], 1)

            def weights(name, shape):
                i = at[name]
                pe.wait_ge(piece_full[i % RING], 16 * (i // RING + 1))
                return ring_view(i, shape)

            due = [0, piece_used]

            def piece_end(count=1):
                due[0] += count

            def product(out, lhsT, rhs, **kw):
                mm = pe.matmul(out, lhsT, rhs, **kw)
                if due[0]:
                    mm.then_inc(due[1], due[0])
                    due[:] = [0, piece_used]
                return mm

            def turn(out, src):
                mm = pe.transpose(out, src, ident[:, :])
                if due[0]:
                    mm.then_inc(due[1], due[0])
                    due[:] = [0, piece_used]
                return mm

            def mod_step(where, i):
                chunks = CHUNKS[where]
                if i < len(chunks):
                    l, v, half = chunks[i]
                    name = f"mod{l}.{v}.{half}"
                    bank = claim(name)
                    if where == "start" and i == 0:
                        pe.wait_ge(ones_set, 1)
                        loaded(pe, in_mod)
                        pe.wait_ge(cond_ready, 2)
                    for kh in range(2):
                        w = weights(f"{name}.{kh}", (4, 512))
                        for g in range(4):
                            mm = product(bank[32 * g:32 * g + 32, :], condT[:, 4 * kh + g, :], w[:, g, :],
                                         start=kh == 0, stop=kh == 1 and g > 0)
                        if kh == 0:
                            mm.then_inc(piece_used, 1)
                    mm.then_inc(piece_used, 1)
                    n = 512 if v in (G1, G2) else 2
                    bias = (chunksel[:, l * 12 + 2 * v + half, :], bmod[:, :]) if n > 2 else (zero2[:, :], zero2[:, :])
                    fill_inc(product(bank[0:2, 0:n], *bias, start=False, stop=True), name)
                if 1 <= i <= len(chunks):
                    l, v, half = chunks[i - 1]
                    row = modrow_of(where, i - 1)
                    drained_wait(pe, f"mod{l}.{v}.{half}")
                    sel = f"modsel{l}.{v}.{half}"
                    if v in (G1, G2):
                        for c in range(2):
                            bank = claim(sel, c)
                            for n0 in (0, 256):
                                mm = product(bank[:, n0:n0 + 256], rowsel[:, c, :], row[:, n0:n0 + 256], start=True, stop=True)
                            fill_inc(mm, sel, c)
                    else:
                        bank = claim(sel)
                        for j in range(KT):
                            mm = product(bank[64 * half:64 * half + 64, 2 * j:2 * j + 2], row[:, j::KT], rowsel[:, :, 0], start=True, stop=True)
                        fill_inc(mm, sel)

            def norm_transposes(l, which):
                stage = f"hT{l}.{which}"
                for t in range(NT):
                    pe.wait_ge(xn_ready, (2 * l + which) * NT + t + 1)
                    for q in range(2):
                        bank = claim(stage, 2 * t + q)
                        for j in range(4):
                            mm = turn(bank[:, j * P:(j + 1) * P], xn[:, t, 4 * q + j::KT])
                        fill_inc(mm, stage, 2 * t + q)

            def out_projection(l):
                for half in range(2):
                    for i in range(NT):
                        claim(f"out{l}", half * NT + i)
                    for kh in range(2):
                        w = weights(f"out{l}.{half}.{kh}", (4, 512))
                        for t in range(NT):
                            bank = ps[B[f"out{l}", half * NT + t][0]]
                            for k in range(4):
                                mm = product(bank[:, :], hT[:, 4 * kh + k, t * P:(t + 1) * P], w[:, k, :],
                                               start=kh == 0 and k == 0, stop=kh == 1 and k == 3)
                            if kh == 1:
                                fill_inc(mm, f"out{l}", half * NT + t)
                        if kh == 0:
                            mm.then_inc(piece_used, 1)
                    piece_end()

            def attention(tag, units, heads_n, lhs_q, rhs_k, v_of):
                n = len(units)
                pT = probsT if tag == "g" else mprobsT
                pr = probs if tag == "g" else mprobs
                S, PT, O = f"{tag}S", f"{tag}PT", f"{tag}O"
                if tag != "g":
                    S, PT, O = f"mS{tag}", f"mPT{tag}", f"mO{tag}"
                for i in range(n + 3):
                    if 2 <= i <= n + 1:
                        j = i - 2
                        t, h = units[j]
                        bank = claim(PT, j)
                        drained_wait(pe, S, j)
                        for kt in range(1 if t == 0 else NT):
                            mm = turn(bank[:, kt * P:(kt + 1) * P], pr[:, j % 2, kt * P:(kt + 1) * P])
                        fill_inc(mm, PT, j)
                    if i < n:
                        t, h = units[i]
                        nk = P if t == 0 else T
                        bank = claim(S, i)
                        mm = product(bank[:, 0:nk], lhs_q(t, h), rhs_k(t, h), start=True, stop=True)
                        fill_inc(mm, S, i)
                    if i >= 3:
                        j = i - 3
                        t, h = units[j]
                        drained_wait(pe, PT, j)
                        if h == 0:
                            claim(O, t)
                        bank = ps[B[O, t][0]]
                        vs = v_of(t, h)
                        for kt, v in enumerate(vs):
                            mm = product(bank[:, h * HD:(h + 1) * HD], pT[:, j % 2, kt, :], v,
                                           start=kt == 0, stop=kt == len(vs) - 1)
                        if h == heads_n - 1:
                            fill_inc(mm, O, t)
                        else:
                            mm.then_inc(pv_done, 1)
                    if tag == "g" and i in GQA_AT:
                        mod_step("gqa", GQA_AT[i])
                    if tag != "g" and (int(tag), i) in MLA_AT:
                        mod_step("mla", MLA_AT[int(tag), i])

            def experts(l):
                nb = blocks_of(pe, l)
                for b, n in enumerate(B.jobs[f"moe{l}"]):
                    pe.wait_ge(drained[b], n)
                for i in range(6):
                    drained_wait(pe, f"htok{l}", i)

                def gather_tables(b1):
                    pe.wait_ge(perm_ready[l], b1)
                    for t in range(NT):
                        turn(ps[5][:, t * P:(t + 1) * P], perm[:, t, :])
                    for t in range(NT):
                        mm = product(ps[5][:, T:T + EPG], perm[:, t, :], plan[:, 64 + 4 * t:68 + 4 * t], start=t == 0, stop=t == 2)
                    mm.then_inc(gather_full[l], 1)

                def gather(half):
                    for q in range(4):
                        k = 4 * half + q
                        for t in range(NT):
                            mm = product(ps[6 + half][:, q * P:(q + 1) * P], htok[:, t, k * P:(k + 1) * P], perm[:, t, :],
                                         start=t == 0, stop=t == 2)
                    mm.then_inc(gather_full[l], 1)

                def both(out, x, w, start, stop):
                    product(out, x[0], w[0], start=start, stop=False)
                    product(out, x[0], w[1], start=False, stop=False)
                    return product(out, x[1], w[0], start=False, stop=stop)

                def split_piece(b, kind, e):
                    pe.wait_ge(split_ready[l], order(kind, e) + 1 if b is None else b * 12 + order(kind, e))
                    return high_of(kind, e), low_of(kind, e)

                def gate_up(b, e, kind):
                    bank = ps[2 + e % 2]
                    if b is not None and kind == "A":
                        pe.wait_ge(mid_ready[l], b * EPG + e)
                    w = [a.rearrange("p (w k n) -> p w k n", w=2, n=DE) for a in split_piece(b, kind, e)]
                    for q in range(4):
                        k = q if kind == "A" else 4 + q
                        mm = both(bank[:, :], (hTs[:, 0, k, :], hTs[:, 1, k, :]), (w[0][:, :, q, :], w[1][:, :, q, :]), k == 0, k == KT - 1)
                    if kind == "A":
                        mm.then_inc(parts_used[l], 1)
                    else:
                        mm.then_inc(gu_full[l], 1)
                        due[:] = [1, parts_used[l]]

                def turn_mid(b, e):
                    pe.wait_ge(mid_ready[l], b * EPG + (e + 2))
                    if e == 0:
                        pe.wait_ge(scatter_read[l], b * 6 + 1)
                    for ft in range(2):
                        mm = turn(ps[4][:, ft * P:(ft + 1) * P], mid[:, e % 2, ft * P:(ft + 1) * P])
                    mm.then_inc(mt_full[l], 1)

                def down(b, e):
                    w = [a.rearrange("p (f n) -> p f n", f=2) for a in split_piece(b, "C", e)]
                    pe.wait_ge(mt_read[l], b * EPG + (e + 1))
                    for half in range(2):
                        for ft in range(2):
                            cols = slice(half * 512, half * 512 + 512)
                            mm = both(ps[half][:, :], (midT[:, e % 2, 0, ft, :], midT[:, e % 2, 1, ft, :]),
                                      (w[0][:, ft, cols], w[1][:, ft, cols]), e == 0 and ft == 0, e == EPG - 1 and ft == 1)
                    if e < EPG - 1:
                        mm.then_inc(parts_used[l], 1)
                    else:
                        mm.then_inc(y_full[l], 1)
                        due[:] = [1, parts_used[l]]

                def scatter(b):
                    pe.wait_ge(y_read[l], b + 1)
                    pe.wait_ge(aux_read[l], b + 1)
                    for c in range(2 * NT):
                        if c == 5:
                            pe.wait_ge(mid_ready[l], b * EPG + (EPG + 2))
                        t, half = c // 2, c % 2
                        for h in range(2):
                            mm = product(ps[SCATTER_BANKS[c]][:, :], permT[:, t, :], ysb[:, h, half * 512:half * 512 + 512], start=h == 0, stop=h == 1)
                        mm.then_inc(scatter_full[l], 1)

                turn(ps[5][:, 0:P], ident[:, :])
                turn(ps[5][:, 0:P], ident[:, :]).then_inc(parts_used[l], 1)
                gather_tables(1)
                gather(0)
                gather(1)
                pe.wait_ge(hts_ready[l], 2)
                gate_up(None, 0, "A")
                gate_up(None, 0, "B")
                turn(ps[3][:, 0:P], ident[:, :])
                with pe.Fori(0, nb) as b:
                    for e in range(1, EPG):
                        gate_up(b, e, "A")
                        turn_mid(b, e - 1)
                        gate_up(b, e, "B")
                        if e == 1:
                            pe.wait_ge(scatter_read[l], b * 6 + 6)
                        down(b, e - 1)
                        if e == 2:
                            pe.wait_ge(aux_read[l], b + 1)
                            gather_tables(b + 2)
                            gather(0)
                            gather(1)
                    turn_mid(b, EPG - 1)
                    pe.wait_ge(hts_ready[l], b * 2 + 4)
                    gate_up(b, EPG, "A")
                    down(b, EPG - 1)
                    gate_up(b, EPG, "B")
                    scatter(b)
                pe.wait_ge(scatter_read[l], nb * 6 + 6)
                pe.wait_ge(mid_ready[l], nb * EPG + 2)
                pe.wait_ge(aux_read[l], nb + 1)
                pe.wait_ge(split_ready[l], nb * 12 + 5)
                turn(ps[3][:, 0:P], ident[:, :]).then_inc(ring_free, 1)

            def moe(l):
                norm_transposes(l, 1)
                for i in range(6):
                    drained_wait(pe, f"hT{l}.1", i)
                bank = claim(f"routerT{l}")
                for k in range(KT):
                    mm = product(bank[0:NE, 0:T], routw[:, k, :], hT[:, k, :], start=k == 0, stop=k == KT - 1)
                fill_inc(mm, f"routerT{l}")
                drained_wait(pe, f"routerT{l}")
                bank = claim(f"router{l}")
                for t in range(NT):
                    mm = pe.transpose(bank[:, t * NE:(t + 1) * NE], modrow[0:NE, t * P:(t + 1) * P], ident[0:NE, 0:NE])
                fill_inc(mm, f"router{l}")
                for t in range(NT):
                    for q in range(2):
                        bank = claim(f"htok{l}", 2 * t + q)
                        for j in range(4):
                            mm = turn(bank[:, j * P:(j + 1) * P], hT[:, 4 * q + j, t * P:(t + 1) * P])
                        fill_inc(mm, f"htok{l}", 2 * t + q)
                for i in range(3):
                    mod_step(f"ffn{l}", i)
                bank = claim(f"rank{l}")
                pe.wait_ge(in_route, 32 * (l + 1))
                pe.wait_ge(plan_sums[l], 1)
                product(bank[:, 0:12], before, sml[:, 5, 0:12], start=True, stop=False)
                product(bank[:, 0:12], onesr, plan[:, 0:12], start=False, stop=True)
                mm = product(bank[:, 12:16], onesr, plan[:, 12:16], start=True, stop=True)
                fill_inc(mm, f"rank{l}")
                experts(l)

            def spectrum(od):
                pe.wait_ge(esq_ready, (od + 1) * NT)
                for ft in range(2):
                    for r in range(2):
                        bank = claim(f"spec{od}", 2 + 2 * ft + r)
                        for k in range(2):
                            mm = product(bank[:, :], dfts[:, r, k, ft * P:(ft + 1) * P], filt[:, 1 + k, r, :],
                                           start=k == 0, stop=k == 1)
                        fill_inc(mm, f"spec{od}", 2 + 2 * ft + r)
                for r in range(2):
                    bank = claim(f"spec{od}", r)
                    mm = product(bank[:, :], dftp[:, r, :], filt[:, 0, r, :], start=True, stop=True)
                    fill_inc(mm, f"spec{od}", r)

            loaded(pe, in_filt)
            bank = claim("filt1")
            mm = product(bank[0:HID, 0:T], filtc[0:EMB, 3 + HID:3 + 2 * HID], zT, start=True, stop=True)
            fill_inc(mm, "filt1")
            mod_step("start", 0)
            pe.wait_ge(sin_done, 1)
            bank = claim("filt2")
            mm = product(bank[0:HID, 0:T], filtc[:, 3:3 + HID], hidden[0:HID, :], start=True, stop=True)
            fill_inc(mm, "filt2")
            mod_step("start", 1)
            loaded(pe, in_filt3)
            pe.wait_ge(sin_done, 2)
            pe.wait_ge(ones_set, 1)
            for od in range(2):
                for t in range(NT):
                    for r in range(2):
                        bank = claim(f"filt3.{od}", 2 * t + r)
                        mm = product(bank[:, :], hidden[:, t * P:(t + 1) * P], w3[:, 2 * od + r, :], start=True, stop=True)
                        fill_inc(mm, f"filt3.{od}", 2 * t + r)
                if od == 0:
                    mod_step("start", 2)
                else:
                    norm_transposes(0, 0)
                for g, tiles in enumerate(([0], [1, 2])):
                    bank = claim(f"energy{od}", g)
                    for t in tiles:
                        n = od * NT + t
                        pe.wait_ge(esq_ready, n + 1)
                        for r in range(2):
                            mm = product(bank[:, :], onesm, sqs[:, n % 2, r, :], start=t == tiles[0] and r == 0, stop=t == tiles[-1] and r == 1)
                        if t == 1:
                            mm.then_inc(esq_used, 1)
                    fill_inc(mm, f"energy{od}", g)
                if od == 0:
                    mod_step("start", 3)
                    loaded(pe, in_dft)
                    spectrum(0)
                if od == 0:
                    mod_step("start", 4)
                    loaded(pe, in_conv)
                    bank = claim("convT")
                    mm = pe.transpose(bank[:, 0:48], convraw, ident[0:48, 0:48])
                    fill_inc(mm, "convT")

            for i in range(6):
                drained_wait(pe, "hT0.0", i)
            for q in (6, 7, 8, 0, 1, 2, 3, 4, 5):
                w = weights(f"in0.{q}", (KT, 256))
                if q == 8:
                    spectrum(1)
                if q == 0:
                    pe.wait_ge(spec_done, 12)
                if q < 6:
                    for mt in range(2):
                        bank = claim("uT", 2 * q + mt)
                        for k in range(KT):
                            mm = product(bank[:, 0:T], w[:, k, mt * P:(mt + 1) * P], hT[:, k, :], start=k == 0, stop=k == KT - 1)
                        fill_inc(mm, "uT", 2 * q + mt)
                else:
                    for t in range(NT):
                        job = ("qkv", (q - 6) * NT + t) if q < 8 else ("qkv2", t)
                        bank = claim(*job)
                        for k in range(KT):
                            mm = product(bank[:, 0:256], hT[:, k, t * P:(t + 1) * P], w[:, k, :], start=k == 0, stop=k == KT - 1)
                        fill_inc(mm, *job)
                piece_end()

            for part, stage in enumerate(("vtok", "x1tok")):
                pe.wait_ge(conv_done, NCH * (part + 1))
                for t in range(NT):
                    bank = claim(stage, t)
                    for c in range(NCH):
                        mm = turn(bank[:, c * P:(c + 1) * P], uc[:, part * NCH + c, t * P:(t + 1) * P])
                    fill_inc(mm, stage, t)
            for od in range(2):
                if od == 0:
                    for t in range(NT):
                        drained_wait(pe, "vtok", t)
                else:
                    for t in range(NT):
                        drained_wait(pe, "inv0", t)
                for ft in range(NT):
                    for r in range(2):
                        i = 2 * ft + r
                        bank = claim(f"fwd{od}", i)
                        if ft == 0:
                            mm = product(bank[:, :], dftp[:, r, :], vtok[:, 0, :], start=True, stop=True)
                        else:
                            for k in range(2):
                                mm = product(bank[:, :], dfts[:, r, k, (ft - 1) * P:ft * P], vtok[:, 1 + k, :],
                                               start=k == 0, stop=k == 1)
                        fill_inc(mm, f"fwd{od}", i)
                mod_step("gqa", 2 * od)
                if od == 0:
                    for t in range(NT):
                        pe.wait_ge(y_ready, 1 if t == 0 else NT)
                        bank = claim("inv0", t)
                        if t == 0:
                            for r in range(2):
                                mm = product(bank[:, :], dftp[:, 2 + r, :], Y[:, 0, r, :], start=r == 0, stop=r == 1)
                        else:
                            for f in range(2):
                                for r in range(2):
                                    mm = product(bank[:, :], dfts[:, 2 + r, f, (t - 1) * P:t * P], Y[:, 1 + f, r, :],
                                                   start=f + r == 0, stop=f + r == 2)
                        fill_inc(mm, "inv0", t)
                    mod_step("gqa", 1)
                else:
                    pe.wait_ge(y_ready, 2 * NT)
                    for c in range(NCH):
                        bank = claim("inv1", c)
                        for r in range(2):
                            mm = product(bank[:, 0:NPR], Y[:, 0, r, c * P:(c + 1) * P], dftp[:, 2 + r, :],
                                           start=r == 0, stop=r == 1)
                        for f in range(2):
                            for r in range(2):
                                mm = product(bank[:, NPR:T], Y[:, 1 + f, r, c * P:(c + 1) * P], dfts[:, 2 + r, f, :],
                                               start=f + r == 0, stop=f + r == 2)
                        fill_inc(mm, "inv1", c)
                    mod_step("gqa", 3)

            pe.wait_ge(qk_ready, NT)
            for t in range(NT):
                for g in range(KVH):
                    bank = claim("qT", KVH * t + g)
                    for h in range(4):
                        c0 = (4 * g + h) * HD
                        mm = turn(bank[0:HD, h * P:(h + 1) * P], qkv[:, t, c0:c0 + HD])
                    fill_inc(mm, "qT", KVH * t + g)
            loaded(pe, in_attn)
            for g in range(KVH):
                bank = claim("kT", g)
                c0 = QH * HD + g * HD
                srcs = [qkv[:, 0, c0:c0 + HD], ck[:, g * HD:(g + 1) * HD], qkv[:, 1, c0:c0 + HD], qkv[:, 2, c0:c0 + HD]]
                for s, src in enumerate(srcs):
                    mm = turn(bank[0:HD, s * P:(s + 1) * P], src)
                fill_inc(mm, "kT", g)
            for i in range(NT * KVH):
                drained_wait(pe, "qT", i)
            for g in range(KVH):
                drained_wait(pe, "kT", g)

            def gqa_v(t, h):
                c0 = (QH + KVH) * HD + (h // 4) * HD
                own = [qkv[:, s, c0:c0 + HD] for s in range(NT)]
                cached = cv[:, (h // 4) * HD:(h // 4 + 1) * HD]
                return [own[0]] if t == 0 else [cached, own[1], own[2]]

            attention("g", units_gqa, QH, lambda t, h: qT[:, t, h, :],
                      lambda t, h: kT[:, h // 4, 0, :] if t == 0 else kT[:, h // 4, 1:4, :].rearrange("p a b -> p (a b)"), gqa_v)
            for t in range(NT):
                drained_wait(pe, "gO", t)
                bank = claim("goT", t)
                for c in range(4):
                    mm = turn(bank[:, c * P:(c + 1) * P], otok[:, t, c * P:(c + 1) * P])
                fill_inc(mm, "goT", t)
            for c in range(NCH):
                drained_wait(pe, "inv1", c)
            for t in range(NT):
                drained_wait(pe, "goT", t)
            out_projection(0)
            moe(0)

            norm_transposes(1, 0)
            for i in range(6):
                drained_wait(pe, "hT1.0", i)
            for t in range(NT):
                claim("um", t)
            for kh in range(2):
                w = weights(f"in1.{kh}", (4, ODD_IN))
                for t in range(NT):
                    bank = ps[B["um", t][0]]
                    for k in range(4):
                        mm = product(bank[:, 0:ODD_IN], hT[:, 4 * kh + k, t * P:(t + 1) * P], w[:, k, :],
                                       start=kh == 0 and k == 0, stop=kh == 1 and k == 3)
                    if kh == 1:
                        fill_inc(mm, "um", t)
                piece_end()
            pe.wait_ge(lora_ready, NT)
            loaded(pe, in_mla)
            for t in range(NT + 1):
                bank = claim("cT", t)
                srcs = [ckv_c] if t == NT else [um[:, t, c * P:(c + 1) * P] for c in range(3)]
                for c, src in enumerate(srcs):
                    mm = turn(bank[:, c * P:(c + 1) * P], src)
                fill_inc(mm, "cT", t)
            for t in range(NT + 1):
                drained_wait(pe, "cT", t)
            loaded(pe, in_mla_w)
            def project(g):
                for t in range(NT):
                    bank = claim(f"mq{g}", t)
                    for k in range(2):
                        mm = product(bank[:, 0:HG * QK], cT[:, k, t * P:(t + 1) * P],
                                       w_q[:, k, g * HG * QK:(g + 1) * HG * QK], start=k == 0, stop=k == 1)
                    fill_inc(mm, f"mq{g}", t)
                project_kv(g, "mk", 0)

            def project_kv(g, stage, e0):
                w = w_kv[:, g * 512:(g + 1) * 512].rearrange("p (h e) -> p h e", h=HG)
                for t in range(NT + 1):
                    bank = claim(f"{stage}{g}", t)
                    lhs = cvT if t == NT else cT[:, 2, t * P:(t + 1) * P]
                    mm = product(bank[:, 0:HG * NOPE].rearrange("p (h e) -> p h e", h=HG), lhs, w[:, :, e0:e0 + NOPE], start=True, stop=True)
                    fill_inc(mm, f"{stage}{g}", t)

            project(0)
            for i in range(MLA_AHEAD):
                mod_step("mla", i)
            for g in range(NHG):
                q4, k4 = q4s[g % 2], k4s[g % 2]
                project_kv(g, "mv", NOPE)
                pe.wait_ge(qk_ready, NT + 1 + g)
                pe.wait_ge(qk_turned, g + 1)
                for t in range(NT):
                    bank = claim(f"mqT{g}", t)
                    for h in range(HG):
                        mm = turn(bank[0:QK, h * P:(h + 1) * P], q4[:, t, h, :])
                    fill_inc(mm, f"mqT{g}", t)
                for s, t in enumerate((0, 3, 1, 2)):
                    bank = claim(f"mkT{g}", s)
                    for h in range(HG):
                        mm = turn(bank[0:QK, h * P:(h + 1) * P], k4[:, t, h, :])
                    fill_inc(mm, f"mkT{g}", s)
                for t in range(NT):
                    drained_wait(pe, f"mqT{g}", t)
                for t in range(NT + 1):
                    drained_wait(pe, f"mkT{g}", t)
                if g + 1 < NHG:
                    project(g + 1)
                for t in range(NT + 1):
                    drained_wait(pe, f"mv{g}", t)
                attention(str(g), units_mla, HG, lambda t, h: q4T[:, t, h, :],
                          lambda t, h: k4T[:, h, 0, :] if t == 0 else k4T[:, h, 1:4, :].rearrange("p a b -> p (a b)"),
                          lambda t, h: [v4[:, s, h, :] for s in ((0,) if t == 0 else (3, 1, 2))])
            for g in range(NHG):
                for t in range(NT):
                    drained_wait(pe, f"mO{g}", t)
            for t in range(NT):
                for q in range(2):
                    bank = claim("moT", 2 * t + q)
                    for c in range(4):
                        mm = turn(bank[:, c * P:(c + 1) * P], mtok[:, t, (4 * q + c) * P:(4 * q + c + 1) * P])
                    fill_inc(mm, "moT", 2 * t + q)
            for i in range(2 * NT):
                drained_wait(pe, "moT", i)
            out_projection(1)
            moe(1)

        @block.scalar
        def _(act):
            load(act, in_cond, condraw[:, 0, :], d["c_ctx"].rearrange("(p j) -> p j", j=KT))
            load(act, in_cond, condraw[:, 1, :], d["c"][0].rearrange("(p j) -> p j", j=KT))
            load(act, in_filt, zT, d["zT"])
            load(act, in_filt, filtc[0:EMB, 3 + HID:3 + 2 * HID], d["ev_filt_w1"][0])
            load(act, in_filt, filtc[:, 0:1], d["ev_filt_b1"].rearrange("a n -> n a"))
            load(act, in_filt, filtc[:, 1:2], d["ev_filt_b2"].rearrange("a n -> n a"))
            load(act, in_filt, filtc[:, 2:3], d["ev_filt_freq"].rearrange("a n -> n a"))
            load(act, in_filt, filtc[:, 3:3 + HID], d["ev_filt_w2"][0])
            load(act, in_mod, ident[:, :], d["ident"])
            load(act, in_mod, rowsel[:, :, :], d["rowsel"].rearrange("p (a b) -> p a b", b=P))
            load(act, in_mod, chunksel[:, :, :], d["chunksel"].rearrange("p (a b) -> p a b", b=2))
            for l in range(2):
                load(act, in_mod, modbias[:, l, :, :], d["b_mod"][l].rearrange("(v p j) -> p v j", v=6, j=KT))
            load(act, in_mod, bmod[:, :], d["b_mod"].rearrange("l (c n) -> (l c) n", n=512))
            for l in range(2):
                load(act, in_mod, gain[:, l, 0, :], d["norm_mix"][l].rearrange("(p j) -> p j", j=KT))
                load(act, in_mod, gain[:, l, 1, :], d["norm_ffn"][l].rearrange("(p j) -> p j", j=KT))
            load(act, in_mod, routw[:, :, :], d["router_w"].rearrange("(p j) n -> p j n", j=KT))
            load(act, in_conv, convraw[0:36, :], d["ev_conv_w"][0].rearrange("k (c n) -> (k c) n", n=P))
            load(act, in_conv, convraw[36:48, :], d["ev_conv_b"][0].rearrange("(c n) -> c n", n=P))

            loaded(act, in_cond)
            act.wait_ge(cond_zero, 1)
            for c in range(2):
                act.activation(condT[:, :, c], condraw[:, c, :], ACT.Silu).then_inc(cond_ready, 1)

            def copy_out(stage, i, dst, src, **kw):
                filled_wait(act, stage, i)
                drain_inc(act.activation(dst, src, kw.pop("func", ACT.Copy), **kw), stage, i)

            def bank_of(stage, i=0):
                return ps[B[stage, i][0]]

            def mod_step(where, i):
                chunks = CHUNKS[where]
                if i < len(chunks):
                    l, v, half = chunks[i]
                    copy_out(f"mod{l}.{v}.{half}", 0, modrow_of(where, i), bank_of(f"mod{l}.{v}.{half}")[:, :])
                if 1 <= i <= len(chunks) and chunks[i - 1][1] in (G1, G2):
                    l, v, half = chunks[i - 1]
                    for c in range(2):
                        sel = f"modsel{l}.{v}.{half}"
                        copy_out(sel, c, gb[:, c, half * 512:half * 512 + 512], bank_of(sel, c)[:, :])

            def norm(l, which, x_sem, x_count):
                s = 2 * l + which
                for t in range(NT):
                    act.wait_ge(x_sem, x_count - (NT - 1 - t) if which else x_count)
                    act.activation(xn[:, t, :], x[:, t, :], ACT.Square, accum_out=ssq[:, s, t:t + 1]).then_inc(squares, 1)
                    act.wait_ge(meansq, s * NT + t + 1)
                    act.activation(ssq[:, s, t:t + 1], ssq[:, s, t:t + 1], ACT.Sqrt).then_inc(rootsq, 1)

            def modulate(l, which):
                act.wait_ge(moda_ready, MODA_ORDER.index((l, which)) + 1)
                sh = 0 if which == 0 else 3
                for i in range(0, 6, 2):
                    t, q = i // 2, i % 2
                    bank = filled_wait(act, f"hT{l}.{which}", i)
                    for j in range(4):
                        k = 4 * q + j
                        ins = act.activation(hT[:, k, t * P:(t + 1) * P], bank[:, j * P:(j + 1) * P], ACT.Identity,
                                             bias=modT[:, l, sh, k, GRP[t]:GRP[t] + 1],
                                             scale=modA[:, l, which, k, GRP[t]:GRP[t] + 1])
                    drain_inc(ins, f"hT{l}.{which}", i)

            def mla_root(g):
                act.wait_ge(qvar, 2 + g)
                act.activation(statA[:, 1, 0:28], statA[:, 0, 0:28], ACT.Sqrt).then_inc(qroot, 1)

            def attention(tag, units):
                S, PT = (f"{tag}S", f"{tag}PT") if tag == "g" else (f"mS{tag}", f"mPT{tag}")
                pr = probs if tag == "g" else mprobs
                first = 0 if tag == "g" else len(units_gqa) + int(tag) * len(units_mla)
                for i, (t, h) in enumerate(units):
                    nk = P if t == 0 else T
                    act.wait_ge(negmax_ready, first + i + 1)
                    if i >= 2:
                        filled_wait(act, PT, i - 2)
                    bank = bank_of(S, i)
                    ins = act.activation(pr[:, i % 2, 0:nk], bank[:, 0:nk], ACT.Exp, bias=negmax[:, i:i + 1],
                                         accum_out=psumexp[:, i:i + 1])
                    drain_inc(ins, S, i)
                    if tag != "g" and int(tag) + 1 < NHG and i == 6:
                        mla_root(int(tag) + 1)
                    if tag == "g" and i in GQA_AT:
                        mod_step("gqa", GQA_AT[i])
                    if tag != "g" and (int(tag), i) in MLA_AT:
                        mod_step("mla", MLA_AT[int(tag), i])

            def experts(l):
                nb = blocks_of(act, l)

                def inputs(half, count):
                    act.wait_ge(gather_full[l], count)
                    act.activation(hTs[:, 0, 4 * half:4 * half + 4, :].rearrange("p a b -> p (a b)"), ps[6 + half][:, :],
                                   ACT.Copy).then_inc(hts_hi[l], 1)

                def high(b, kind, e):
                    each = 16 if kind == "C" else 32
                    act.wait_ge(loaded_w[l][kind + str(e % 2)], each if b is None else b * (2 * each) + (e // 2 + 1) * each)
                    act.activation(high_of(kind, e), raw(kind, e), ACT.Copy).then_inc(hi_ready[l], 1)

                def turned(b, e):
                    act.wait_ge(mt_full[l], b * EPG + (e + 1))
                    act.activation(midT[:, e % 2, 0, :, :].rearrange("p a b -> p (a b)"), ps[4][:, 0:DE], ACT.Copy).then_inc(mt_hi[l], 1)

                def silu(b, e):
                    if b is None:
                        act.wait_ge(gu_full[l], 1)
                    else:
                        act.wait_ge(gu_full[l], b * EPG + (e + 1))
                        act.wait_ge(mid_ready[l], b * EPG + e)
                    act.activation(sil[:, e % 2, :], ps[2 + e % 2][:, 0:DE], ACT.Silu).then_inc(silu_ready[l], 1)

                high(None, "A", 0)
                inputs(0, 2)
                inputs(1, 3)
                for kind, e in FIRST_PIECES[1:4]:
                    high(None, kind, e)
                silu(None, 0)
                high(None, "C", 0)
                with act.Fori(0, nb) as b:
                    for e in range(1, EPG + 1):
                        if e == EPG:
                            turned(b, e - 1)
                        high(b, "A", e + 1)
                        if e == EPG:
                            high(b, "B", e + 1)
                            act.wait_ge(y_full[l], b + 1)
                            for half in range(2):
                                ins = act.activation(ysb[:, 0, half * 512:half * 512 + 512], ps[half][:, :], ACT.Copy)
                            ins.then_inc(y_hi[l], 1)
                            silu(b, e)
                        else:
                            high(b, "B", e + 1)
                            turned(b, e - 1)
                            if e == EPG - 1:
                                act.wait_ge(gu_full[l], b * EPG + (e + 1))
                                inputs(0, b * 3 + 5)
                                inputs(1, b * 3 + 6)
                            silu(b, e)
                        high(b, "C", e)

            def moe(l):
                norm(l, 1, x_mixed, 2 * NT * (l + 1))
                modulate(l, 1)
                copy_out(f"routerT{l}", 0, modrow[0:NE, 0:T], bank_of(f"routerT{l}")[0:NE, 0:T], func=ACT.Sigmoid)
                for i in range(6):
                    t, q = i // 2, i % 2
                    copy_out(f"htok{l}", i, htok[:, t, q * 512:q * 512 + 512], bank_of(f"htok{l}", i)[:, :])
                for i in range(3):
                    mod_step(f"ffn{l}", i)
                experts(l)

            for i in range(2):
                act.wait_ge(sin_arg, i + 1)
                act.activation(hidden[0:HID, :], hidden[0:HID, :], ACT.Sin).then_inc(sin_done, 1)
                mod_step("start", i)
            for od in range(2):
                for t in range(NT):
                    n = od * NT + t
                    if od == 0 and t == 2:
                        mod_step("start", 2)
                    act.wait_ge(sum_ready, n + 1)
                    if n >= 2:
                        m = n - 2
                        if m % NT == 1:
                            act.wait_ge(esq_used, m // NT + 1)
                        else:
                            filled_wait(act, f"energy{m // NT}", 0 if m % NT == 0 else 1)
                    act.activation(filt[:, t, 0, :], sqd, ACT.Copy)
                    act.activation(sqs[:, n % 2, 0, :], sqd, ACT.Square)
                    act.activation(sqs[:, n % 2, 1, :], filt[:, t, 1, :], ACT.Square)
                    act.drain().then_inc(esq_ready, 1)
                if od == 1:
                    modulate(0, 0)
                for g in range(2):
                    act.wait_ge(eroot, 2 * od + g + 1)
                    act.activation(esc[:, g, :], esc[:, g, :], ACT.Sqrt).then_inc(escale_ready, 1)
                if od == 0:
                    mod_step("start", 3)
                    norm(0, 0, in_x, 16 * LOADS["in_x"])
            for q in range(3):
                for t in range(NT):
                    job = ("qkv", q * NT + t) if q < 2 else ("qkv2", t)
                    copy_out(*job, qkv[:, t, q * 256:(q + 1) * 256], bank_of(*job)[:, 0:256])
            act.wait_ge(qvar, 1)
            act.activation(statA[:, 1, 0:30], statA[:, 0, 0:30], ACT.Sqrt).then_inc(qroot, 1)
            act.wait_ge(conv_copied, 1)
            for m in range(3 * NCH):
                bank = filled_wait(act, "uT", m)
                act.activation(uc[:, m, :], bank[:, 0:T], ACT.Identity, bias=convT[:, 3, m:m + 1], scale=convT[:, 1, m:m + 1])
                drain_inc(act.activation(uT[:, m, :], bank[:, 0:T], ACT.Copy), "uT", m)
            for t in range(NT):
                copy_out("vtok", t, vtok[:, t, :], bank_of("vtok", t)[:, :])
            for t in range(NT):
                copy_out("x1tok", t, x1tok[:, t, :], bank_of("x1tok", t)[:, :])
            for i in range(GQA_AHEAD):
                mod_step("gqa", i)
            for i in range(NT * KVH):
                t, g = i // KVH, i % KVH
                copy_out("qT", i, qT[:, t, 4 * g:4 * g + 4, :].rearrange("p a b -> p (a b)"), bank_of("qT", i)[0:HD, :])
            for g in range(KVH):
                copy_out("kT", g, kT[:, g, :, :].rearrange("p a b -> p (a b)"), bank_of("kT", g)[0:HD, :])
            attention("g", units_gqa)
            for t in range(NT):
                copy_out("goT", t, hT[:, 4:8, t * P:(t + 1) * P], bank_of("goT", t)[:, :].rearrange("p (a b) -> p a b", b=P))
            moe(0)

            norm(1, 0, x_done, 1)
            modulate(1, 0)
            for t in range(NT):
                copy_out("um", t, um[:, t, :], bank_of("um", t)[:, 0:ODD_IN])
            act.drain()
            for t in range(NT):
                act.activation(junk[:, t, 0:QR], um[:, t, 0:QR], ACT.Square, accum_out=statA[:, 0, t:t + 1])
                ins = act.activation(junk[:, t, QR:QR + KVR], um[:, t, QR:QR + KVR], ACT.Square, accum_out=statA[:, 0, NT + t:NT + t + 1])
            ins.then_inc(lora_sq, 1)
            act.wait_ge(lora_var, 1)
            act.activation(statA[:, 1, 0:2 * NT], statA[:, 0, 0:2 * NT], ACT.Sqrt).then_inc(lora_root, 1)
            for t in range(NT + 1):
                if t < NT:
                    copy_out("cT", t, cT[:, :, t * P:(t + 1) * P], bank_of("cT", t)[:, 0:3 * P].rearrange("p (a b) -> p a b", b=P))
                else:
                    copy_out("cT", t, cvT, bank_of("cT", t)[:, 0:P])
            def queries_keys(g):
                for t in range(NT):
                    copy_out(f"mq{g}", t, q4s[g % 2][:, t, :, :].rearrange("p h e -> p (h e)"), bank_of(f"mq{g}", t)[:, 0:HG * QK])
                for t in range(NT + 1):
                    copy_out(f"mk{g}", t, k4s[g % 2][:, t, :, 0:NOPE],
                             bank_of(f"mk{g}", t)[:, 0:HG * NOPE].rearrange("p (h e) -> p h e", h=HG))

            queries_keys(0)
            mod_step("mla", 0)
            mla_root(0)
            for i in range(1, MLA_AHEAD):
                mod_step("mla", i)
            for g in range(NHG):
                for t in range(NT + 1):
                    copy_out(f"mv{g}", t, v4[:, t, :, :], bank_of(f"mv{g}", t)[:, 0:HG * VD].rearrange("p (h e) -> p h e", h=HG))
                for t in range(NT):
                    copy_out(f"mqT{g}", t, q4T[:, t, :, :].rearrange("p a b -> p (a b)"), bank_of(f"mqT{g}", t)[0:QK, :])
                for s in range(NT + 1):
                    copy_out(f"mkT{g}", s, k4T[:, :, s, :], bank_of(f"mkT{g}", s)[0:QK, :].rearrange("p (a b) -> p a b", b=P))
                if g + 1 < NHG:
                    queries_keys(g + 1)
                attention(str(g), units_mla)
            for i in range(2 * NT):
                t, q = i // 2, i % 2
                copy_out("moT", i, hT[:, 4 * q:4 * q + 4, t * P:(t + 1) * P], bank_of("moT", i)[:, :].rearrange("p (a b) -> p a b", b=P))
            moe(1)

        @block.vector
        def _(dve):
            def settle():
                dve.drain()

            def bank_of(stage, i=0):
                return ps[B[stage, i][0]]

            def mod_step(where, i):
                if not 1 <= i <= len(CHUNKS[where]) or CHUNKS[where][i - 1][1] in (G1, G2):
                    return
                l, v, half = CHUNKS[where][i - 1]
                sel = f"modsel{l}.{v}.{half}"
                bank = filled_wait(dve, sel)
                rows = slice(64 * half, 64 * half + 64)
                drain_inc(dve.tensor_tensor(modT[rows, l, v, :, :], bank[rows, 0:2 * KT].rearrange("p (a b) -> p a b", b=2),
                                            modT[rows, l, v, :, :], ALU.add), sel)
                if half == 0 or v in (SH1, SH2):
                    return
                which = 0 if v == SC1 else 1
                settle()
                A = modA[:, l, which, :, :]
                dve.tensor_scalar(A, modT[:, l, v, :, :], 1.0, None, ALU.add)
                settle()
                g = gain[:, l, which, :].unsqueeze(2).broadcast_to([P, KT, 2])
                dve.tensor_tensor(A, A, g, ALU.mult).then_inc(moda_ready, 1)

            def norm_tile(s, t):
                dve.wait_ge(squares, s * NT + t + 1)
                r = ssq[:, s, t:t + 1]
                dve.tensor_scalar(r, r, 1.0 / D, EPS, ALU.mult, ALU.add).then_inc(meansq, 1)
                dve.wait_ge(rootsq, s * NT + t + 1)
                dve.reciprocal(r, r)
                settle()
                dve.tensor_scalar(xn[:, t, :], x[:, t, :], r, None, ALU.mult).then_inc(xn_ready, 1)

            def norm(s):
                for t in range(NT):
                    norm_tile(s, t)

            def modulate(l, which):
                settle()
                sh = 0 if which == 0 else 3
                for i in range(1, 6, 2):
                    t, q = i // 2, i % 2
                    bank = filled_wait(dve, f"hT{l}.{which}", i)
                    for j in range(4):
                        k = 4 * q + j
                        ins = dve.tensor_scalar(hT[:, k, t * P:(t + 1) * P], bank[:, j * P:(j + 1) * P],
                                                modA[:, l, which, k, GRP[t]:GRP[t] + 1],
                                                modT[:, l, sh, k, GRP[t]:GRP[t] + 1], ALU.mult, ALU.add)
                    drain_inc(ins, f"hT{l}.{which}", i)

            def attention(tag, units, heads, o_dst):
                S, PT, O = (f"{tag}S", f"{tag}PT", f"{tag}O") if tag == "g" else (f"mS{tag}", f"mPT{tag}", f"mO{tag}")
                pT = probsT if tag == "g" else mprobsT
                pvs = 0 if tag == "g" else NT * (QH - 1) + int(tag) * NT * (HG - 1)
                n = len(units)
                for i in range(n + 3):
                    if 2 <= i <= n + 1:
                        j = i - 2
                        t, h = units[j]
                        nk = P if t == 0 else T
                        bank = filled_wait(dve, PT, j)
                        if j >= 2:
                            tj, hj = units[j - 2]
                            if hj == heads - 1:
                                filled_wait(dve, O, tj)
                            else:
                                dve.wait_ge(pv_done, pvs + tj * (heads - 1) + hj + 1)
                        drain_inc(dve.tensor_copy(pT[:, j % 2, :, :].rearrange("p a b -> p (a b)")[:, 0:nk], bank[:, 0:nk]), PT, j)
                    if i < n:
                        t, h = units[i]
                        nk = P if t == 0 else T
                        bank = filled_wait(dve, S, i)
                        dve.tensor_reduce(negmax[:, i:i + 1], bank[:, 0:nk], AXX, ALU.max, negate=True).then_inc(negmax_ready, 1)
                    if tag == "g" and i - 1 in GQA_AT:
                        mod_step("gqa", GQA_AT[i - 1])
                    if tag != "g" and (int(tag), i - 1) in MLA_AT:
                        mod_step("mla", MLA_AT[int(tag), i - 1])
                    if tag != "g" and int(tag) + 1 < NHG and i in MLA_NORM_AT:
                        for step in MLA_NORM_AT[i]:
                            mla_norm(int(tag) + 1, step)
                    if i >= 3 and units[i - 3][1] == heads - 1:
                        t = units[i - 3][0]
                        dve.reciprocal(rinv[:, 0:heads], psumexp[:, t * heads:(t + 1) * heads])
                        settle()
                        bank = filled_wait(dve, O, t)
                        ins = dve.tensor_tensor(o_dst(t), bank[:, 0:heads * HD].rearrange("p (h e) -> p h e", e=HD),
                                                rinv[:, 0:heads].unsqueeze(2).broadcast_to([P, heads, HD]), ALU.mult)
                        drain_inc(ins, O, t)

            def mla_norm(g, step):
                nq, nkk = NT * HG, (NT + 1) * HG
                q4, k4 = q4s[g % 2], k4s[g % 2]
                flat = lambda a: a.rearrange("p t h e -> p (t h) e")
                settle()
                if step == 0:
                    for t in range(NT):
                        drained_wait(dve, f"mq{g}", t)
                    for t in range(NT + 1):
                        kr = kr_c if t == NT else um[:, t, QR + KVR:ODD_IN]
                        dve.tensor_copy(k4[:, t, :, NOPE:QK], kr.unsqueeze(1).broadcast_to([P, HG, ROPE]))
                    dve.tensor_tensor(flat(msq)[:, 0:nq, :], flat(q4), flat(q4), ALU.mult)
                elif step == 1:
                    dve.tensor_reduce(statA[:, 0, 0:nq], flat(msq)[:, 0:nq, :], AXX, ALU.add)
                elif step == 2:
                    for t in range(NT + 1):
                        drained_wait(dve, f"mk{g}", t)
                    dve.tensor_tensor(flat(msq), flat(k4), flat(k4), ALU.mult)
                elif step == 3:
                    dve.tensor_reduce(statA[:, 0, nq:nq + nkk], flat(msq), AXX, ALU.add)
                    settle()
                    dve.tensor_scalar(statA[:, 0, 0:28], statA[:, 0, 0:28], 1.0 / QK, EPS, ALU.mult, ALU.add).then_inc(qvar, 1)
                elif step == 4:
                    dve.wait_ge(qroot, 2 + g)
                    dve.reciprocal(statA[:, 1, 0:28], statA[:, 1, 0:28]).then_inc(inv_root, 1)
                    settle()
                if step >= 8:
                    mla_turn(dve, g, step, (mrb[:, 0, :, :], mrb[:, 1, :, :]))
                    if step == 11:
                        dve.drain().then_inc(qk_ready, 1)

            def out_projection(l):
                for half in range(2):
                    cols = slice(half * 512, half * 512 + 512)
                    for t in range(NT):
                        i = half * NT + t
                        if i == 0:
                            for h2 in range(2):
                                for c in range(2):
                                    drained_wait(dve, f"modsel{l}.{G1}.{h2}", c)
                        bank = filled_wait(dve, f"out{l}", i)
                        tmp = tmpa if i % 2 == 0 else tmpb
                        drain_inc(dve.tensor_tensor(tmp, bank[:, :], gb[:, GRP[t], cols], ALU.mult), f"out{l}", i)
                        settle()
                        dve.tensor_tensor(x[:, t, cols], x[:, t, cols], tmp, ALU.add).then_inc(x_mixed, 1)
                        if half == 1:
                            norm_tile(2 * l + 1, t)

            def route(l):
                col = lambda i, n: sml[:, i, 0:n]
                by = lambda a, n: a.rearrange("p (a b) -> p a b", b=n)
                wide = lambda a, n, m: a.unsqueeze(2).broadcast_to([P, n, m])
                every = lambda a, n: a.unsqueeze(1).broadcast_to([P, NT, n])
                scores, sel, pairs, t3, t4 = col(0, 48), col(1, 48), col(2, 72), col(3, 48), col(4, 48)
                gmask, hot = col(5, 12), col(6, 48)
                small = col(7, 72)
                bank = filled_wait(dve, f"router{l}")
                drain_inc(dve.tensor_copy(scores, bank[:, 0:NT * NE]), f"router{l}")
                settle()
                dve.tensor_tensor(by(sel, NE), by(scores, NE), every(routb[:, :], NE), ALU.add)
                settle()
                s4, p6 = by(sel, EPG), by(pairs, 6)
                dve.tensor_tensor(p6[:, :, 0:3], s4[:, :, 0:3], s4[:, :, 1:4], ALU.add)
                dve.tensor_tensor(p6[:, :, 3:5], s4[:, :, 0:2], s4[:, :, 2:4], ALU.add)
                dve.tensor_tensor(p6[:, :, 5:6], s4[:, :, 0:1], s4[:, :, 3:4], ALU.add)
                settle()
                dve.tensor_reduce(small[:, 0:12], p6, AXX, ALU.max)
                settle()

                def first_best(out, v, n, rank, best):
                    dve.tensor_reduce(best, by(v, n), AXX, ALU.max)
                    settle()
                    dve.tensor_tensor(by(out, n), by(v, n), wide(best, NT, n), ALU.is_equal)
                    settle()
                    dve.tensor_tensor(by(out, n), by(out, n), every(rank, n), ALU.mult)
                    settle()
                    dve.tensor_reduce(best, by(out, n), AXX, ALU.max)
                    settle()
                    dve.tensor_tensor(by(out, n), by(out, n), wide(best, NT, n), ALU.is_equal)
                    settle()

                first_best(gmask, small[:, 0:12], NG, rank_e[:, NE - NG:], small[:, 12:15])
                dve.tensor_scalar(small[:, 16:28], gmask, 1e30, -1e30, ALU.mult, ALU.add)
                dve.tensor_tensor(by(t3, EPG), by(sel, EPG), wide(gmask, NT * NG, EPG), ALU.mult)
                settle()
                dve.tensor_tensor(by(t3, EPG), by(t3, EPG), wide(small[:, 16:28], NT * NG, EPG), ALU.add)
                settle()
                first_best(hot, t3, NE, rank_e[:, :], small[:, 12:15])
                dve.scalar_tensor_tensor(out=t3, in0=hot, scalar=-2e30, in1=t3, op0=ALU.mult, op1=ALU.add)
                settle()
                first_best(t4, t3, NE, rank_e[:, :], small[:, 12:15])
                dve.tensor_tensor(hot, hot, t4, ALU.add)
                settle()
                dve.tensor_tensor(t3, hot, scores, ALU.mult)
                settle()
                dve.tensor_reduce(small[:, 12:15], by(t3, NE), AXX, ALU.add)
                settle()
                dve.reciprocal(small[:, 12:15], small[:, 12:15])
                settle()
                dve.tensor_tensor(gates[:, :, :], by(t3, NE), wide(small[:, 12:15], NT, NE), ALU.mult)
                settle()

            def make_plan(l):
                gm = sml[:, 5, 0:12]
                small = sml[:, 7, :]
                cum, tot, rank, size, nblk, end, first, slot, grp = (
                    plan[:, 0:12], plan[:, 12:16], plan[:, 16:28], plan[:, 28:32], plan[:, 32:36],
                    plan[:, 36:40], plan[:, 40:44], plan[:, 44:47], plan[:, 48:48 + NBLK + 1])
                tile = lambda t: gm[:, 4 * t:4 * t + 4]
                dve.memset(onesr, 1.0)
                dve.memset(cum[:, 0:4], 0.0)
                dve.tensor_copy(cum[:, 4:8], tile(0))
                dve.tensor_tensor(cum[:, 8:12], tile(0), tile(1), ALU.add)
                settle()
                dve.tensor_tensor(tot, cum[:, 8:12], tile(2), ALU.add).then_inc(plan_sums[l], 1)
                g4 = gates[:, :, :].rearrange("p t (g e) -> p t g e", e=EPG)
                gsum = plan[:, 64:76].rearrange("p (t e) -> p t e", e=EPG)
                dve.tensor_tensor(gsum, g4[:, :, 0, :], g4[:, :, 1, :], ALU.add)
                for g in (2, 3):
                    settle()
                    dve.tensor_tensor(gsum, gsum, g4[:, :, g, :], ALU.add)
                bank = filled_wait(dve, f"rank{l}")
                drain_inc(dve.tensor_copy(plan[:, 16:32], bank[:, 0:16]), f"rank{l}")
                settle()
                dve.tensor_scalar(nblk, size, 0.0, None, ALU.is_gt)
                for m in (1, 2):
                    settle()
                    dve.scalar_tensor_tensor(out=nblk, in0=size, scalar=float(m * P), in1=nblk, op0=ALU.is_gt, op1=ALU.add)
                settle()
                dve.tensor_copy(end, nblk)
                for g in range(1, NG):
                    settle()
                    dve.tensor_tensor(end[:, g:g + 1], end[:, g - 1:g], nblk[:, g:g + 1], ALU.add)
                settle()
                dve.tensor_tensor(first, end, nblk, ALU.subtract)
                dve.tensor_scalar(grp, slots[:, 0:NBLK + 1], end[:, 0:1], None, ALU.is_ge)
                for g in (1, 2):
                    settle()
                    dve.scalar_tensor_tensor(out=grp, in0=slots[:, 0:NBLK + 1], scalar=end[:, g:g + 1], in1=grp, op0=ALU.is_ge, op1=ALU.add)
                settle()
                dve.tensor_copy(meta[0:1, l, 0:1], end[0:1, 3:4])
                dve.tensor_copy(meta[0:1, l, 1:2 + NBLK], grp[0:1, :]).then_inc(plan_ready[l], 1)
                dve.tensor_scalar(first, first, float(P), None, ALU.mult)
                settle()
                by = lambda a: a.rearrange("p (t g) -> p t g", g=NG)
                dve.tensor_tensor(by(rank), by(rank), first.unsqueeze(1).broadcast_to([P, NT, NG]), ALU.add)
                settle()
                dve.tensor_tensor(rank, rank, gm, ALU.mult)
                settle()
                dve.tensor_reduce(slot, by(rank), AXX, ALU.add)
                settle()

            def experts(l):
                slot, gslot = plan[:, 44:47], plan[:, 80:84]
                nb = blocks_of(dve, l)

                def permute():
                    for t in range(NT):
                        ins = dve.tensor_scalar(perm[:, t, :], slots, slot[:, t:t + 1], None, ALU.is_equal)
                    ins.then_inc(perm_ready[l], 1)
                    settle()
                    dve.tensor_scalar(slot, slot, float(-P), None, ALU.add)
                    settle()

                def slot_gates(count):
                    settle()
                    dve.wait_ge(gather_full[l], count)
                    dve.tensor_copy(gslot, ps[5][:, T:T + EPG])
                    settle()

                def back_table():
                    dve.tensor_copy(permT.rearrange("p a b -> p (a b)"), ps[5][:, 0:T]).then_inc(aux_read[l], 1)

                def low(b, kind, e):
                    dve.wait_ge(hi_ready[l], b * 12 + order(kind, e) if b is not None else FIRST_PIECES.index((kind, e)) + 1)
                    dve.tensor_tensor(low_of(kind, e), raw(kind, e), high_of(kind, e).bitcast(F32), ALU.subtract).then_inc(split_ready[l], 1)

                def inputs(half, count):
                    dve.wait_ge(hts_hi[l], count)
                    flat = lambda h: hTs[:, h, 4 * half:4 * half + 4, :].rearrange("p a b -> p (a b)")
                    dve.tensor_tensor(flat(1), ps[6 + half][:, :], flat(0).bitcast(F32), ALU.subtract).then_inc(hts_ready[l], 1)

                def turned(b, e):
                    dve.wait_ge(mt_hi[l], b * EPG + (e + 1))
                    flat = lambda h: midT[:, e % 2, h, :, :].rearrange("p a b -> p (a b)")
                    dve.tensor_tensor(flat(1), ps[4][:, 0:DE], flat(0).bitcast(F32), ALU.subtract).then_inc(mt_read[l], 1)

                def middle(b, e):
                    dve.wait_ge(silu_ready[l], 1 if b is None else b * EPG + (e + 1))
                    dve.scalar_tensor_tensor(out=mid[:, e % 2, :], in0=sil[:, e % 2, :], scalar=gslot[:, e % EPG:e % EPG + 1],
                                             in1=ps[2 + e % 2][:, DE:2 * DE], op0=ALU.mult, op1=ALU.mult).then_inc(mid_ready[l], 1)

                for h2 in range(2):
                    for c in range(2):
                        drained_wait(dve, f"modsel{l}.{G2}.{h2}", c)
                permute()
                slot_gates(1)
                back_table()
                dve.drain().then_inc(scatter_read[l], 6)
                dve.drain().then_inc(mid_ready[l], 1)
                low(None, "A", 0)
                inputs(0, 1)
                inputs(1, 2)
                for kind, e in FIRST_PIECES[1:4]:
                    low(None, kind, e)
                middle(None, 0)
                low(None, "C", 0)
                with dve.Fori(0, nb) as b:
                    for e in range(1, EPG + 1):
                        if e in (1, EPG):
                            turned(b, e - 1)
                        low(b, "A", e + 1)
                        if e == EPG:
                            low(b, "B", e + 1)
                            dve.wait_ge(y_hi[l], b + 1)
                            for half in range(2):
                                cols = slice(half * 512, half * 512 + 512)
                                ins = dve.tensor_tensor(ysb[:, 1, cols], ps[half][:, :], ysb[:, 0, cols].bitcast(F32), ALU.subtract)
                            ins.then_inc(y_read[l], 1)
                            middle(b, e)
                            break
                        if e == 2:
                            turned(b, e - 1)
                        elif e == 1:
                            dve.wait_ge(gather_full[l], b * 3 + 3)
                            permute()
                        low(b, "B", e + 1)
                        if e == EPG - 1:
                            turned(b, e - 1)
                            inputs(0, b * 2 + 3)
                            inputs(1, b * 2 + 4)
                        middle(b, e)
                        if e == EPG - 1:
                            slot_gates(b * 3 + 4)
                        low(b, "C", e)
                    dve.wait_ge(x_added[l], b + 1)
                    for c in range(2 * NT):
                        t, half = c // 2, c % 2
                        dve.wait_ge(scatter_full[l], b * 6 + (c + 1))
                        dve.tensor_tensor(gtmp[:, c, :], ps[SCATTER_BANKS[c]][:, :], gb[:, GRP[t], half * 512:half * 512 + 512],
                                          ALU.mult).then_inc(scatter_read[l], 1)
                    low(b, "C", EPG)
                    back_table()

            def moe(l):
                modulate(l, 1)
                route(l)
                dve.wait_ge(in_route, 32 * (l + 1))
                make_plan(l)
                experts(l)

            dve.memset(hidden[HID:HID + 1, :], 1.0)
            dve.memset(zero2[:, :], 0.0)
            dve.memset(onesm, 1.0)
            dve.drain().then_inc(ones_set, 1)
            for e in range(NE):
                dve.memset(rank_e[:, e:e + 1], float(NE - e))
            loaded(dve, in_mod)
            dve.tensor_copy(modT[:, :, :, :, :].rearrange("p l v j c -> p (l v j) c"),
                            modbias.rearrange("p l v j -> p (l v j)").unsqueeze(2).broadcast_to([P, 12 * KT, 2]))
            hid = hidden[0:HID, :]
            loaded(dve, in_filt)
            for i in range(2):
                bank = filled_wait(dve, f"filt{i + 1}")
                drain_inc(dve.tensor_scalar(hid, bank[0:HID, 0:T], filtc[:, i:i + 1], filtc[:, 2:3], ALU.add, ALU.mult), f"filt{i + 1}")
                settle()
                dve.tensor_scalar(turns, hid, 1.0 / (2 * math.pi), ROUNDER, ALU.mult, ALU.add)
                settle()
                dve.tensor_scalar(turns, turns, ROUNDER, None, ALU.subtract)
                for part in (TWO_PI_A, TWO_PI_B, TWO_PI_C):
                    settle()
                    dve.scalar_tensor_tensor(out=hid, in0=turns, scalar=-part, in1=hid, op0=ALU.mult, op1=ALU.add)
                settle()
                dve.tensor_scalar(hid, hid, SIN_MAX, -SIN_MAX, ALU.min, ALU.max).then_inc(sin_arg, 1)
                mod_step("start", i)
            loaded(dve, in_filt3)

            for od in range(2):
                for t in range(NT):
                    for r in range(2):
                        bank = filled_wait(dve, f"filt3.{od}", 2 * t + r)
                        drain_inc(dve.tensor_tensor(filt[:, t, r, :], bank[:, :], decay[:, t, :], ALU.mult), f"filt3.{od}", 2 * t + r)
                    settle()
                    if t < 2:
                        dve.memset(filt[0:1, t, 1, :], 0.0)
                        settle()
                    if od + t:
                        dve.wait_ge(esq_ready, od * NT + t)
                    dve.tensor_tensor(sqd, filt[:, t, 0, :], filt[:, t, 1, :], ALU.add)
                    dve.tensor_tensor(filt[:, t, 1, :], filt[:, t, 0, :], filt[:, t, 1, :], ALU.subtract).then_inc(sum_ready, 1)
                if od == 0:
                    mod_step("start", 2)
                else:
                    modulate(0, 0)
                for g in range(2):
                    bank = filled_wait(dve, f"energy{od}", g)
                    drain_inc(dve.tensor_scalar(esc[:, g, :], bank[:, :], 0.5, EPS, ALU.mult, ALU.add), f"energy{od}", g)
                    dve.drain().then_inc(eroot, 1)
                for g in range(2):
                    dve.wait_ge(escale_ready, 2 * od + g + 1)
                    dve.reciprocal(esc[:, g, :], esc[:, g, :])
                settle()
                if od == 0:
                    mod_step("start", 3)
                    norm(0)
                for i in range(2 * NT):
                    ft, r = i // 2, i % 2
                    bank = filled_wait(dve, f"spec{od}", i)
                    ins = dve.tensor_tensor(H[:, od, r, ft, :], bank[:, :], esc[:, GRP[ft], :], ALU.mult)
                    drain_inc(ins, f"spec{od}", i)
                settle()
                for ft in range(NT):
                    dve.tensor_tensor(H[:, od, 0, ft, :], H[:, od, 0, ft, :], hybias[:, od, :], ALU.add)
                dve.drain().then_inc(spec_done, 6)
                if od == 0:
                    loaded(dve, in_mod)
                    mod_step("start", 4)
                    bank = filled_wait(dve, "convT")
                    ins = dve.tensor_copy(convT[:, :, :], bank[:, 0:48].rearrange("p (a b) -> p a b", b=3 * NCH))
                    drain_inc(ins, "convT")
                    dve.drain().then_inc(conv_copied, 1)

            loaded(dve, in_attn)
            dve.tensor_scalar(qkgain[:, 0, :], qkgain[:, 0, :], HD ** -0.5, None, ALU.mult)
            QKH = QH + KVH
            for t in range(NT):
                for q in range(3):
                    drained_wait(dve, *(("qkv", q * NT + t) if q < 2 else ("qkv2", t)))
                v = qkv[:, t, 0:QKH * HD].rearrange("p (h e) -> p h e", e=HD)
                dve.tensor_tensor(qsq, v, v, ALU.mult)
                settle()
                dve.tensor_reduce(statA[:, 0, QKH * t:QKH * (t + 1)], qsq, AXX, ALU.add)
                settle()
            dve.tensor_scalar(statA[:, 0, 0:30], statA[:, 0, 0:30], 1.0 / HD, EPS, ALU.mult, ALU.add).then_inc(qvar, 1)
            dve.wait_ge(qroot, 1)
            dve.reciprocal(statA[:, 1, 0:30], statA[:, 1, 0:30])
            settle()
            for t in range(NT):
                v = qkv[:, t, 0:QKH * HD].rearrange("p (h e) -> p h e", e=HD)
                dve.tensor_tensor(v, v, statA[:, 1, QKH * t:QKH * (t + 1)].unsqueeze(2).broadcast_to([P, QKH, HD]), ALU.mult)
                settle()
                dve.tensor_tensor(v[:, 0:QH, :], v[:, 0:QH, :], qkgain[:, 0, :].unsqueeze(1).broadcast_to([P, QH, HD]), ALU.mult)
                ins = dve.tensor_tensor(v[:, QH:QKH, :], v[:, QH:QKH, :], qkgain[:, 1, :].unsqueeze(1).broadcast_to([P, KVH, HD]), ALU.mult)
                if t:
                    settle()
                    ins = rope(dve, v, ropeq[:, t - 1, :, :], qsq, qrb, QKH, HD)
                ins.then_inc(qk_ready, 1)

            for m in range(3 * NCH):
                drained_wait(dve, "uT", m)
                for a, b in ((0, NPR), (NPR, T)):
                    dve.scalar_tensor_tensor(out=uc[:, m, a + 1:b], in0=uT[:, m, a:b - 1], scalar=convT[:, 0, m:m + 1],
                                             in1=uc[:, m, a + 1:b], op0=ALU.mult, op1=ALU.add)
                settle()
                for a, b in ((0, NPR), (NPR, T)):
                    ins = dve.scalar_tensor_tensor(out=uc[:, m, a:b - 1], in0=uT[:, m, a + 1:b], scalar=convT[:, 2, m:m + 1],
                                                   in1=uc[:, m, a:b - 1], op0=ALU.mult, op1=ALU.add)
                ins.then_inc(conv_done, 1)

            for od in range(2):
                for ft in range(NT):
                    Hr, Hi = H[:, od, 0, ft, :], H[:, od, 1, ft, :]
                    settle()
                    bank = filled_wait(dve, f"fwd{od}", 2 * ft)
                    dve.tensor_tensor(Y[:, ft, 0, :], bank[:, :], Hr, ALU.mult)
                    drain_inc(dve.tensor_tensor(Y[:, ft, 1, :], bank[:, :], Hi, ALU.mult), f"fwd{od}", 2 * ft)
                    bank = filled_wait(dve, f"fwd{od}", 2 * ft + 1)
                    dve.tensor_tensor(tmpa, bank[:, :], Hi, ALU.mult)
                    drain_inc(dve.tensor_tensor(tmpb, bank[:, :], Hr, ALU.mult), f"fwd{od}", 2 * ft + 1)
                    settle()
                    dve.tensor_tensor(Y[:, ft, 0, :], Y[:, ft, 0, :], tmpa, ALU.subtract)
                    dve.tensor_tensor(Y[:, ft, 1, :], Y[:, ft, 1, :], tmpb, ALU.add).then_inc(y_ready, 1)
                if od == 0:
                    for t in range(NT):
                        drained_wait(dve, "x1tok", t)
                        bank = filled_wait(dve, "inv0", t)
                        drain_inc(dve.tensor_tensor(vtok[:, t, :], bank[:, :], x1tok[:, t, :], ALU.mult), "inv0", t)
                else:
                    for c in range(NCH):
                        bank = filled_wait(dve, "inv1", c)
                        drain_inc(dve.tensor_tensor(hT[:, c, :], bank[:, 0:T], uc[:, 2 * NCH + c, :], ALU.mult), "inv1", c)

            for i in range(GQA_AHEAD):
                mod_step("gqa", i)
            attention("g", units_gqa, QH, lambda t: otok[:, t, :].rearrange("p (h e) -> p h e", e=HD))
            out_projection(0)
            moe(0)

            dve.wait_ge(x_done, 1)
            norm(2)
            modulate(1, 0)
            loaded(dve, in_mla)
            dve.wait_ge(lora_sq, 1)
            dve.tensor_scalar(statA[:, 0, 0:NT], statA[:, 0, 0:NT], 1.0 / QR, EPS, ALU.mult, ALU.add)
            dve.tensor_scalar(statA[:, 0, NT:2 * NT], statA[:, 0, NT:2 * NT], 1.0 / KVR, EPS, ALU.mult, ALU.add).then_inc(lora_var, 1)
            dve.tensor_scalar(mgain[:, 0, :], mgain[:, 0, :], QK ** -0.5, None, ALU.mult)
            dve.wait_ge(lora_root, 1)
            dve.reciprocal(statA[:, 1, 0:2 * NT], statA[:, 1, 0:2 * NT])
            settle()
            for t in range(NT):
                for c0, c1, i in ((0, QR, t), (QR, QR + KVR, NT + t)):
                    ins = dve.scalar_tensor_tensor(out=um[:, t, c0:c1], in0=um[:, t, c0:c1], scalar=statA[:, 1, i:i + 1],
                                                   in1=lgain[:, c0:c1], op0=ALU.mult, op1=ALU.mult)
                ins.then_inc(lora_ready, 1)
            for step in range(MLA_NORM_STEPS):
                mla_norm(0, step)
            for g in range(NHG):
                attention(str(g), units_mla, HG,
                          lambda t, g=g: mtok[:, t, g * HG * VD:(g + 1) * HG * VD].rearrange("p (h e) -> p h e", e=VD))
            out_projection(1)
            moe(1)


_OUTS = [(1, NPR, D), (1, NSA, D), (1, 1, NPR, KVH, HD), (1, 1, NPR, KVH, HD), (1, 1, NPR, KVR), (1, 1, NPR, ROPE)]


def kernel(**inputs):
    import concourse.bacc as _bacc
    from concourse.bass_utils import run_bass_kernel_spmd as _run

    nc = _bacc.Bacc("TRN2", target_bir_lowering=False, num_devices=1)
    arrays, dram = {}, {}
    for name, a in list(inputs.items()) + list(shape_constants().items()):
        a = np.ascontiguousarray(a)
        arrays[f"in_{name}_dram"] = a
        dram[name] = nc.dram_tensor(f"in_{name}_dram", a.shape, mybir.dt.from_np(a.dtype), kind="ExternalInput").ap()
    outs = [nc.dram_tensor(f"out_{i}_dram", shape, F32, kind="ExternalOutput").ap() for i, shape in enumerate(_OUTS)]
    build_step(nc, dram, outs)
    r = _run(nc, [arrays], core_ids=[0])
    return tuple(r.results[0][f"out_{i}_dram"] for i in range(len(_OUTS)))
```
